# Optimizing a Trainium2 kernel written in Bass

```python
import math
import jax
import jax.numpy as jnp
from jax import lax
import numpy as np

D_MODEL = 1024
BATCH = 1
SEQ = 1024
DEPTH = 2

NORM_EPS = 1e-6
N_MOD = 6
ADA_SCALE = 0.02

ATT_HEADS = 8
HEAD_DIM = 64
ATT_WIDTH = ATT_HEADS * HEAD_DIM
MOBA_BLOCK = 256
MOBA_TOPK = 3
MOBA_CHUNK = 128
CONV_CH = D_MODEL // 2
CONV_WIDTH = 31
HY_IN = 3 * ATT_WIDTH + 2 * CONV_CH
HY_MIX = ATT_WIDTH + CONV_CH

SSM_INNER = 2 * D_MODEL
SSM_HEAD_DIM = 64
SSM_HEADS = SSM_INNER // SSM_HEAD_DIM
SSM_GROUPS = 4
SSM_STATE = 128
SSM_CONV = 4
SSM_CHUNK = 256
SSM_CONV_DIM = SSM_INNER + 2 * SSM_GROUPS * SSM_STATE
SSM_IN = SSM_INNER + SSM_CONV_DIM + SSM_HEADS
DT_MIN = 1e-3
DT_MAX = 1e-1

N_EXPERTS = 16
N_EXPERT_GROUPS = 4
EXPERTS_PER_GROUP = N_EXPERTS // N_EXPERT_GROUPS
TOP_K = 2
EXPERT_FF = 512
MOE_CHUNK = 256

N_EVEN = (DEPTH + 1) // 2
N_ODD = DEPTH // 2

kernel_name = 'hybrid_moba_conformer_ssd_moe'

def _rmsnorm(x, g):
    xf = x.astype(jnp.float32)
    y = xf * lax.rsqrt(jnp.mean(xf * xf, axis=-1, keepdims=True) + NORM_EPS)
    return (y * g.astype(jnp.float32)).astype(x.dtype)

def _pad_seq(t, s_pad):
    pad = [(0, 0)] * t.ndim
    pad[1] = (0, s_pad - t.shape[1])
    return jnp.pad(t, pad)

def _causal_depthwise_conv(u, w, b):
    width, ch = w.shape
    y = lax.conv_general_dilated(u, w[:, None, :].astype(u.dtype), window_strides=(1,),
                                 padding=[(width - 1, 0)],
                                 dimension_numbers=('NWC', 'WIO', 'NWC'),
                                 feature_group_count=ch)
    return y + b.astype(u.dtype)

def _moba_head(q, k, v):
    s_pad = q.shape[0]
    nb = s_pad // MOBA_BLOCK
    k_eff = min(MOBA_TOPK, nb)
    n_pairs = s_pad * k_eff
    n_slots = n_pairs + nb * MOBA_CHUNK
    n_chunks = n_slots // MOBA_CHUNK
    scale = HEAD_DIM ** -0.5
    qb = q.reshape(nb, MOBA_BLOCK, HEAD_DIM)
    kb = k.reshape(nb, MOBA_BLOCK, HEAD_DIM)
    vb = v.reshape(nb, MOBA_BLOCK, HEAD_DIM)
    causal = jnp.tril(jnp.ones((MOBA_BLOCK, MOBA_BLOCK), bool))
    s_own = jnp.where(causal, jnp.einsum('nqd,nkd->nqk', qb, kb) * scale, -jnp.inf)
    lse_own = jax.nn.logsumexp(s_own, axis=-1)
    o_own = jnp.einsum('nqk,nkd->nqd', jnp.exp(s_own - lse_own[..., None]), vb)
    q_blk = jnp.arange(s_pad) // MOBA_BLOCK
    gate = q @ kb.mean(axis=1).T
    gate = jnp.where(jnp.arange(nb)[None, :] < q_blk[:, None], gate, -jnp.inf)
    _, sel = lax.top_k(gate, k_eff)
    valid = jnp.arange(k_eff)[None, :] < q_blk[:, None]
    pair_blk = jnp.where(valid, sel, nb).reshape(-1)
    pair_q = jnp.repeat(jnp.arange(s_pad), k_eff)
    order = jnp.argsort(pair_blk)
    s_blk = pair_blk[order]
    counts = jax.ops.segment_sum(jnp.ones((n_pairs,), jnp.int32), pair_blk, num_segments=nb + 1)
    start = jnp.cumsum(counts) - counts
    padded = (counts[:nb] + MOBA_CHUNK - 1) // MOBA_CHUNK * MOBA_CHUNK
    padded_end = jnp.cumsum(padded)
    padded_start = jnp.concatenate([jnp.zeros((1,), padded_end.dtype), padded_end])
    dest = padded_start[s_blk] + jnp.arange(n_pairs) - start[s_blk]
    dest = jnp.where(s_blk < nb, dest, n_slots)
    slot_q = jnp.zeros((n_slots,), jnp.int32).at[dest].set(pair_q[order].astype(jnp.int32), mode='drop')
    slot_pair = jnp.full((n_slots,), n_pairs, jnp.int32).at[dest].set(order.astype(jnp.int32), mode='drop')
    chunk_blk = jnp.minimum(jnp.searchsorted(padded_end, jnp.arange(n_chunks) * MOBA_CHUNK, side='right'), nb - 1)
    qc = q[slot_q].reshape(n_chunks, MOBA_CHUNK, HEAD_DIM)
    s_c = jnp.einsum('ncd,nkd->nck', qc, kb[chunk_blk]) * scale
    lse_c = jax.nn.logsumexp(s_c, axis=-1)
    o_c = jnp.einsum('nck,nkd->ncd', jnp.exp(s_c - lse_c[..., None]), vb[chunk_blk])
    o_sel = jnp.zeros((n_pairs, HEAD_DIM), q.dtype).at[slot_pair].set(o_c.reshape(n_slots, HEAD_DIM), mode='drop')
    lse_sel = jnp.full((n_pairs,), -jnp.inf, q.dtype).at[slot_pair].set(lse_c.reshape(n_slots), mode='drop')
    lse_all = jnp.concatenate([lse_sel.reshape(s_pad, k_eff), lse_own.reshape(s_pad, 1)], axis=1)
    o_all = jnp.concatenate([o_sel.reshape(s_pad, k_eff, HEAD_DIM), o_own.reshape(s_pad, 1, HEAD_DIM)], axis=1)
    return jnp.einsum('sr,srd->sd', jax.nn.softmax(lse_all, axis=-1), o_all)

def _moba_attention(q, k, v):
    s = q.shape[1]
    s_pad = -(-s // MOBA_BLOCK) * MOBA_BLOCK
    q, k, v = (_pad_seq(t.astype(jnp.float32), s_pad).transpose(0, 2, 1, 3) for t in (q, k, v))
    o = lax.map(lambda args: jax.vmap(_moba_head)(*args), (q, k, v))
    return o.transpose(0, 2, 1, 3)[:, :s]

def _conformer_conv(u, dw_w, dw_b, ln_g, ln_b):
    a, g = jnp.split(u, 2, axis=-1)
    y = _causal_depthwise_conv(a * jax.nn.sigmoid(g), dw_w, dw_b)
    yf = y.astype(jnp.float32)
    mu = jnp.mean(yf, axis=-1, keepdims=True)
    var = jnp.mean(jnp.square(yf - mu), axis=-1, keepdims=True)
    yf = (yf - mu) * lax.rsqrt(var + NORM_EPS) * ln_g.astype(jnp.float32) + ln_b.astype(jnp.float32)
    return jax.nn.silu(yf).astype(u.dtype)

def _hybrid_mixer(h, w_in, q_norm, k_norm, dw_w, dw_b, ln_g, ln_b, w_out):
    bsz, s, _ = h.shape
    proj = h @ w_in
    q, k, v, u = jnp.split(proj, [ATT_WIDTH, 2 * ATT_WIDTH, 3 * ATT_WIDTH], axis=-1)
    q = _rmsnorm(q.reshape(bsz, s, ATT_HEADS, HEAD_DIM), q_norm)
    k = _rmsnorm(k.reshape(bsz, s, ATT_HEADS, HEAD_DIM), k_norm)
    v = v.reshape(bsz, s, ATT_HEADS, HEAD_DIM)
    att = _moba_attention(q, k, v).reshape(bsz, s, ATT_WIDTH).astype(h.dtype)
    conv = _conformer_conv(u, dw_w, dw_b, ln_g, ln_b)
    return jnp.concatenate([att, conv], axis=-1) @ w_out

def _segsum(a):
    t = a.shape[-1]
    cs = jnp.cumsum(a, axis=-1)
    mask = jnp.tril(jnp.ones((t, t), bool))
    return jnp.where(mask, cs[..., :, None] - cs[..., None, :], -jnp.inf)

def _ssd_chunked(x, a, bm, cm):
    s = x.shape[0]
    nc = s // SSM_CHUNK
    e = SSM_HEADS // SSM_GROUPS
    x = x.reshape(nc, SSM_CHUNK, SSM_GROUPS, e, SSM_HEAD_DIM)
    a = a.reshape(nc, SSM_CHUNK, SSM_GROUPS, e).transpose(2, 3, 0, 1)
    bm = bm.reshape(nc, SSM_CHUNK, SSM_GROUPS, SSM_STATE)
    cm = cm.reshape(nc, SSM_CHUNK, SSM_GROUPS, SSM_STATE)
    a_cs = jnp.cumsum(a, axis=-1)
    decay = jnp.exp(_segsum(a))
    cb = jnp.einsum('clgn,csgn->gcls', cm, bm)
    y_diag = jnp.einsum('gcls,gecls,csgep->clgep', cb, decay, x)
    decay_states = jnp.exp(a_cs[..., -1:] - a_cs)
    states = jnp.einsum('clgn,gecl,clgep->cgepn', bm, decay_states, x)
    states = jnp.concatenate([jnp.zeros_like(states[:1]), states], axis=0)
    chunk_decay = jnp.exp(_segsum(jnp.pad(a_cs[..., -1], ((0, 0), (0, 0), (1, 0)))))
    states = jnp.einsum('gezc,cgepn->zgepn', chunk_decay, states)[:-1]
    y_off = jnp.einsum('clgn,cgepn,gecl->clgep', cm, states, jnp.exp(a_cs))
    return (y_diag + y_off).reshape(s, SSM_HEADS, SSM_HEAD_DIM)

def _mamba2_mixer(h, w_in, conv_w, conv_b, dt_bias, a_log, d_skip, norm_g, w_out):
    bsz, s, _ = h.shape
    proj = h @ w_in
    z, xbc, dt = jnp.split(proj, [SSM_INNER, SSM_INNER + SSM_CONV_DIM], axis=-1)
    xbc = jax.nn.silu(_causal_depthwise_conv(xbc, conv_w, conv_b)).astype(jnp.float32)
    xs, bm, cm = jnp.split(xbc, [SSM_INNER, SSM_INNER + SSM_GROUPS * SSM_STATE], axis=-1)
    xs = xs.reshape(bsz, s, SSM_HEADS, SSM_HEAD_DIM)
    bm = bm.reshape(bsz, s, SSM_GROUPS, SSM_STATE)
    cm = cm.reshape(bsz, s, SSM_GROUPS, SSM_STATE)
    dt = jax.nn.softplus(dt.astype(jnp.float32) + dt_bias.astype(jnp.float32))
    a = -jnp.exp(a_log.astype(jnp.float32))
    s_pad = -(-s // SSM_CHUNK) * SSM_CHUNK
    y = lax.map(lambda args: _ssd_chunked(*args),
                (_pad_seq(xs * dt[..., None], s_pad), _pad_seq(dt * a, s_pad),
                 _pad_seq(bm, s_pad), _pad_seq(cm, s_pad)))[:, :s]
    y = (y + xs * d_skip.astype(jnp.float32)[:, None]).reshape(bsz, s, SSM_INNER)
    g = (y * jax.nn.silu(z.astype(jnp.float32))).reshape(bsz, s, SSM_GROUPS, SSM_INNER // SSM_GROUPS)
    g = g * lax.rsqrt(jnp.mean(g * g, axis=-1, keepdims=True) + NORM_EPS)
    g = g.reshape(bsz, s, SSM_INNER) * norm_g.astype(jnp.float32)
    return g.astype(h.dtype) @ w_out

def _route(h, router_w, router_bias):
    t = h.shape[0]
    aff = jax.nn.sigmoid((h @ router_w).astype(jnp.float32))
    score = (aff + router_bias.astype(jnp.float32)).reshape(t, N_EXPERT_GROUPS, EXPERTS_PER_GROUP)
    group_score = lax.top_k(score, TOP_K)[0].sum(axis=-1)
    group = jnp.argmax(group_score, axis=-1)
    in_group = jnp.take_along_axis(score, group[:, None, None], axis=1)[:, 0]
    _, local = lax.top_k(in_group, TOP_K)
    expert = (group[:, None] * EXPERTS_PER_GROUP + local).astype(jnp.int32)
    w = jnp.take_along_axis(aff, expert, axis=1)
    return expert, w / jnp.sum(w, axis=-1, keepdims=True)

def _moe(h, router_w, router_bias, w_gate, w_up, w_down):
    t, d = h.shape
    expert, w = _route(h, router_w, router_bias)
    n_pairs = t * TOP_K
    n_slots = -(-n_pairs // MOE_CHUNK) * MOE_CHUNK + N_EXPERTS * MOE_CHUNK
    n_chunks = n_slots // MOE_CHUNK
    pair_e = expert.reshape(-1)
    pair_t = jnp.repeat(jnp.arange(t), TOP_K)
    order = jnp.argsort(pair_e)
    s_e = pair_e[order]
    counts = jax.ops.segment_sum(jnp.ones((n_pairs,), jnp.int32), pair_e, num_segments=N_EXPERTS)
    start = jnp.cumsum(counts) - counts
    padded = (counts + MOE_CHUNK - 1) // MOE_CHUNK * MOE_CHUNK
    padded_end = jnp.cumsum(padded)
    dest = padded_end[s_e] - padded[s_e] + jnp.arange(n_pairs) - start[s_e]
    slot_t = jnp.zeros((n_slots,), jnp.int32).at[dest].set(pair_t[order].astype(jnp.int32))
    slot_pair = jnp.full((n_slots,), n_pairs, jnp.int32).at[dest].set(order.astype(jnp.int32))
    chunk_e = jnp.minimum(jnp.searchsorted(padded_end, jnp.arange(n_chunks) * MOE_CHUNK, side='right'), N_EXPERTS - 1)
    xs = h[slot_t].reshape(n_chunks, MOE_CHUNK, d)

    def expert_block(args):
        xc, e = args
        return (jax.nn.silu(xc @ w_gate[e]) * (xc @ w_up[e])) @ w_down[e]

    ys = lax.map(expert_block, (xs, chunk_e))
    y_pair = jnp.zeros((n_pairs, d), ys.dtype).at[slot_pair].set(ys.reshape(n_slots, d), mode='drop')
    y = jnp.einsum('tk,tkd->td', w, y_pair.reshape(t, TOP_K, d).astype(jnp.float32))
    return y.astype(h.dtype)

def setup_inputs(seed: int = 0) -> dict:
    key = jax.random.key(seed)
    ks = jax.random.split(key, 32)
    f32 = jnp.float32

    def nrm(k, shape, scale):
        return jax.random.normal(k, shape, f32) * scale

    def gain(k, shape):
        return 1.0 + 0.02 * jax.random.normal(k, shape, f32)

    dt0 = jnp.exp(jax.random.uniform(ks[17], (N_ODD, SSM_HEADS), f32, math.log(DT_MIN), math.log(DT_MAX)))
    return {
        'x': nrm(ks[0], (BATCH, SEQ, D_MODEL), 1.0),
        'c': nrm(ks[1], (BATCH, D_MODEL), 1.0),
        'ada_w': nrm(ks[2], (DEPTH, D_MODEL, N_MOD * D_MODEL), ADA_SCALE),
        'ada_b': nrm(ks[3], (DEPTH, N_MOD * D_MODEL), 0.02),
        'norm_mix': gain(ks[4], (DEPTH, D_MODEL)),
        'norm_ffn': gain(ks[5], (DEPTH, D_MODEL)),
        'hy_w_in': nrm(ks[6], (N_EVEN, D_MODEL, HY_IN), D_MODEL ** -0.5),
        'hy_q_norm': gain(ks[7], (N_EVEN, HEAD_DIM)),
        'hy_k_norm': gain(ks[8], (N_EVEN, HEAD_DIM)),
        'hy_dw_w': nrm(ks[9], (N_EVEN, CONV_WIDTH, CONV_CH), CONV_WIDTH ** -0.5),
        'hy_dw_b': nrm(ks[10], (N_EVEN, CONV_CH), 0.02),
        'hy_ln_g': gain(ks[11], (N_EVEN, CONV_CH)),
        'hy_ln_b': nrm(ks[12], (N_EVEN, CONV_CH), 0.02),
        'hy_w_out': nrm(ks[13], (N_EVEN, HY_MIX, D_MODEL), HY_MIX ** -0.5),
        'ssm_w_in': nrm(ks[14], (N_ODD, D_MODEL, SSM_IN), D_MODEL ** -0.5),
        'ssm_conv_w': nrm(ks[15], (N_ODD, SSM_CONV, SSM_CONV_DIM), SSM_CONV ** -0.5),
        'ssm_conv_b': nrm(ks[16], (N_ODD, SSM_CONV_DIM), 0.02),
        'ssm_dt_bias': dt0 + jnp.log(-jnp.expm1(-dt0)),
        'ssm_a_log': jnp.log(jax.random.uniform(ks[18], (N_ODD, SSM_HEADS), f32, 1.0, 16.0)),
        'ssm_d': gain(ks[19], (N_ODD, SSM_HEADS)),
        'ssm_norm': gain(ks[20], (N_ODD, SSM_INNER)),
        'ssm_w_out': nrm(ks[21], (N_ODD, SSM_INNER, D_MODEL), SSM_INNER ** -0.5),
        'router_w': nrm(ks[22], (D_MODEL, N_EXPERTS), D_MODEL ** -0.5),
        'router_bias': nrm(ks[23], (N_EXPERTS,), 0.01),
        'exp_w_gate': nrm(ks[24], (DEPTH, N_EXPERTS, D_MODEL, EXPERT_FF), D_MODEL ** -0.5),
        'exp_w_up': nrm(ks[25], (DEPTH, N_EXPERTS, D_MODEL, EXPERT_FF), D_MODEL ** -0.5),
        'exp_w_down': nrm(ks[26], (DEPTH, N_EXPERTS, EXPERT_FF, D_MODEL), EXPERT_FF ** -0.5),
    }

def reference(x, c, ada_w, ada_b, norm_mix, norm_ffn, hy_w_in, hy_q_norm, hy_k_norm, hy_dw_w, hy_dw_b,
              hy_ln_g, hy_ln_b, hy_w_out, ssm_w_in, ssm_conv_w, ssm_conv_b, ssm_dt_bias, ssm_a_log, ssm_d,
              ssm_norm, ssm_w_out, router_w, router_bias, exp_w_gate, exp_w_up, exp_w_down):
    bsz, s, d = x.shape
    cond = jax.nn.silu(c)
    for layer in range(DEPTH):
        mod = (cond @ ada_w[layer] + ada_b[layer])[:, None, :]
        sh1, sc1, g1, sh2, sc2, g2 = jnp.split(mod, N_MOD, axis=-1)
        h = _rmsnorm(x, norm_mix[layer]) * (1 + sc1) + sh1
        j = layer // 2
        if layer % 2 == 0:
            m = _hybrid_mixer(h, hy_w_in[j], hy_q_norm[j], hy_k_norm[j], hy_dw_w[j], hy_dw_b[j],
                              hy_ln_g[j], hy_ln_b[j], hy_w_out[j])
        else:
            m = _mamba2_mixer(h, ssm_w_in[j], ssm_conv_w[j], ssm_conv_b[j], ssm_dt_bias[j], ssm_a_log[j],
                              ssm_d[j], ssm_norm[j], ssm_w_out[j])
        x = x + g1 * m
        h = _rmsnorm(x, norm_ffn[layer]) * (1 + sc2) + sh2
        f = _moe(h.reshape(bsz * s, d), router_w, router_bias, exp_w_gate[layer], exp_w_up[layer],
                 exp_w_down[layer]).reshape(bsz, s, d)
        x = x + g2 * f
    return x


_drawn_inputs = setup_inputs


def setup_inputs(seed=0):
    import zlib

    import numpy as np

    out = dict(_drawn_inputs(seed))
    spreads = {}
    factors = {'hy_q_norm': 4.787,
     'hy_k_norm': 8.0,
     'ssm_conv_b': 3.041,
     'ssm_d': 5.274,
     'ssm_norm': 3.594,
     'hy_dw_b': 3.031,
     'hy_ln_g': 3.153,
     'hy_ln_b': 5.177}
    for name, (base, spread) in spreads.items():
        noise = np.random.default_rng([zlib.crc32(name.encode()), seed]).standard_normal(out[name].shape)
        drawn = base * np.exp(spread * noise) if base else spread * noise
        out[name] = jnp.asarray(drawn.astype(out[name].dtype))
    for name, factor in factors.items():
        out[name] = (out[name] * factor).astype(out[name].dtype)
    return out
```

```python
import concourse.bass as bass
from concourse import mybir
from contextlib import ExitStack

P = 128
SEQ = 1024
D = 1024
DEPTH = 2
NT = SEQ // P
KD = D // P
HALF = 512
N_MOD = 6
EPS = 1e-6
HEADS = 8
HD = 64
ATT_W = HEADS * HD
PAIRS = ATT_W // P
CONV_CH = D // 2
CT = CONV_CH // P
CONV_W = 31
NEG = -1e30
SSM_INNER = 2 * D
SSM_HEADS = 32
SSM_HEAD_DIM = SSM_INNER // SSM_HEADS
SSM_G = 4
HPG = SSM_HEADS // SSM_G
GW = SSM_INNER // SSM_G
NST = 128
SCONV = 4
CHUNK = 256
NCH = SEQ // CHUNK
E = 16
G = 4
J = E // G
FF = 512
FT = FF // P
TOPK = 2
SLOTS = (SEQ * TOPK) // P + E

CONST = {}
_at = 0
for _name, _n in (("ident", P), ("tri_strict", P), ("tri_inc", P), ("ones", P), ("tri_inc2", P), ("maskneg", P),
                  ("before4", J * J), ("group_key", G), ("step128", NT), ("before16", E * E),
                  ("chunk_end", SLOTS), ("iota_chunk", SLOTS), ("iota128", P), ("token_id", NT),
                  ("eps", 1)):
    CONST[_name] = (_at, _n)
    _at += _n
NCONST = _at
PCOL = {}
_at = 0
for _name, _n in (("c", KD), ("ada_b", N_MOD * KD), ("norm0", KD), ("norm1", KD)):
    PCOL[_name] = (_at, _n)
    _at += _n
NPCOL = _at
MIX0 = {"gq": (0, 1), "gk": (1, 1), "dw_b": (2, CT), "ln_g": (2 + CT, CT), "ln_b": (2 + 2 * CT, CT),
        "dw_w": (2 + 3 * CT, CT * CONV_W)}
NMIX0 = 2 + 3 * CT + CT * CONV_W
XBC_T = (SSM_INNER + 2 * SSM_G * NST) // P
MIX1 = {"conv_b": (0, XBC_T), "norm": (XBC_T, SSM_INNER // P),
        "conv_w": (XBC_T + SSM_INNER // P, XBC_T * SCONV)}
NMIX1 = XBC_T + SSM_INNER // P + XBC_T * SCONV
ROWS = {"rbias": (0, E), "dt_bias": (E, SSM_HEADS), "a_log": (E + SSM_HEADS, SSM_HEADS),
        "ssm_d": (E + 2 * SSM_HEADS, SSM_HEADS)}
NROWS = E + 3 * SSM_HEADS


def bc(ap, axis, n):
    ap = ap.unsqueeze(axis)
    shape = list(ap.shape)
    shape[axis] = n
    return ap.to_broadcast(shape)


class Steps:

    def __init__(self, eng, sem, base=0, turn=None, per=0):
        self.eng, self.sem, self.n, self.base, self.turn, self.per = eng, sem, 0, base, turn, per

    def did(self, ins):
        ins.then_inc(self.sem, 1)
        self.n += 1
        return ins

    def wait(self):
        at = self.base + self.n
        self.eng.wait_ge(self.sem, at if self.turn is None else self.turn * self.per + at)

    def link(self, ins):
        self.did(ins)
        self.wait()

    def end(self):
        assert self.turn is None or self.n == self.per, (self.n, self.per)


def build(nc, ins, out, stages):
    f32 = mybir.dt.float32
    i32 = mybir.dt.int32
    u32 = mybir.dt.uint32
    ALU = mybir.AluOpType
    ACT = mybir.ActivationFunctionType
    X = mybir.AxisListType.X
    ctx = ExitStack()
    uid = [0]
    live = []

    def sb(name, shape, dt=f32):
        return ctx.enter_context(nc.sbuf_tensor(name, shape, dt))

    def sem(name):
        uid[0] += 1
        live.append(nc.alloc_semaphore(name=f"{name}_{uid[0]}"))
        return live[-1]

    def clear_sems():
        nc.clear_and_free_semaphores(live[:])
        live.clear()
        nc.all_engine_barrier()

    with ctx:
        ctx.enter_context(nc.allow_non_contiguous_dma(reason="parameter columns"))
        x = sb("x", [P, NT, D])
        hT = sb("hT", [P, KD, SEQ])
        cst = sb("cst", [P, NCONST])
        pcol = sb("pcol", [P, DEPTH, NPCOL])
        mix0 = sb("mix0", [P, NMIX0])
        mix1 = sb("mix1", [P, NMIX1])
        rows = sb("rows", [P, NROWS])
        gate = sb("gate", [P, 2, D])
        modc = sb("modc", [P, DEPTH, 2, 2, KD])
        small = sb("small", [P, 256])
        WORK = 32640
        work = sb("work", [P, WORK])
        ps = ctx.enter_context(nc.psum_tensor("ps", [P, 8, HALF], f32))
        hrows = nc.dram_tensor("hrows", [SEQ, D], f32, kind="Internal").ap()
        yrows = nc.dram_tensor("yrows", [SLOTS * P, D], f32, kind="Internal").ap()
        acs_rows = nc.dram_tensor("acs_rows", [SSM_HEADS, SEQ], f32, kind="Internal").ap()

        def const(name):
            at, n = CONST[name]
            return cst[:, at:at + n]

        def view(at, shape):
            n = 1
            for s in shape:
                n *= s
            assert at + n <= WORK, (at, n)
            v = work[:, at:at + n]
            if len(shape) == 2:
                v = v.rearrange("p (a b) -> p a b", b=shape[1])
            elif len(shape) == 3:
                v = v.rearrange("p (a b c) -> p a b c", b=shape[1], c=shape[2])
            return v, at + n

        ident, ones = const("ident"), const("ones")
        eps = const("eps")

        with nc.Block() as block:
            s_in = sem("inputs_loaded")
            s_cond = sem("cond_ready")

            @block.sync
            def _(sp):
                sp.dma_start(cst[:, :], ins["consts"]).then_inc(s_in, 16)
                sp.dma_start(pcol[:, :, :], ins["pcols"]).then_inc(s_in, 16)
                sp.dma_start(mix0[:, :], ins["mix0"]).then_inc(s_in, 16)
                sp.dma_start(mix1[:, :], ins["mix1"]).then_inc(s_in, 16)
                sp.dma_start(rows[:, :], ins["rows"]).then_inc(s_in, 16)
                sp.dma_start(x[:, :, :], ins["x"].rearrange("(t p) d -> p t d", p=P)).then_inc(s_in, 16)
                sp.wait_ge(s_in, 96)

            @block.scalar
            def _(act):
                act.wait_ge(s_in, 96)
                nc.scalar.activation(pcol[:, 0, 0:KD], pcol[:, 0, 0:KD], ACT.Silu).then_inc(s_cond, 1)

        def ada_phase(layer):
            wv, at = view(0, (3, KD, D))
            acc = hT[:, 0:3, :]
            w_src = ins["ada_w"][layer].rearrange("c p (k n) -> c p k n", n=D)
            loaded = [sem(f"ada_w_loaded{q}") for q in range(3)]
            bias_loaded = sem("gate_bias_loaded")
            acc_ready = sem("ada_acc_ready")
            summed = sem("ada_summed")
            chain = sem("ada_chain")
            with nc.Block() as block:
                @block.sync
                def _(sp):
                    sp.dma_start(gate[:, :, :], ins["gate_bias"][layer]).then_inc(bias_loaded, 16)
                    with sp.Fori(0, 2) as i:
                        for q in range(3):
                            sp.wait_ge(acc_ready, i * 3 + 3)
                            sp.dma_start(wv[:, q], w_src[bass.ds(i * 3 + q, 1)].rearrange("c p k n -> p (c k) n")).then_inc(loaded[q], 16)

                @block.vector
                def _(dve):
                    dve.sem_inc(acc_ready, 3)
                    with dve.Fori(0, 2) as i:
                        st = Steps(dve, chain, turn=i, per=3 * (KD - 1))
                        for q in range(3):
                            dve.wait_ge(loaded[q], i * 16 + 16)
                            dve.wait_ge(summed, i * 3 + 3)
                            for k in range(KD):
                                ck = pcol[:, 0, k:k + 1]
                                if k == 0:
                                    op = nc.vector.tensor_scalar(acc[:, q], wv[:, q, k], ck, None, ALU.mult)
                                else:
                                    st.wait()
                                    op = nc.vector.scalar_tensor_tensor(acc[:, q], wv[:, q, k], ck, acc[:, q], ALU.mult, ALU.add)
                                if k < KD - 1:
                                    st.did(op)
                                else:
                                    op.then_inc(acc_ready, 1)
                        st.end()
                    dve.wait_ge(bias_loaded, 16)
                    dve.wait_ge(summed, 9)
                    ab = pcol[:, layer, PCOL["ada_b"][0]:PCOL["ada_b"][0] + N_MOD * KD].rearrange("p (h q k) -> p h q k", h=2, q=3)
                    sums = ps[:, 0, 0:2 * 2 * KD].rearrange("p (h q k) -> p h q k", h=2, q=2)
                    st = Steps(dve, chain, base=2 * 3 * (KD - 1))
                    st.did(nc.vector.tensor_tensor(modc[:, layer], sums, ab[:, :, 0:2], ALU.add))
                    nc.vector.tensor_tensor(gate[:, :, :], ps[:, 1:5, :].rearrange("p (h a) n -> p h (a n)", h=2), gate[:, :, :], ALU.add)
                    st.wait()
                    nrm = pcol[:, layer, PCOL["norm0"][0]:PCOL["norm0"][0] + 2 * KD].rearrange("p (h k) -> p h k", h=2)
                    for h in range(2):
                        nc.vector.scalar_tensor_tensor(modc[:, layer, h, 1], modc[:, layer, h, 1], 1.0, nrm[:, h], ALU.add, ALU.mult)

                @block.tensor
                def _(pe):
                    pe.sem_inc(summed, 3)
                    with pe.Fori(0, 2) as i:
                        for q in range(3):
                            pe.wait_ge(acc_ready, i * 3 + q + 4)
                            if q == 2:
                                for h in range(2):
                                    last = nc.tensor.matmul(ps[:, bass.ds(i * 2 + 1 + h, 1), :].rearrange("p a n -> p (a n)"), ones, acc[:, q, h * HALF:(h + 1) * HALF], start=True, stop=True)
                            else:
                                for k in range(KD):
                                    last = nc.tensor.matmul(ps[:, 0, bass.ds((i * 2 + q) * KD + k, 1)], acc[:, q, k * P:(k + 1) * P], ones[:, 0:1], start=True, stop=True)
                            last.then_inc(summed, 1)

        def norm_phase(layer, sub, rows_out):
            xn, at = view(0, (4, D))
            junk, at = view(at, (D,))
            squares = sem("squares_summed")
            rms = sem("rms_ready")
            rstd_ready = sem("rstd_ready")
            xn_ready = sem("xn_ready")
            turned = sem("transposed")
            by_act = sem("evacuated_by_scalar")
            by_dve = sem("evacuated_by_vector")
            stored = sem("rows_stored")
            ss, rstd = small[:, 0:NT], small[:, NT:2 * NT]
            shift, scale = modc[:, layer, sub, 0], modc[:, layer, sub, 1]
            with nc.Block() as block:
                @block.scalar
                def _(act):
                    act.sem_inc(by_act, 2)
                    act.sem_inc(squares, 1)
                    with act.Fori(0, NT) as t:
                        act.wait_ge(squares, t + 1)
                        nc.scalar.activation(junk, x[:, bass.ds(t, 1), :].rearrange("p a d -> p (a d)"), ACT.Square, accum_out=ss[:, bass.ds(t, 1)]).then_inc(squares, 1)
                    act.wait_ge(squares, NT + 1)
                    nc.scalar.activation(rstd, ss, ACT.Sqrt, bias=eps, scale=1.0 / D).then_inc(rms, 1)
                    with act.Fori(0, 2) as h:
                        for d in range(0, KD, 2):
                            act.wait_ge(turned, h * KD + d + KD + 1)
                            nc.scalar.activation(hT[:, d, bass.ds(h * HALF, HALF)], ps[:, d % 4], ACT.Identity, bias=shift[:, d:d + 1], scale=scale[:, d:d + 1]).then_inc(by_act, 1)

                @block.vector
                def _(dve):
                    dve.sem_inc(by_dve, 2)
                    dve.wait_ge(rms, 1)
                    nc.vector.reciprocal(rstd, rstd).then_inc(rstd_ready, 1)
                    dve.wait_ge(rstd_ready, 1)
                    with dve.Fori(0, 2) as h:
                        dve.wait_ge(turned, h * KD + KD)
                        if rows_out:
                            dve.wait_ge(stored, h * 16 + 16)
                        for u in range(4):
                            nc.vector.tensor_scalar(xn[:, u], x[:, bass.ds(h * 4 + u, 1), :].rearrange("p a d -> p (a d)"), rstd[:, bass.ds(h * 4 + u, 1)], None, ALU.mult).then_inc(xn_ready, 1)
                        for d in range(1, KD, 2):
                            dve.wait_ge(turned, h * KD + d + KD + 1)
                            nc.vector.tensor_scalar(hT[:, d, bass.ds(h * HALF, HALF)], ps[:, d % 4], scale[:, d:d + 1], shift[:, d:d + 1], ALU.mult, ALU.add).then_inc(by_dve, 1)

                @block.tensor
                def _(pe):
                    pe.sem_inc(turned, KD)
                    with pe.Fori(0, 2) as h:
                        pe.wait_ge(xn_ready, h * 4 + 4)
                        for d in range(KD):
                            pe.wait_ge(by_dve if d % 2 else by_act, h * 4 + d // 2 + 1)
                            for u in range(4):
                                last = nc.tensor.transpose(ps[:, d % 4, u * P:(u + 1) * P], xn[:, u, d * P:(d + 1) * P], ident)
                            last.then_inc(turned, 1)

                if rows_out:
                    @block.sync
                    def _(sp):
                        sp.sem_inc(stored, 16)
                        with sp.Fori(0, 2) as h:
                            sp.wait_ge(xn_ready, h * 4 + 4)
                            sp.dma_start(hrows[bass.ds(h * HALF, HALF), :].rearrange("(u p) d -> p u d", p=P), xn).then_inc(stored, 16)
                        sp.wait_ge(stored, 48)

        def moe_phase(layer, last_layer):
            sub = 1
            rw, at = view(0, (KD, E))
            score, at = view(at, (NT, E))
            aff, at = view(at, (NT, E))
            cmpa, at = view(at, (NT * G, J, J))
            cmpb, at = view(at, (NT * G, J, J))
            rank, at = view(at, (NT * G, J))
            sel, at = view(at, (NT * G, J))
            gs, at = view(at, (NT, G))
            gsel, at = view(at, (NT, G))
            gmax, at = view(at, (NT,))
            oh, at = view(at, (2, NT, E))
            both, at = view(at, (NT, E))
            off, at = view(at, (NT + 1, E))
            pos, at = view(at, (NT, E))
            nch_c, at = view(at, (E, NT))
            nch, at = view(at, (E,))
            st16, at = view(at, (E, E))
            first, at = view(at, (E,))
            ends, at = view(at, (E,))
            prod, at = view(at, (2, NT, E))
            dest, at = view(at, (2 * NT,))
            ge, at = view(at, (2 * NT, SLOTS))
            hi, at = view(at, (2 * NT,))
            lo, at = view(at, (2 * NT,))
            tv, at = view(at, (2 * NT, SLOTS))
            oh_lo, at = view(at, (2 * NT, P))
            ce, at = view(at, (SLOTS, E))
            cef, at = view(at, (SLOTS,))
            wsel = small[:, 16:32]
            dest_i = small[:, 32:48].bitcast(u32)
            slot_i = small[:, 48:48 + SLOTS + 1].bitcast(u32)
            exp_i = small[:, 96:96 + SLOTS].bitcast(i32)
            wsum = small[:, 130:138]
            rw_loaded = sem("router_w_loaded")
            logits = sem("router_logits")
            affs = sem("affinities")
            routed = sem("routed")
            counted = sem("counted")
            placed = sem("slots_placed")
            tabled = sem("slot_table")
            chain = sem("route_chain")
            with nc.Block() as block:
                @block.sync
                def _(sp):
                    sp.dma_start(rw, ins["router_w"].rearrange("(k p) e -> p k e", p=P)).then_inc(rw_loaded, 16)

                @block.tensor
                def _(pe):
                    pe.wait_ge(rw_loaded, 16)
                    for t in range(NT):
                        for k in range(KD):
                            last = nc.tensor.matmul(ps[:, 0, t * E:(t + 1) * E], hT[:, k, t * P:(t + 1) * P], rw[:, k], start=(k == 0), stop=(k == KD - 1))
                    last.then_inc(logits, 1)
                    pe.wait_ge(routed, 1)
                    bf = both.rearrange("p t e -> p (t e)")
                    nc.tensor.matmul(ps[:, 1, 0:P], const("tri_strict"), bf, start=True, stop=True)
                    nc.tensor.matmul(ps[:, 2, 0:P], ones, bf, start=True, stop=True).then_inc(counted, 1)
                    pe.wait_ge(placed, 1)
                    for n in range(2 * NT):
                        last = nc.tensor.matmul(ps[:, 3, 0:SLOTS], oh_lo[:, n], tv[:, n], start=(n == 0), stop=(n == 2 * NT - 1))
                    last.then_inc(tabled, 1)

                @block.scalar
                def _(act):
                    act.wait_ge(logits, 1)
                    nc.scalar.activation(aff.rearrange("p t e -> p (t e)"), ps[:, 0, 0:NT * E], ACT.Sigmoid).then_inc(affs, 1)

                @block.vector
                def _(dve):
                    v = nc.vector
                    st = Steps(dve, chain)
                    dve.wait_ge(affs, 1)
                    st.link(v.tensor_tensor(score, aff, bc(rows[:, 0:E], 1, NT), ALU.add))
                    sg = score.rearrange("p t (g j) -> p (t g) j", g=G)
                    st.did(v.tensor_tensor(cmpa, bc(sg, 2, J), bc(sg, 3, J), ALU.is_gt))
                    st.link(v.tensor_tensor(cmpb, bc(sg, 2, J), bc(sg, 3, J), ALU.is_equal))
                    st.link(v.tensor_tensor(cmpb, cmpb, bc(const("before4").rearrange("p (a b) -> p a b", b=J), 1, NT * G), ALU.mult))
                    st.link(v.tensor_tensor(cmpa, cmpa, cmpb, ALU.add))
                    st.link(v.tensor_reduce(rank, cmpa, X, ALU.add))
                    st.link(v.scalar_tensor_tensor(sel, rank, float(TOPK), sg, ALU.is_lt, ALU.mult))
                    st.link(v.tensor_reduce(gs, sel.rearrange("p (t g) j -> p t g j", g=G), X, ALU.add))
                    st.link(v.tensor_reduce(gmax, gs, X, ALU.max))
                    st.link(v.tensor_tensor(gsel, gs, bc(gmax, 2, G), ALU.is_equal))
                    gk = bc(const("group_key"), 1, NT)
                    st.link(v.tensor_tensor(gsel, gsel, gk, ALU.mult))
                    st.link(v.tensor_reduce(gmax, gsel, X, ALU.max))
                    st.link(v.tensor_tensor(gsel, gk, bc(gmax, 2, G), ALU.is_equal))
                    gflat = bc(gsel.rearrange("p t g -> p (t g)"), 2, J)
                    for k in range(2):
                        st.did(v.scalar_tensor_tensor(oh[:, k].rearrange("p t (g j) -> p (t g) j", g=G), rank, float(k), gflat, ALU.is_equal, ALU.mult))
                    st.wait()
                    v.tensor_tensor(both, oh[:, 0], oh[:, 1], ALU.add).then_inc(routed, 1)
                    st.link(v.tensor_tensor(prod, oh, bc(aff, 1, 2), ALU.mult))
                    w2 = wsel.rearrange("p (k t) -> p k t", k=2)
                    st.link(v.tensor_reduce(w2, prod, X, ALU.add))
                    st.link(v.tensor_tensor(wsum, w2[:, 0], w2[:, 1], ALU.add))
                    st.link(v.reciprocal(wsum, wsum))
                    st.link(v.tensor_tensor(w2, w2, bc(wsum, 1, 2), ALU.mult))
                    dve.wait_ge(counted, 1)
                    tot = ps[:, 2, 0:P].rearrange("p (t e) -> p t e", e=E)
                    st.link(v.memset(off[:, 0], 0.0))
                    for t in range(NT):
                        st.link(v.tensor_tensor(off[:, t + 1], tot[:, t], off[:, t], ALU.add))
                    st.link(v.tensor_tensor(nch_c, bc(off[:, NT], 2, NT), bc(const("step128"), 1, E), ALU.is_gt))
                    st.link(v.tensor_reduce(nch, nch_c, X, ALU.add))
                    st.link(v.tensor_tensor(st16, const("before16").rearrange("p (a b) -> p a b", b=E), bc(nch, 1, E), ALU.mult))
                    st.link(v.tensor_reduce(first, st16, X, ALU.add))
                    st.did(v.tensor_tensor(ends, first, nch, ALU.add))
                    st.link(v.tensor_tensor(pos, ps[:, 1, 0:P].rearrange("p (t e) -> p t e", e=E), off[:, 0:NT], ALU.add))
                    st.link(v.scalar_tensor_tensor(pos, bc(first, 1, NT), float(P), pos, ALU.mult, ALU.add))
                    st.link(v.tensor_tensor(prod, oh, bc(pos, 1, 2), ALU.mult))
                    st.link(v.tensor_reduce(dest.rearrange("p (k t) -> p k t", k=2), prod, X, ALU.add))
                    st.did(v.tensor_copy(dest_i, dest))
                    st.link(v.tensor_tensor(ge, bc(dest, 2, SLOTS), bc(const("chunk_end"), 1, 2 * NT), ALU.is_ge))
                    st.link(v.tensor_reduce(hi, ge, X, ALU.add))
                    st.link(v.scalar_tensor_tensor(lo, hi, -float(P), dest, ALU.mult, ALU.add))
                    st.did(v.tensor_tensor(tv, bc(hi, 2, SLOTS), bc(const("iota_chunk"), 1, 2 * NT), ALU.is_equal))
                    st.link(v.tensor_tensor(oh_lo, bc(lo, 2, P), bc(const("iota128"), 1, 2 * NT), ALU.is_equal))
                    tid = bc(bc(const("token_id"), 1, 2), 3, SLOTS)
                    v.tensor_tensor(tv.rearrange("p (k t) c -> p k t c", k=2), tv.rearrange("p (k t) c -> p k t c", k=2), tid, ALU.mult).then_inc(placed, 1)
                    st.link(v.tensor_tensor(ce, bc(ends, 1, SLOTS), bc(const("iota_chunk"), 2, E), ALU.is_le))
                    st.link(v.tensor_reduce(cef, ce, X, ALU.add))
                    st.did(v.tensor_scalar(exp_i, cef, float(E - 1), None, ALU.min))
                    st.did(v.memset(slot_i[:, SLOTS:SLOTS + 1], 0))
                    dve.wait_ge(tabled, 1)
                    st.did(v.tensor_copy(slot_i[:, 0:SLOTS], ps[:, 3, 0:SLOTS]))

            wg, at = view(0, (2, KD, FF))
            wu, at = view(at, (2, KD, FF))
            wd, at = view(at, (2, FT, D))
            xg, at = view(at, (2, D))
            ysb, at = view(at, (2, D))
            xgT = hT[:, 0, :].rearrange("p (k n) -> p k n", n=P)
            sg_, act_ = hT[:, 1, 0:HALF], hT[:, 1, HALF:2 * HALF]
            idx = [small[:, 140:141].bitcast(u32), small[:, 141:142].bitcast(u32)]
            shift, scale = modc[:, layer, sub, 0], modc[:, layer, sub, 1]
            g_loaded = [sem("gate_w_loaded0"), sem("gate_w_loaded1")]
            u_loaded = [sem("up_w_loaded0"), sem("up_w_loaded1")]
            d_loaded = [sem("down_w_loaded0"), sem("down_w_loaded1")]
            g_done, u_done, d_done = sem("gate_done"), sem("up_done"), sem("down_done")
            idx_ready = sem("index_ready")
            idx_seen = sem("index_seen")
            gathered = [sem("gathered0"), sem("gathered1")]
            turned = sem("gathered_transposed")
            xa, xv = sem("xgT_by_scalar"), sem("xgT_by_vector")
            silu_done, act_ready = sem("silu_done"), sem("hidden_ready")
            y_act, y_dve = sem("y_by_scalar"), sem("y_by_vector")
            y_stored = [sem("y_stored0"), sem("y_stored1")]
            dve_busy = sem("moe_chain")
            with nc.Block() as block:
                @block.sync
                def _(sp):
                    with sp.Fori(0, SLOTS // 2) as i:
                        for s in range(2):
                            e = sp.value_load(exp_i[0:1, bass.ds(i * 2 + s, 1)], min_val=0, max_val=E - 1)
                            sp.wait_ge(g_done, i * 2 + s + 1)
                            sp.dma_start(wg[:, s].rearrange("p k n -> p (k n)"), ins["exp_g"][layer][bass.ds(e, 1)].rearrange("e p n -> p (e n)")).then_inc(g_loaded[s], 16)
                            sp.wait_ge(u_done, i * 2 + s + 1)
                            sp.dma_start(wu[:, s].rearrange("p k n -> p (k n)"), ins["exp_u"][layer][bass.ds(e, 1)].rearrange("e p n -> p (e n)")).then_inc(u_loaded[s], 16)
                            sp.wait_ge(d_done, i * 2 + s + 1)
                            sp.dma_start(wd[:, s].rearrange("p k n -> p (k n)"), ins["exp_d"][layer][bass.ds(e, 1)].rearrange("e p n -> p (e n)")).then_inc(d_loaded[s], 16)

                @block.gpsimd
                def _(pool):
                    def gather(j, s):
                        pool.wait_ge(turned, j + 1)
                        nc.gpsimd.tensor_copy(idx[s], slot_i[:, bass.ds(j, 1)]).then_inc(idx_ready, 1)
                        pool.wait_ge(idx_ready, j + 1)
                        pool.sem_inc(idx_seen, 1)
                        nc.gpsimd.indirect_dma_start(out=xg[:, s], out_offset=None, in_=hrows[:, :],
                                                     in_offset=bass.IndirectOffsetOnAxis(ap=idx[s], axis=0)).then_inc(gathered[s], 16)

                    with pool.Fori(0, SLOTS // 2) as i:
                        for s in range(2):
                            gather(i * 2 + s, s)
                    gather(SLOTS, 0)

                @block.tensor
                def _(pe):
                    def transposes(s, n):
                        pe.wait_ge(gathered[s], n * 16 + 16)
                        for k in range(KD):
                            last = nc.tensor.transpose(ps[:, k // 4, (k % 4) * P:(k % 4 + 1) * P], xg[:, s, k * P:(k + 1) * P], ident)
                        last.then_inc(turned, 1)

                    pe.sem_inc(g_done, 2)
                    pe.sem_inc(u_done, 2)
                    pe.sem_inc(d_done, 2)
                    pe.sem_inc(turned, 2)
                    transposes(0, 0)
                    with pe.Fori(0, SLOTS // 2) as i:
                        for s in range(2):
                            j = i * 2 + s
                            pe.wait_ge(xa, j + 1)
                            pe.wait_ge(xv, j + 1)
                            pe.wait_ge(g_loaded[s], i * 16 + 16)
                            for f in range(FT):
                                for k in range(KD):
                                    last = nc.tensor.matmul(ps[:, 2, f * P:(f + 1) * P], wg[:, s, k, f * P:(f + 1) * P], xgT[:, k], start=(k == 0), stop=(k == KD - 1))
                            last.then_inc(g_done, 1)
                            pe.wait_ge(u_loaded[s], i * 16 + 16)
                            for f in range(FT):
                                for k in range(KD):
                                    last = nc.tensor.matmul(ps[:, 3, f * P:(f + 1) * P], wu[:, s, k, f * P:(f + 1) * P], xgT[:, k], start=(k == 0), stop=(k == KD - 1))
                            last.then_inc(u_done, 1)
                            transposes(1 - s, i if s == 0 else i + 1)
                            pe.wait_ge(act_ready, j + 2)
                            pe.wait_ge(d_loaded[s], i * 16 + 16)
                            pe.wait_ge(y_act, j + 1)
                            pe.wait_ge(y_dve, j + 1)
                            for h in range(2):
                                for f in range(FT):
                                    last = nc.tensor.matmul(ps[:, 4 + h], act_[:, f * P:(f + 1) * P], wd[:, s, f, h * HALF:(h + 1) * HALF], start=(f == 0), stop=(f == FT - 1))
                            last.then_inc(d_done, 1)

                @block.scalar
                def _(act):
                    def evacuate(n):
                        act.wait_ge(turned, n + 3)
                        for k in range(4):
                            last = nc.scalar.activation(xgT[:, k], ps[:, 0, k * P:(k + 1) * P], ACT.Identity, bias=shift[:, k:k + 1], scale=scale[:, k:k + 1])
                        last.then_inc(xa, 1)

                    act.sem_inc(y_act, 1)
                    act.sem_inc(y_stored[0], 16)
                    act.sem_inc(y_stored[1], 16)
                    evacuate(0)
                    with act.Fori(0, SLOTS // 2) as i:
                        for s in range(2):
                            j = i * 2 + s
                            act.wait_ge(g_done, j + 3)
                            act.wait_ge(act_ready, j + 1)
                            nc.scalar.activation(sg_, ps[:, 2], ACT.Silu).then_inc(silu_done, 1)
                            evacuate(j + 1)
                            act.wait_ge(d_done, j + 3)
                            act.wait_ge(y_stored[s], i * 16 + 16)
                            nc.scalar.copy(ysb[:, s, 0:HALF], ps[:, 4]).then_inc(y_act, 1)
                            act.wait_ge(y_act, j + 2)
                            act.wait_ge(y_dve, j + 2)
                            act.dma_start(yrows[bass.ds(j * P, P), :], ysb[:, s]).then_inc(y_stored[s], 16)
                    for s in range(2):
                        act.wait_ge(y_stored[s], SLOTS // 2 * 16 + 16)

                @block.vector
                def _(dve):
                    def evacuate(n):
                        dve.wait_ge(turned, n + 3)
                        for k in range(4, KD):
                            last = nc.vector.tensor_scalar(xgT[:, k], ps[:, 1, (k - 4) * P:(k - 3) * P], scale[:, k:k + 1], shift[:, k:k + 1], ALU.mult, ALU.add)
                        last.then_inc(xv, 1)

                    dve.sem_inc(y_dve, 1)
                    dve.sem_inc(act_ready, 1)
                    evacuate(0)
                    with dve.Fori(0, SLOTS // 2) as i:
                        for s in range(2):
                            j = i * 2 + s
                            dve.wait_ge(u_done, j + 3)
                            dve.wait_ge(silu_done, j + 1)
                            dve.wait_ge(d_done, j + 2)
                            nc.vector.tensor_tensor(act_, ps[:, 3], sg_, ALU.mult).then_inc(act_ready, 1)
                            evacuate(j + 1)
                            dve.wait_ge(d_done, j + 3)
                            dve.wait_ge(y_stored[s], i * 16 + 16)
                            nc.vector.tensor_copy(ysb[:, s, HALF:D], ps[:, 5]).then_inc(y_dve, 1)


            y0, at = view(0, (2, D))
            y1, at = view(at, (2, D))
            ta, at = view(at, (2, D))
            idxs = small[:, 142:146].bitcast(u32)
            idx2_ready = sem("index2_ready")
            idx2_seen = sem("index2_seen")
            got = [sem("y_gathered0"), sem("y_gathered1")]
            w0_done, x_done = sem("y0_weighted"), sem("x_updated")
            chain2 = sem("combine_chain")
            o_stored = sem("out_stored")
            with nc.Block() as block:
                @block.gpsimd
                def _(pool):
                    with pool.Fori(0, NT // 2) as i:
                        for s in range(2):
                            t = i * 2 + s
                            pool.wait_ge(x_done, i * 2 + 2)
                            for k in range(2):
                                nc.gpsimd.tensor_copy(idxs[:, 2 * s + k:2 * s + k + 1], dest_i[:, bass.ds(t + k * NT, 1)]).then_inc(idx2_ready, 1)
                            pool.wait_ge(idx2_ready, t * 2 + 2)
                            pool.sem_inc(idx2_seen, 1)
                            for k, y in enumerate((y0, y1)):
                                nc.gpsimd.indirect_dma_start(out=y[:, s], out_offset=None, in_=yrows[:, :],
                                                             in_offset=bass.IndirectOffsetOnAxis(ap=idxs[:, 2 * s + k:2 * s + k + 1], axis=0)).then_inc(got[s], 16)

                @block.scalar
                def _(act):
                    with act.Fori(0, NT // 2) as i:
                        for s in range(2):
                            act.wait_ge(got[s], i * 32 + 32)
                            act.wait_ge(x_done, i * 2 + 2)
                            nc.scalar.activation(ta[:, s], y0[:, s], ACT.Copy, scale=wsel[:, bass.ds(i * 2 + s, 1)]).then_inc(w0_done, 1)

                @block.vector
                def _(dve):
                    dve.sem_inc(x_done, 2)
                    with dve.Fori(0, NT // 2) as i:
                        st = Steps(dve, chain2, turn=i, per=4)
                        for s in range(2):
                            dve.wait_ge(got[s], i * 32 + 32)
                            dve.wait_ge(w0_done, i * 2 + s + 1)
                            xt = x[:, bass.ds(i * 2 + s, 1), :].rearrange("p a d -> p (a d)")
                            st.link(nc.vector.scalar_tensor_tensor(ta[:, s], y1[:, s], wsel[:, bass.ds(i * 2 + s + NT, 1)], ta[:, s], ALU.mult, ALU.add))
                            st.link(nc.vector.tensor_tensor(ta[:, s], ta[:, s], gate[:, 1], ALU.mult))
                            nc.vector.tensor_tensor(xt, xt, ta[:, s], ALU.add).then_inc(x_done, 1)
                        st.end()

                if last_layer:
                    @block.sync
                    def _(sp):
                        with sp.Fori(0, NT) as t:
                            sp.wait_ge(x_done, t + 3)
                            sp.dma_start(out[0, bass.ds(t * P, P), :], x[:, bass.ds(t, 1), :].rearrange("p a d -> p (a d)")).then_inc(o_stored, 16)
                        sp.wait_ge(o_stored, NT * 16)

        def hybrid_phase(layer):
            QW = 2 * P
            qkv, at = view(0, (3, NT, ATT_W))
            upad, at = view(at, (CT, SEQ + CONV_W - 1))
            conv, at = view(at, (CT, SEQ))
            wring, at = view(at, (2, KD * QW))
            sgm, at = view(at, (2, HALF))
            par = {k: mix0[:, v[0]:v[0] + v[1]] for k, v in MIX0.items()}
            dw = par["dw_w"].rearrange("p (c j) -> p c j", j=CONV_W)
            w_loaded = [sem("w_in_loaded0"), sem("w_in_loaded1")]
            w_used = sem("w_in_used")
            u_done = sem("conv_product_done")
            sig_done, a_done = sem("sigmoid_done"), sem("a_copied")
            glu_done = sem("glu_done")
            qkv_done, qkv_out = sem("qkv_block_done"), sem("qkv_evacuated")
            padded = sem("pad_zeroed")
            chain = sem("conv_chain")
            NU, NB = CT, 3 * ATT_W // QW
            with nc.Block() as block:
                @block.sync
                def _(sp):
                    with sp.Fori(0, (NU + NB) // 2) as i:
                        for s in range(2):
                            sp.wait_ge(w_used, i * 2 + s + 1)
                            sp.dma_start(wring[:, s], ins["hy_in"][bass.ds(i * 2 + s, 1)].rearrange("c p n -> p (c n)")).then_inc(w_loaded[s], 16)

                @block.tensor
                def _(pe):
                    pe.sem_inc(w_used, 2)
                    with pe.Fori(0, NU // 2) as i:
                        for s in range(2):
                            w = wring[:, s].rearrange("p (k n) -> p k n", n=QW)
                            pe.wait_ge(w_loaded[s], i * 16 + 16)
                            pe.wait_ge(sig_done, i * 4 + 4)
                            pe.wait_ge(a_done, i * 4 + 4)
                            for h in range(2):
                                for q in range(2):
                                    for k in range(KD):
                                        last = nc.tensor.matmul(ps[:, s * 4 + h * 2 + q], w[:, k, q * P:(q + 1) * P], hT[:, k, h * HALF:(h + 1) * HALF], start=(k == 0), stop=(k == KD - 1))
                                last.then_inc(u_done, 1)
                            pe.wait_ge(u_done, i * 4 + s * 2 + 2)
                            pe.sem_inc(w_used, 1)
                    pe.wait_ge(sig_done, NU * 2 + 4)
                    pe.wait_ge(a_done, NU * 2 + 4)
                    with pe.Fori(0, NB // 2) as i:
                        for s in range(2):
                            w = wring[:, s].rearrange("p (k n) -> p k n", n=QW)
                            pe.wait_ge(w_loaded[s], i * 16 + 16 * (NU // 2 + 1))
                            for t in range(NT):
                                pe.wait_ge(qkv_out, i * 2 * NT + s * NT + t + 1)
                                for k in range(KD):
                                    last = nc.tensor.matmul(ps[:, t, 0:QW], hT[:, k, t * P:(t + 1) * P], w[:, k], start=(k == 0), stop=(k == KD - 1))
                                last.then_inc(qkv_done, 1)
                            pe.wait_ge(qkv_done, i * 2 * NT + (s + 1) * NT)
                            pe.sem_inc(w_used, 1)

                @block.scalar
                def _(act):
                    act.sem_inc(qkv_out, NT)
                    act.sem_inc(sig_done, 4)
                    act.sem_inc(a_done, 4)
                    with act.Fori(0, NU // 2) as i:
                        for s in range(2):
                            for h in range(2):
                                n = i * 4 + s * 2 + h
                                act.wait_ge(u_done, n + 1)
                                act.wait_ge(glu_done, i * 4 + s * 2 + 2)
                                nc.scalar.activation(sgm[:, h], ps[:, s * 4 + h * 2 + 1], ACT.Sigmoid).then_inc(sig_done, 1)
                                nc.scalar.copy(upad[:, bass.ds(i * 2 + s, 1), CONV_W - 1 + h * HALF:CONV_W - 1 + (h + 1) * HALF].rearrange("p a n -> p (a n)"), ps[:, s * 4 + h * 2]).then_inc(a_done, 1)
                    with act.Fori(0, NB // 2) as i:
                        for s in range(2):
                            for t in range(NT):
                                act.wait_ge(qkv_done, i * 2 * NT + s * NT + t + 1)
                                nc.scalar.copy(qkv[:, bass.ds(i, 1), t, s * QW:(s + 1) * QW].rearrange("p a n -> p (a n)"), ps[:, t, 0:QW]).then_inc(qkv_out, 1)

                @block.gpsimd
                def _(pool):
                    pool.sem_inc(glu_done, 2)
                    with pool.Fori(0, NU) as c:
                        for h in range(2):
                            pool.wait_ge(sig_done, c * 2 + h + 5)
                            pool.wait_ge(a_done, c * 2 + h + 5)
                            u = upad[:, bass.ds(c, 1), CONV_W - 1 + h * HALF:CONV_W - 1 + (h + 1) * HALF].rearrange("p a n -> p (a n)")
                            nc.gpsimd.tensor_tensor(u, u, sgm[:, h], ALU.mult).then_inc(glu_done, 1)

                @block.vector
                def _(dve):
                    nc.vector.memset(upad[:, :, 0:CONV_W - 1], 0.0).then_inc(padded, 1)
                    dve.wait_ge(padded, 1)
                    with dve.Fori(0, CT) as c:
                        dve.wait_ge(glu_done, c * 2 + 4)
                        st = Steps(dve, chain, turn=c, per=CONV_W)
                        y = conv[:, bass.ds(c, 1), :].rearrange("p a n -> p (a n)")
                        for j in range(CONV_W):
                            u = upad[:, bass.ds(c, 1), j:j + SEQ].rearrange("p a n -> p (a n)")
                            w = dw[:, bass.ds(c, 1), j]
                            if j == 0:
                                st.link(nc.vector.tensor_scalar(y, u, w, par["dw_b"][:, bass.ds(c, 1)], ALU.mult, ALU.add))
                            else:
                                st.link(nc.vector.scalar_tensor_tensor(y, u, w, y, ALU.mult, ALU.add))
                        st.end()

            sq, _ = view(at - 2 * HALF - 2 * KD * QW, (CT, HALF))
            mu = hT[:, 0, 0:HALF]
            sd = hT[:, 1, 0:HALF]
            qsq = hT[:, 2:6, :].rearrange("p a b -> p (a b)")
            rqk = small[:, 16:16 + 2 * NT * HEADS]
            gq8 = small[:, 150:151]
            summed, centred, sq_done, var_sum = sem("ln_summed"), sem("centred"), sem("ln_squared"), sem("ln_var_summed")
            sd_done, normed = sem("ln_sd"), sem("ln_normed")
            qsq_done, qss_done, qrms = sem("qk_squared"), sem("qk_summed"), sem("qk_rms")
            chain = sem("ln_chain")
            wo_loaded = sem("w_out_loaded")
            with nc.Block() as block:
                @block.tensor
                def _(pe):
                    for h in range(2):
                        cols = slice(h * HALF, (h + 1) * HALF)
                        for c in range(CT):
                            last = nc.tensor.matmul(ps[:, h], ones, conv[:, c, cols], start=(c == 0), stop=(c == CT - 1))
                        last.then_inc(summed, 1)
                        pe.wait_ge(sq_done, h + 1)
                        for c in range(CT):
                            last = nc.tensor.matmul(ps[:, 2 + h], ones, sq[:, c], start=(c == 0), stop=(c == CT - 1))
                        last.then_inc(var_sum, 1)

                @block.vector
                def _(dve):
                    st = Steps(dve, chain)
                    for h in range(2):
                        y = conv[:, :, h * HALF:(h + 1) * HALF]
                        dve.wait_ge(summed, h + 1)
                        st.link(nc.vector.tensor_scalar(mu, ps[:, h], 1.0 / CONV_CH, None, ALU.mult))
                        nc.vector.tensor_tensor(y, y, bc(mu, 1, CT), ALU.subtract).then_inc(centred, 1)
                        dve.wait_ge(centred, h + 1)
                        dve.wait_ge(sd_done, h + 1)
                        st.link(nc.vector.reciprocal(sd, sd))
                        nc.vector.tensor_tensor(y, y, bc(sd, 1, CT), ALU.mult).then_inc(normed, 1)
                        dve.wait_ge(normed, h + 1)
                    for n in range(2):
                        dve.wait_ge(qsq_done, n + 1)
                        nc.vector.tensor_reduce(rqk[:, n * NT * HEADS:(n + 1) * NT * HEADS], qsq.rearrange("p (a d) -> p a d", d=HD), X, ALU.add).then_inc(qss_done, 1)
                    dve.wait_ge(qrms, 1)
                    st.did(nc.vector.reciprocal(rqk, rqk))
                    st.did(nc.vector.tensor_scalar(gq8, par["gq"], float(HD) ** -0.5, None, ALU.mult))

                @block.scalar
                def _(act):
                    for h in range(2):
                        act.wait_ge(centred, h + 1)
                        if h:
                            act.wait_ge(var_sum, h)
                        nc.scalar.activation(sq, conv[:, :, h * HALF:(h + 1) * HALF], ACT.Square).then_inc(sq_done, 1)
                        act.wait_ge(var_sum, h + 1)
                        if h:
                            act.wait_ge(normed, h)
                        nc.scalar.activation(sd, ps[:, 2 + h], ACT.Sqrt, bias=eps, scale=1.0 / CONV_CH).then_inc(sd_done, 1)
                    act.wait_ge(normed, 2)
                    for c in range(CT):
                        nc.scalar.activation(conv[:, c], conv[:, c], ACT.Silu, bias=par["ln_b"][:, c:c + 1], scale=par["ln_g"][:, c:c + 1])
                    for n in range(2):
                        if n:
                            act.wait_ge(qss_done, n)
                        nc.scalar.activation(qsq, qkv[:, n].rearrange("p t d -> p (t d)"), ACT.Square).then_inc(qsq_done, 1)
                    act.wait_ge(qss_done, 2)
                    nc.scalar.activation(rqk, rqk, ACT.Sqrt, bias=eps, scale=1.0 / HD).then_inc(qrms, 1)

            at = NT * ATT_W * 3
            attT, at = view(at, (PAIRS, SEQ))
            at = NT * ATT_W * 3 + CT * (SEQ + CONV_W - 1) + CT * SEQ
            qn, at = view(at, (NT, P))
            kn, at = view(at, (NT, P))
            qT, at = view(at, (SEQ,))
            kT, at = view(at, (SEQ,))
            pr, at = view(at, (2, SEQ))
            pT, at = view(at, (2, SEQ))
            att, at = view(at, (NT, P))
            nmax = small[:, 152:154]
            rsum = small[:, 156:160]
            U = 2 * NT
            qk_ready, qk_turned = sem("qk_normed"), sem("qk_transposed")
            qT_ready, kT_ready = sem("qT_ready"), sem("kT_ready")
            s_done, m_done, p_done = sem("scores_ready"), sem("max_ready"), sem("probs_ready")
            t_done, pa, pb = sem("probs_transposed"), sem("pT_by_vector"), sem("pT_by_scalar")
            o_done, o_out = sem("pv_ready"), sem("out_normed")
            att_turned, att_out = sem("att_transposed"), sem("attT_ready")
            chain = sem("attention_chain")
            with nc.Block() as block:
                @block.sync
                def _(sp):
                    sp.dma_start(hT[:, :, :].rearrange("p k n -> p (k n)"), ins["hy_out"]).then_inc(wo_loaded, 16)
                    sp.wait_ge(wo_loaded, 16)

                @block.gpsimd
                def _(pool):
                    with pool.Fori(0, PAIRS) as i:
                        pool.wait_ge(att_out, i + 1)
                        for n, dst in enumerate((qn, kn)):
                            r = rqk[:, n * NT * HEADS:(n + 1) * NT * HEADS].rearrange("p (t h) -> p t h", h=HEADS)
                            for hh in range(2):
                                src = qkv[:, n, :, bass.ds(i * P + hh * HD, HD)]
                                nc.gpsimd.tensor_tensor(dst[:, :, hh * HD:(hh + 1) * HD], src, r[:, :, bass.ds(i * 2 + hh, 1)].to_broadcast([P, NT, HD]), ALU.mult).then_inc(qk_ready, 1)

                @block.tensor
                def _(pe):
                    with pe.Fori(0, PAIRS) as i:
                        for n, src in enumerate((qn, kn)):
                            pe.wait_ge(qk_ready, i * 4 + 2 * n + 2)
                            for t in range(NT):
                                last = nc.tensor.transpose(ps[:, 4 + 2 * n + t // 4, (t % 4) * P:(t % 4 + 1) * P], src[:, t], ident)
                            last.then_inc(qk_turned, 1)
                        pe.wait_ge(qT_ready, i + 1)
                        pe.wait_ge(kT_ready, i + 1)

                        def scores(u):
                            head, qt = divmod(u, NT)
                            rows_ = slice(head * HD, (head + 1) * HD)
                            b = (u % 2) * 2
                            if u >= 2:
                                pe.wait_ge(p_done, i * U + u - 1)
                            for h in range(0, (qt + 1) * P, HALF):
                                n = min(HALF, (qt + 1) * P - h)
                                diag = h + n == (qt + 1) * P
                                last = nc.tensor.matmul(ps[:, b + h // HALF, 0:n], qT[rows_, qt * P:(qt + 1) * P], kT[rows_, h:h + n], start=True, stop=True)
                                if diag:
                                    last = nc.tensor.matmul(ps[:, b + h // HALF, n - P:n], ident, const("maskneg"), start=False, stop=True, skip_group_check=True)
                            last.then_inc(s_done, 1)

                        def turn(u):
                            qt = u % NT
                            pe.wait_ge(p_done, i * U + u + 1)
                            if u:
                                pe.wait_ge(pa, i * U + u)
                                pe.wait_ge(pb, i * U + u)
                            for k in range(qt + 1):
                                last = nc.tensor.transpose(ps[:, 4 + k // 4, (k % 4) * P:(k % 4 + 1) * P], pr[:, u % 2, k * P:(k + 1) * P], ident)
                            last.then_inc(t_done, 1)

                        def values(u):
                            head, qt = divmod(u, NT)
                            pe.wait_ge(pa, i * U + u + 1)
                            pe.wait_ge(pb, i * U + u + 1)
                            if u >= 2:
                                pe.wait_ge(o_out, i * U + u - 1)
                            for k in range(qt + 1):
                                last = nc.tensor.matmul(ps[:, 6 + u % 2, 0:HD], pT[:, u % 2, k * P:(k + 1) * P], qkv[:, 2, k, bass.ds(i * P + head * HD, HD)], start=(k == 0), stop=(k == qt))
                            last.then_inc(o_done, 1)

                        scores(0)
                        scores(1)
                        for u in range(U):
                            turn(u)
                            if u + 2 < U:
                                scores(u + 2)
                            if u:
                                values(u - 1)
                        values(U - 1)
                        pe.wait_ge(o_out, i * U + U)
                        for t in range(NT):
                            last = nc.tensor.transpose(ps[:, 4 + t // 4, (t % 4) * P:(t % 4 + 1) * P], att[:, t], ident)
                        last.then_inc(att_turned, 1)
                        pe.wait_ge(att_out, i + 2)

                @block.scalar
                def _(act):
                    with act.Fori(0, PAIRS) as i:
                        act.wait_ge(qk_turned, i * 2 + 1)
                        nc.scalar.activation(qT, ps[:, 4:6].rearrange("p a n -> p (a n)"), ACT.Copy, scale=gq8).then_inc(qT_ready, 1)

                        def probs(u):
                            n = (u % NT + 1) * P
                            act.wait_ge(m_done, i * U + u + 1)
                            if u >= 2:
                                act.wait_ge(t_done, i * U + u - 1)
                            if u >= 4:
                                act.wait_ge(o_out, i * U + u - 3)
                            b = (u % 2) * 2
                            nc.scalar.activation(pr[:, u % 2, 0:n], ps[:, b:b + 2].rearrange("p a n -> p (a n)")[:, 0:n], ACT.Exp, bias=nmax[:, u % 2:u % 2 + 1], accum_out=rsum[:, u % 4:u % 4 + 1]).then_inc(p_done, 1)

                        probs(0)
                        for u in range(U):
                            if u + 1 < U:
                                probs(u + 1)
                            act.wait_ge(t_done, i * U + u + 1)
                            n = (u % NT + 1) * P
                            if n > HALF:
                                if u >= 2:
                                    act.wait_ge(o_done, i * U + u - 1)
                                nc.scalar.copy(pT[:, u % 2, HALF:n], ps[:, 5, 0:n - HALF]).then_inc(pb, 1)
                            else:
                                act.sem_inc(pb, 1)
                        act.wait_ge(att_out, i + 2)

                @block.vector
                def _(dve):
                    dve.sem_inc(att_out, 1)
                    with dve.Fori(0, PAIRS) as i:
                        st = Steps(dve, chain, turn=i, per=U)
                        dve.wait_ge(qk_turned, i * 2 + 2)
                        nc.vector.tensor_scalar(kT, ps[:, 6:8].rearrange("p a n -> p (a n)"), par["gk"], None, ALU.mult).then_inc(kT_ready, 1)

                        def maxes(u):
                            n = (u % NT + 1) * P
                            b = (u % 2) * 2
                            dve.wait_ge(s_done, i * U + u + 1)
                            if u >= 2:
                                dve.wait_ge(p_done, i * U + u - 1)
                            nc.vector.tensor_reduce(nmax[:, u % 2:u % 2 + 1], ps[:, b:b + 2].rearrange("p a n -> p (a n)")[:, 0:n], X, ALU.max, negate=True).then_inc(m_done, 1)

                        def normed(u):
                            head, qt = divmod(u, NT)
                            dve.wait_ge(p_done, i * U + u + 1)
                            r = rsum[:, u % 4:u % 4 + 1]
                            st.link(nc.vector.reciprocal(rinv, r))
                            dve.wait_ge(o_done, i * U + u + 1)
                            nc.vector.tensor_scalar(att[:, qt, head * HD:(head + 1) * HD], ps[:, 6 + u % 2, 0:HD], rinv, None, ALU.mult).then_inc(o_out, 1)
                            dve.wait_ge(o_out, i * U + u + 1)

                        rinv = small[:, 154:155]
                        maxes(0)
                        maxes(1)
                        for u in range(U):
                            dve.wait_ge(t_done, i * U + u + 1)
                            n = min((u % NT + 1) * P, HALF)
                            if u >= 2:
                                dve.wait_ge(o_done, i * U + u - 1)
                            nc.vector.tensor_copy(pT[:, u % 2, 0:n], ps[:, 4, 0:n]).then_inc(pa, 1)
                            if u + 2 < U:
                                maxes(u + 2)
                            if u:
                                normed(u - 1)
                        normed(U - 1)
                        st.end()
                        dve.wait_ge(att_turned, i + 1)
                        nc.vector.tensor_copy(attT[:, bass.ds(i, 1), :].rearrange("p a n -> p (a n)"), ps[:, 4:6].rearrange("p a n -> p (a n)")).then_inc(att_out, 1)
                        dve.wait_ge(att_out, i + 2)

            tmp, at = view(at - NT * P, (2, HALF))
            done, updated = sem("out_product"), sem("x_updated")
            chain = sem("out_chain")
            with nc.Block() as block:
                @block.tensor
                def _(pe):
                    with pe.Fori(0, 2) as h:
                        for t in range(NT):
                            pe.wait_ge(updated, h * NT + NT)
                            for k in range(KD):
                                src = attT[:, k] if k < PAIRS else conv[:, k - PAIRS]
                                last = nc.tensor.matmul(ps[:, t], src[:, t * P:(t + 1) * P], hT[:, k, bass.ds(h * HALF, HALF)], start=(k == 0), stop=(k == KD - 1))
                            last.then_inc(done, 1)

                @block.vector
                def _(dve):
                    dve.sem_inc(updated, NT)
                    with dve.Fori(0, 2) as h:
                        st = Steps(dve, chain, turn=h, per=NT)
                        for t in range(NT):
                            dve.wait_ge(done, h * NT + t + 1)
                            st.link(nc.vector.tensor_tensor(tmp[:, t % 2], ps[:, t], gate[:, 0, bass.ds(h * HALF, HALF)], ALU.mult))
                            xt = x[:, t, bass.ds(h * HALF, HALF)]
                            nc.vector.tensor_tensor(xt, xt, tmp[:, t % 2], ALU.add).then_inc(updated, 1)
                            dve.wait_ge(updated, h * NT + t + NT + 1)
                        st.end()

        def ssm_phase(layer):
            TPC = CHUNK // P
            GT = GW // P
            CTG = GT + 2
            H, DH = SSM_HEADS, SSM_HEAD_DIM
            LC = CHUNK + P
            par = {k: mix1[:, v[0]:v[0] + v[1]] for k, v in MIX1.items()}
            cw = par["conv_w"].rearrange("p (c j) -> p c j", j=SCONV)
            row = {k: rows[:, v[0]:v[0] + v[1]] for k, v in ROWS.items()}
            dt, at = view(0, (NT, H))
            acs, at = view(at, (NT, H))
            eacs, at = view(at, (NT, H))
            dst, at = view(at, (NT, H))
            cdec, at = view(at, (NCH, H))
            base = at
            wdt, at = view(at, (KD, H))
            t0_, at = view(at, (NT, H))
            t1_, at = view(at, (NT, H))
            t2_, at = view(at, (NT, H))
            da, at = view(at, (NT, H))
            nega, at = view(at, (H,))
            arow, at = view(at, (SEQ,))
            wdt_loaded, dt_raw, chain = sem("dt_w_loaded"), sem("dt_product"), sem("dt_chain")
            exp_done, ln_done, a_done = sem("dt_exp"), sem("dt_ln"), sem("a_exp")
            abs_done, u_done2 = sem("dt_abs"), sem("dt_one_plus")
            da_ready, cums, e_done, arow_out = sem("da_ready"), sem("cumsums"), sem("decays"), sem("acs_row_ready")
            cum_out, dec_in = sem("acs_ready"), sem("decay_in_ready")
            arow_stored = sem("acs_rows_stored")
            with nc.Block() as block:
                @block.sync
                def _(sp):
                    sp.dma_start(wdt.rearrange("p k n -> p (k n)"), ins["ssm_dt"]).then_inc(wdt_loaded, 16)
                    sp.wait_ge(arow_out, 1)
                    sp.dma_start(acs_rows[:, :], arow[0:H, :]).then_inc(arow_stored, 16)
                    sp.wait_ge(arow_stored, 16)

                @block.tensor
                def _(pe):
                    pe.wait_ge(wdt_loaded, 16)
                    for t in range(NT):
                        for k in range(KD):
                            last = nc.tensor.matmul(ps[:, 0, t * H:(t + 1) * H], hT[:, k, t * P:(t + 1) * P], wdt[:, k], start=(k == 0), stop=(k == KD - 1))
                    last.then_inc(dt_raw, 1)
                    pe.wait_ge(da_ready, 1)
                    for c in range(NCH):
                        a, b = 2 * c, 2 * c + 1
                        nc.tensor.matmul(ps[:, 1, a * H:(a + 1) * H], const("tri_inc"), da[:, a], start=True, stop=True)
                        nc.tensor.matmul(ps[:, 1, b * H:(b + 1) * H], const("tri_inc"), da[:, b], start=True, stop=False)
                        nc.tensor.matmul(ps[:, 1, b * H:(b + 1) * H], ones, da[:, a], start=False, stop=True)
                        nc.tensor.matmul(ps[:, 2, c * H:(c + 1) * H], ones, da[:, a], start=True, stop=False)
                        nc.tensor.matmul(ps[:, 2, c * H:(c + 1) * H], ones, da[:, b], start=False, stop=True)
                        r = ps[0:H, 3 + c // 2, (c % 2) * CHUNK:(c % 2 + 1) * CHUNK]
                        at_, n_ = CONST["tri_inc"]
                        nc.tensor.matmul(r, da[:, a], cst[:, at_:at_ + 2 * P], start=True, stop=True)
                        last = nc.tensor.matmul(r[:, P:2 * P], da[:, b], const("tri_inc"), start=False, stop=True, skip_group_check=True)
                    last.then_inc(cums, 1)

                @block.scalar
                def _(act):
                    nc.scalar.activation(nega, row["a_log"], ACT.Exp).then_inc(a_done, 1)
                    act.wait_ge(abs_done, 1)
                    f = lambda v: v.rearrange("p t h -> p (t h)")
                    nc.scalar.activation(f(t1_), f(t1_), ACT.Exp, scale=-1.0).then_inc(exp_done, 1)
                    act.wait_ge(u_done2, 1)
                    nc.scalar.activation(f(da), f(t2_), ACT.Ln).then_inc(ln_done, 1)
                    act.wait_ge(dec_in, 1)
                    nc.scalar.activation(f(eacs), f(acs), ACT.Exp)
                    nc.scalar.activation(f(dst), f(dst), ACT.Exp)
                    nc.scalar.activation(f(cdec), f(cdec), ACT.Exp).then_inc(e_done, 1)
                    act.wait_ge(cums, 1)
                    nc.scalar.copy(arow[0:H, :], ps[0:H, 3:5].rearrange("p a n -> p (a n)")).then_inc(arow_out, 1)

                @block.vector
                def _(dve):
                    v = nc.vector
                    st = Steps(dve, chain)
                    dve.wait_ge(dt_raw, 1)
                    st.link(v.tensor_tensor(t0_, ps[:, 0, 0:NT * H].rearrange("p (t h) -> p t h", h=H), bc(row["dt_bias"], 1, NT), ALU.add))
                    st.link(v.tensor_scalar(t1_, t0_, -1.0, None, ALU.mult))
                    v.tensor_tensor(t1_, t0_, t1_, ALU.max).then_inc(abs_done, 1)
                    dve.wait_ge(exp_done, 1)
                    v.tensor_scalar(t2_, t1_, 1.0, None, ALU.add).then_inc(u_done2, 1)
                    dve.wait_ge(u_done2, 1)
                    dve.wait_ge(ln_done, 1)
                    st.link(v.tensor_scalar(t2_, t2_, 1.0, None, ALU.subtract))
                    st.link(v.tensor_scalar(dt, t2_, 0.0, None, ALU.is_equal))
                    st.did(v.tensor_tensor(da, da, dt, ALU.add))
                    st.link(v.tensor_tensor(t2_, t2_, dt, ALU.add))
                    st.link(v.reciprocal(t2_, t2_))
                    st.link(v.tensor_tensor(da, da, t1_, ALU.mult))
                    st.link(v.tensor_tensor(da, da, t2_, ALU.mult))
                    st.link(v.scalar_tensor_tensor(dt, t0_, 0.0, da, ALU.max, ALU.add))
                    dve.wait_ge(a_done, 1)
                    st.link(v.tensor_scalar(nega, nega, -1.0, None, ALU.mult))
                    v.tensor_tensor(da, dt, bc(nega, 1, NT), ALU.mult).then_inc(da_ready, 1)
                    dve.wait_ge(cums, 1)
                    st.link(v.tensor_copy(acs.rearrange("p t h -> p (t h)"), ps[:, 1, 0:NT * H]))
                    st.link(v.tensor_copy(cdec.rearrange("p t h -> p (t h)"), ps[:, 2, 0:NCH * H]))
                    v.tensor_tensor(dst.rearrange("p (c a) h -> p c a h", a=TPC), bc(cdec, 2, TPC), acs.rearrange("p (c a) h -> p c a h", a=TPC), ALU.subtract).then_inc(dec_in, 1)

            HB = 2
            NBAT = HPG // HB
            at = base
            xw, at = view(at, (2, KD * P))
            zw, at = view(at, (KD, GW))
            ow, at = view(at, (GT, D))
            raw, at = view(at, (2, SEQ + SCONV))
            cv, at = view(at, (2, SEQ))
            BT, at = view(at, (SEQ,))
            CTt, at = view(at, (SEQ,))
            xs, at = view(at, (NT, GW))
            Btok, at = view(at, (NT, P))
            rbc, at = view(at, (HPG, CHUNK))
            cbt, at = view(at, (LC,))
            mt, at = view(at, (2, HB, LC))
            xdt, at = view(at, (TPC, GW))
            xdec, at = view(at, (TPC, GW))
            state, at = view(at, (GW,))
            zs, at = view(at, (TPC, GW))
            y, at = view(at, (TPC, GW))
            tq, at = view(at, (GW,))
            gT, at = view(at, (GT, P))
            acg = small[:, 16:16 + NT * HPG].rearrange("p (t h) -> p t h", h=HPG)
            normg = small[:, 96:96 + GT]
            ssq = small[:, 90:92]
            w_xbc = [sem("xbc_w_loaded0"), sem("xbc_w_loaded1")]
            w_z, w_o = sem("z_w_loaded"), sem("out_w_loaded")
            xw_used, z_used, o_used = sem("xbc_w_used"), sem("z_product"), sem("out_product")
            raw_out, zeroed = sem("raw_evacuated"), sem("pads_zeroed")
            convd, cv_ready = sem("convolved"), sem("conv_silu")
            turned, tv, ta = sem("xs_transposed"), sem("xs_by_vector"), sem("xs_by_scalar")
            rb_loaded, acg_ready = sem("acs_broadcast"), sem("acs_group_copied")
            cb_done, cb_out = sem("cb_ready"), sem("cb_masked")
            slot_seen = sem("decay_slot_seen")
            diff, expd, mt_ready = sem("decay_exponent"), sem("decay_exp"), sem("decayed_cb")
            xdt_ready, xdec_ready = sem("xdt_ready"), sem("xdec_ready")
            st_done, st_out = sem("state_product"), sem("state_updated")
            yo_done, yd_done = sem("y_off_ready"), sem("y_diag_ready")
            z_out, y1_, y2_ = sem("z_silu"), sem("y_gated"), sem("y_normed")
            sq_done, rt_done = sem("y_squared"), sem("y_rms")
            g_turned, g_out = sem("y_transposed"), sem("gT_ready")
            o_out = sem("x_updated")
            chain = sem("ssd_chain")
            CPG = NCH * TPC
            with nc.Block() as block:
                @block.sync
                def _(sp):
                    with sp.Fori(0, SSM_G) as g:
                        for c in range(CTG):
                            sp.wait_ge(xw_used, g * CTG + c + 1)
                            sp.dma_start(xw[:, c % 2], ins["ssm_xbc"][bass.ds(g * CTG + c, 1)].rearrange("c p n -> p (c n)")).then_inc(w_xbc[c % 2], 16)
                            if c == 1:
                                sp.wait_ge(z_used, (g + 1) * CPG)
                                sp.dma_start(zw.rearrange("p k n -> p (k n)"), ins["ssm_z"][bass.ds(g, 1)].rearrange("c p n -> p (c n)")).then_inc(w_z, 16)
                            if c == 2:
                                sp.wait_ge(o_used, (g + 1) * 2 * CPG)
                                sp.dma_start(ow.rearrange("p k n -> p (k n)"), ins["ssm_out"][bass.ds(g, 1)].rearrange("c p n -> p (c n)")).then_inc(w_o, 16)
                        for c in range(NCH):
                            sp.wait_ge(diff, (g * NCH + c + 1) * NBAT)
                            sp.dma_start(rbc, acs_rows[bass.ds(g * HPG, HPG), c * CHUNK:(c + 1) * CHUNK].unsqueeze(0).to_broadcast([P, HPG, CHUNK])).then_inc(rb_loaded, 16)

                @block.tensor
                def _(pe):
                    pe.sem_inc(xw_used, 2)
                    pe.sem_inc(z_used, CPG)
                    pe.sem_inc(o_used, 2 * CPG)
                    pe.sem_inc(yd_done, NBAT)
                    with pe.Fori(0, SSM_G) as g:
                        def conv_turn(c):
                            src = cv[:, c % 2] if c < GT else BT
                            pe.wait_ge(cv_ready, g * CTG + c + 1)
                            if c:
                                pe.wait_ge(tv, g * (GT + 1) + c)
                                pe.wait_ge(ta, g * (GT + 1) + c)
                            for t in range(NT):
                                last = nc.tensor.transpose(ps[:, 4 + t // 4, (t % 4) * P:(t % 4 + 1) * P], src[:, t * P:(t + 1) * P], ident)
                            last.then_inc(turned, 1)

                        for c in range(CTG):
                            w = xw[:, c % 2].rearrange("p (k n) -> p k n", n=P)
                            pe.wait_ge(w_xbc[c % 2], g * (CTG // 2 * 16) + 16 * (c // 2 + 1))
                            if c >= 2:
                                pe.wait_ge(raw_out, g * CTG + c - 1)
                            for h in range(2):
                                for k in range(KD):
                                    last = nc.tensor.matmul(ps[:, (c % 2) * 2 + h], w[:, k], hT[:, k, h * HALF:(h + 1) * HALF], start=(k == 0), stop=(k == KD - 1))
                            last.then_inc(xw_used, 1)
                            if 1 <= c <= GT + 1:
                                conv_turn(c - 1)

                        def z_product(c, a):
                            t = c * TPC + a
                            if t == 0:
                                pe.wait_ge(w_z, g * 16 + 16)
                                pe.wait_ge(raw_out, g * CTG + CTG)
                            if t >= TPC:
                                pe.wait_ge(z_out, g * CPG + t - TPC + 1)
                            for k in range(KD):
                                last = nc.tensor.matmul(ps[:, 1 + a], hT[:, k, t * P:(t + 1) * P], zw[:, k], start=(k == 0), stop=(k == KD - 1))
                            last.then_inc(z_used, 1)

                        def cb_product(c):
                            if c == 0:
                                pe.wait_ge(cv_ready, g * CTG + CTG)
                                pe.wait_ge(raw_out, g * CTG + CTG)
                            else:
                                pe.wait_ge(cb_out, g * NCH + c)
                            l0 = c * CHUNK
                            nc.tensor.matmul(ps[:, 0, 0:CHUNK], BT[:, l0:l0 + P], CTt[:, l0:l0 + CHUNK], start=True, stop=True)
                            nc.tensor.matmul(ps[:, 0, CHUNK:LC], BT[:, l0 + P:l0 + CHUNK], CTt[:, l0 + P:l0 + CHUNK], start=True, stop=True).then_inc(cb_done, 1)

                        def out_product(c, a):
                            t = c * TPC + a
                            pe.wait_ge(y2_, g * CPG + t + 1)
                            if t:
                                pe.wait_ge(g_out, g * CPG + t)
                            for k in range(GT):
                                last = nc.tensor.transpose(ps[:, 5, k * P:(k + 1) * P], y[:, a, k * P:(k + 1) * P], ident)
                            last.then_inc(g_turned, 1)
                            pe.wait_ge(g_out, g * CPG + t + 1)
                            if t == 0:
                                pe.wait_ge(w_o, g * 16 + 16)
                            for h in range(2):
                                if t:
                                    pe.wait_ge(o_out, (g * CPG + t) * 2 + h - 1)
                                for k in range(GT):
                                    last = nc.tensor.matmul(ps[:, 6 + h], gT[:, k], ow[:, k, h * HALF:(h + 1) * HALF], start=(k == 0), stop=(k == GT - 1))
                                last.then_inc(o_used, 1)

                        for c in range(NCH):
                            cb_product(c)
                            for a in range(TPC):
                                z_product(c, a)
                            if c:
                                for a in range(TPC):
                                    out_product(c - 1, a)
                            if c:
                                pe.wait_ge(st_out, g * (NCH - 1) + c)
                                for a in range(TPC):
                                    t = c * TPC + a
                                    last = nc.tensor.matmul(ps[:, 3 + a], CTt[:, t * P:(t + 1) * P], state, start=True, stop=True)
                                last.then_inc(yo_done, 1)
                            if c < NCH - 1:
                                pe.wait_ge(xdec_ready, g * (NCH - 1) + c + 1)
                                if c == 0:
                                    pe.wait_ge(tv, (g + 1) * (GT + 1))
                                    pe.wait_ge(ta, (g + 1) * (GT + 1))
                                for a in range(TPC):
                                    last = nc.tensor.matmul(ps[:, 5], Btok[:, c * TPC + a], xdec[:, a], start=(a == 0), stop=(a == TPC - 1))
                                last.then_inc(st_done, 1)
                            pe.wait_ge(xdt_ready, g * NCH + c + 1)
                            if c:
                                pe.wait_ge(o_out, (g * CPG + c * TPC) * 2)
                            for b in range(NBAT):
                                pe.wait_ge(mt_ready, (g * NCH + c) * NBAT + b + 1)
                                for hh in range(HB):
                                    hd = b * HB + hh
                                    cols = slice(hd * DH, (hd + 1) * DH)
                                    m = mt[:, b % 2, hh]
                                    nc.tensor.matmul(ps[:, 6, cols], m[:, 0:P], xdt[:, 0, cols], start=True, stop=True)
                                    nc.tensor.matmul(ps[:, 7, cols], m[:, P:2 * P], xdt[:, 0, cols], start=True, stop=False)
                                    last = nc.tensor.matmul(ps[:, 7, cols], m[:, 2 * P:3 * P], xdt[:, 1, cols], start=False, stop=True)
                                last.then_inc(yd_done, 1)
                        for a in range(TPC):
                            out_product(NCH - 1, a)
                        pe.wait_ge(o_out, (g + 1) * 2 * CPG)

                @block.gpsimd
                def _(pool):
                    pool.sem_inc(diff, NBAT)
                    with pool.Fori(0, SSM_G) as g:
                        nc.gpsimd.tensor_copy(acg, acs[:, :, bass.ds(g * HPG, HPG)])
                        nc.gpsimd.tensor_copy(normg, par["norm"][:, bass.ds(g * GT, GT)]).then_inc(acg_ready, 1)
                        pool.wait_ge(acg_ready, g + 1)
                        for c in range(NCH):
                            pool.wait_ge(rb_loaded, (g * NCH + c) * 16 + 16)
                            for b in range(NBAT):
                                if b >= 2:
                                    pool.wait_ge(yd_done, (g * NCH + c + 1) * NBAT + b - 1)
                                else:
                                    pool.wait_ge(yd_done, (g * NCH + c + 1) * NBAT)
                                pool.sem_inc(slot_seen, 1)
                                for hh in range(HB):
                                    hd = b * HB + hh
                                    nc.gpsimd.tensor_scalar(mt[:, b % 2, hh, 0:CHUNK], rbc[:, hd], acg[:, c * TPC, hd:hd + 1], 0.0, ALU.subtract, ALU.min)
                                    last = nc.gpsimd.tensor_scalar(mt[:, b % 2, hh, CHUNK:LC], rbc[:, hd, P:CHUNK], acg[:, c * TPC + 1, hd:hd + 1], 0.0, ALU.subtract, ALU.min)
                                last.then_inc(diff, 1)
                        pool.wait_ge(o_out, (g + 1) * 2 * CPG)

                @block.scalar
                def _(act):
                    with act.Fori(0, SSM_G) as g:
                        def silu(c):
                            dst = BT if c == GT else CTt if c == GT + 1 else cv[:, c % 2]
                            act.wait_ge(convd, g * CTG + c + 1)
                            nc.scalar.activation(dst, cv[:, c % 2], ACT.Silu).then_inc(cv_ready, 1)

                        def turn_evac(c):
                            act.wait_ge(turned, g * (GT + 1) + c + 1)
                            dst = xs[:, 4:8, c * P:(c + 1) * P] if c < GT else Btok[:, 4:8]
                            nc.scalar.copy(dst, ps[:, 5].rearrange("p (t n) -> p t n", n=P)).then_inc(ta, 1)

                        act.wait_ge(zeroed, 1)
                        for c in range(CTG):
                            act.wait_ge(xw_used, g * CTG + c + 3)
                            if c >= 2:
                                act.wait_ge(convd, g * CTG + c - 1)
                            nc.scalar.copy(raw[:, c % 2, SCONV - 1:SCONV - 1 + SEQ], ps[:, (c % 2) * 2:(c % 2) * 2 + 2].rearrange("p a n -> p (a n)")).then_inc(raw_out, 1)
                            if c >= 1:
                                silu(c - 1)
                            if c >= 2:
                                turn_evac(c - 2)
                        silu(CTG - 1)
                        turn_evac(GT)

                        def tail(c, a):
                            t = c * TPC + a
                            act.wait_ge(y1_, g * CPG + t + 1)
                            nc.scalar.activation(zs[:, a], y[:, a], ACT.Square, accum_out=ssq[:, a:a + 1]).then_inc(sq_done, 1)
                            act.wait_ge(sq_done, g * CPG + t + 1)
                            nc.scalar.activation(ssq[:, a:a + 1], ssq[:, a:a + 1], ACT.Sqrt, bias=eps, scale=1.0 / GW).then_inc(rt_done, 1)

                        def evac_gT(c, a):
                            t = c * TPC + a
                            act.wait_ge(acg_ready, g + 1)
                            act.wait_ge(g_turned, g * CPG + t + 1)
                            if t:
                                act.wait_ge(o_used, ((g + 1) * CPG + t) * 2)
                            for k in range(GT):
                                last = nc.scalar.activation(gT[:, k], ps[:, 5, k * P:(k + 1) * P], ACT.Copy, scale=normg[:, k:k + 1])
                            last.then_inc(g_out, 1)

                        for c in range(NCH):
                            for a in range(TPC):
                                t = c * TPC + a
                                act.wait_ge(z_used, (g + 1) * CPG + t + 1)
                                if t >= TPC:
                                    act.wait_ge(y1_, g * CPG + t - TPC + 1)
                                nc.scalar.activation(zs[:, a], ps[:, 1 + a], ACT.Silu).then_inc(z_out, 1)
                            if c:
                                for a in range(TPC):
                                    evac_gT(c - 1, a)
                            for b in range(NBAT):
                                act.wait_ge(diff, (g * NCH + c + 1) * NBAT + b + 1)
                                nc.scalar.activation(mt[:, b % 2], mt[:, b % 2], ACT.Exp).then_inc(expd, 1)
                            for a in range(TPC):
                                tail(c, a)
                        for a in range(TPC):
                            evac_gT(NCH - 1, a)
                        act.wait_ge(o_out, (g + 1) * 2 * CPG)

                @block.vector
                def _(dve):
                    v = nc.vector
                    nc.vector.memset(raw[:, :, 0:SCONV - 1], 0.0).then_inc(zeroed, 1)
                    dve.wait_ge(zeroed, 1)
                    with dve.Fori(0, SSM_G) as g:
                        st = Steps(dve, chain, turn=g, per=CTG * (SCONV - 1) + (NCH - 2) + TPC * (2 + 4 * (NCH - 1)) + 3 * CPG)

                        def turn_evac(c):
                            dve.wait_ge(turned, g * (GT + 1) + c + 1)
                            dst = xs[:, 0:4, c * P:(c + 1) * P] if c < GT else Btok[:, 0:4]
                            v.tensor_copy(dst, ps[:, 4].rearrange("p (t n) -> p t n", n=P)).then_inc(tv, 1)

                        for c in range(CTG):
                            dve.wait_ge(raw_out, g * CTG + c + 1)
                            if c >= 2:
                                dve.wait_ge(cv_ready, g * CTG + c - 1)
                                dve.wait_ge(turned, g * (GT + 1) + c - 1)
                            yv = cv[:, c % 2]
                            for j in range(SCONV):
                                u = raw[:, c % 2, j:j + SEQ]
                                w = cw[:, bass.ds(g * CTG + c, 1), j]
                                if j == 0:
                                    st.link(v.tensor_scalar(yv, u, w, par["conv_b"][:, bass.ds(g * CTG + c, 1)], ALU.mult, ALU.add))
                                elif j < SCONV - 1:
                                    st.link(v.scalar_tensor_tensor(yv, u, w, yv, ALU.mult, ALU.add))
                                else:
                                    v.scalar_tensor_tensor(yv, u, w, yv, ALU.mult, ALU.add).then_inc(convd, 1)
                            if c >= 2:
                                turn_evac(c - 2)
                        turn_evac(GT)
                        dve.wait_ge(tv, (g + 1) * (GT + 1))
                        dve.wait_ge(ta, (g + 1) * (GT + 1))

                        def heads(ap):
                            return ap.rearrange("p (h d) -> p h d", d=DH)

                        def out_add(c, a):
                            t = c * TPC + a
                            for h in range(2):
                                dve.wait_ge(o_used, ((g + 1) * CPG + t) * 2 + h + 1)
                                st.link(v.tensor_tensor(tq, ps[:, 6 + h], gate[:, 0, h * HALF:(h + 1) * HALF], ALU.mult))
                                xt = x[:, t, h * HALF:(h + 1) * HALF]
                                v.tensor_tensor(xt, xt, tq, ALU.add).then_inc(o_out, 1)
                                dve.wait_ge(o_out, (g * CPG + t) * 2 + h + 1)

                        for c in range(NCH):
                            hs = bass.ds(g * HPG, HPG)
                            t0, t1 = c * TPC, (c + 1) * TPC
                            for a in range(TPC):
                                last = v.tensor_tensor(heads(xdt[:, a]), heads(xs[:, t0 + a]), dt[:, t0 + a, hs].unsqueeze(2).to_broadcast([P, HPG, DH]), ALU.mult)
                            last.then_inc(xdt_ready, 1)
                            dve.wait_ge(xdt_ready, g * NCH + c + 1)
                            if c < NCH - 1:
                                for a in range(TPC):
                                    last = v.tensor_tensor(heads(xdec[:, a]), heads(xdt[:, a]), dst[:, t0 + a, hs].unsqueeze(2).to_broadcast([P, HPG, DH]), ALU.mult)
                                last.then_inc(xdec_ready, 1)
                            dve.wait_ge(cb_done, g * NCH + c + 1)
                            at_, n_ = CONST["tri_inc"]
                            v.tensor_tensor(cbt, ps[:, 0, 0:LC], cst[:, at_:at_ + LC], ALU.mult).then_inc(cb_out, 1)
                            dve.wait_ge(cb_out, g * NCH + c + 1)
                            if c:
                                for a in range(TPC):
                                    out_add(c - 1, a)
                            for b in range(NBAT):
                                dve.wait_ge(expd, (g * NCH + c) * NBAT + b + 1)
                                v.tensor_tensor(mt[:, b % 2], mt[:, b % 2], bc(cbt, 1, HB), ALU.mult).then_inc(mt_ready, 1)
                            if c:
                                dve.wait_ge(yo_done, g * (NCH - 1) + c)
                                for a in range(TPC):
                                    last = st.did(v.tensor_tensor(heads(y[:, a]), heads(ps[:, 3 + a]), eacs[:, t0 + a, hs].unsqueeze(2).to_broadcast([P, HPG, DH]), ALU.mult))
                            if c < NCH - 1:
                                dve.wait_ge(st_done, g * (NCH - 1) + c + 1)
                                if c == 0:
                                    v.tensor_copy(state, ps[:, 5]).then_inc(st_out, 1)
                                else:
                                    st.link(v.tensor_tensor(heads(state), heads(state), cdec[:, c, hs].unsqueeze(2).to_broadcast([P, HPG, DH]), ALU.mult))
                                    v.tensor_tensor(state, state, ps[:, 5], ALU.add).then_inc(st_out, 1)
                                dve.wait_ge(st_out, g * (NCH - 1) + c + 1)
                            dve.wait_ge(yd_done, (g * NCH + c + 2) * NBAT)
                            for a in range(TPC):
                                t = t0 + a
                                st.link(v.tensor_tensor(heads(tq), heads(xs[:, t]), bc(row["ssm_d"][:, hs], 2, DH), ALU.mult))
                                if c:
                                    st.link(v.tensor_tensor(y[:, a], y[:, a], ps[:, 6 + a], ALU.add))
                                    st.link(v.tensor_tensor(y[:, a], y[:, a], tq, ALU.add))
                                else:
                                    st.link(v.tensor_tensor(y[:, a], tq, ps[:, 6 + a], ALU.add))
                                dve.wait_ge(z_out, g * CPG + t + 1)
                                v.tensor_tensor(y[:, a], y[:, a], zs[:, a], ALU.mult).then_inc(y1_, 1)
                            for a in range(TPC):
                                t = t0 + a
                                dve.wait_ge(rt_done, g * CPG + t + 1)
                                st.link(v.reciprocal(ssq[:, a:a + 1], ssq[:, a:a + 1]))
                                v.tensor_scalar(y[:, a], y[:, a], ssq[:, a:a + 1], None, ALU.mult).then_inc(y2_, 1)
                        for a in range(TPC):
                            out_add(NCH - 1, a)
                        st.end()


        for layer in range(DEPTH):
            if f"ada{layer}" in stages:
                ada_phase(layer)
            if f"mix{layer}" in stages:
                norm_phase(layer, 0, False)
                (hybrid_phase if layer % 2 == 0 else ssm_phase)(layer)
                clear_sems()
            if f"moe{layer}" in stages:
                norm_phase(layer, 1, True)
                moe_phase(layer, layer == DEPTH - 1)
                if layer < DEPTH - 1:
                    clear_sems()
        if "dump" in stages:
            o_stored = sem("dumped")
            with nc.Block() as block:
                @block.sync
                def _(sp):
                    sp.dma_start(out[0].rearrange("(t p) d -> p t d", p=P), x[:, :, :]).then_inc(o_stored, 16)
                    sp.wait_ge(o_stored, 16)


STAGES = ("ada0", "mix0", "moe0", "ada1", "mix1", "moe1")


def kernel(**inputs):
    import numpy as np
    import concourse.bacc as bacc
    from concourse import mybir as mb
    from concourse.bass_utils import run_bass_kernel_spmd as run

    a = {k: np.asarray(v) for k, v in inputs.items()}
    f = np.float32
    p = np.arange(P)
    parts = {
        "ident": np.eye(P, dtype=f),
        "tri_strict": (p[:, None] < p[None]).astype(f),
        "tri_inc": (p[:, None] <= p[None]).astype(f),
        "ones": np.ones((P, P), f),
        "tri_inc2": (p[:, None] <= p[None]).astype(f),
        "maskneg": np.where(p[:, None] >= p[None], 0.0, NEG).astype(f),
        "before4": np.broadcast_to((np.arange(J)[None] < np.arange(J)[:, None]).astype(f).reshape(1, -1), (P, J * J)),
        "group_key": np.broadcast_to((G - np.arange(G)).astype(f)[None], (P, G)),
        "step128": np.broadcast_to((P * np.arange(NT)).astype(f)[None], (P, NT)),
        "before16": np.broadcast_to((np.arange(E)[None] < np.arange(E)[:, None]).astype(f).reshape(1, -1), (P, E * E)),
        "chunk_end": np.broadcast_to((P * (1 + np.arange(SLOTS))).astype(f)[None], (P, SLOTS)),
        "iota_chunk": np.broadcast_to(np.arange(SLOTS).astype(f)[None], (P, SLOTS)),
        "iota128": np.broadcast_to(p.astype(f)[None], (P, P)),
        "token_id": (p[:, None] + P * np.arange(NT)[None]).astype(f),
        "eps": np.full((P, 1), EPS, f),
    }
    arrays = {}
    arrays["consts"] = np.concatenate([parts[n] for n in CONST], axis=1)

    def cols(v):
        return v.reshape(-1, P).T

    arrays["pcols"] = np.stack([np.concatenate([cols(a["c"][0]), cols(a["ada_b"][l]), cols(a["norm_mix"][l]), cols(a["norm_ffn"][l])], axis=1)
                                for l in range(DEPTH)], axis=1)
    arrays["mix0"] = np.concatenate([np.tile(a["hy_q_norm"][0], 2)[:, None], np.tile(a["hy_k_norm"][0], 2)[:, None],
                                     cols(a["hy_dw_b"][0]), cols(a["hy_ln_g"][0]), cols(a["hy_ln_b"][0]),
                                     a["hy_dw_w"][0].reshape(CONV_W, CT, P).transpose(2, 1, 0).reshape(P, -1)], axis=1)
    order = [i for g in range(SSM_G) for i in [*range(g * GW // P, (g + 1) * GW // P), SSM_INNER // P + g, SSM_INNER // P + SSM_G + g]]
    arrays["mix1"] = np.concatenate([cols(a["ssm_conv_b"][0])[:, order], cols(a["ssm_norm"][0]),
                                     a["ssm_conv_w"][0].reshape(SCONV, XBC_T, P).transpose(2, 1, 0)[:, order].reshape(P, -1)], axis=1)
    arrays["rows"] = np.broadcast_to(np.concatenate([a["router_bias"], a["ssm_dt_bias"][0], a["ssm_a_log"][0], a["ssm_d"][0]])[None], (P, NROWS))
    ab = a["ada_b"].reshape(DEPTH, N_MOD, D)[:, [2, 5]]
    arrays["gate_bias"] = np.broadcast_to(ab[:, None], (DEPTH, P, 2, D))
    arrays["x"] = a["x"][0]
    arrays["router_w"] = a["router_w"]

    def tiled(w, n):
        k, m = w.shape
        return w.reshape(k // P, P, m // n, n).transpose(2, 1, 0, 3).reshape(m // n, P, -1)

    arrays["ada_w"] = np.stack([tiled(a["ada_w"][l], D) for l in range(DEPTH)])
    for name, key in (("exp_g", "exp_w_gate"), ("exp_u", "exp_w_up"), ("exp_d", "exp_w_down")):
        w = a[key]
        arrays[name] = w.reshape(DEPTH, E, -1, P, w.shape[-1]).transpose(0, 1, 3, 2, 4).reshape(DEPTH, E, P, -1)
    w = a["hy_w_in"][0]
    u = w[:, 3 * ATT_W:].reshape(D, 2, CT, P).transpose(0, 2, 1, 3).reshape(D, -1)
    arrays["hy_in"] = tiled(np.concatenate([u, w[:, :3 * ATT_W]], axis=1), 2 * P)
    arrays["hy_out"] = tiled(a["hy_w_out"][0], D)[0]
    w = a["ssm_w_in"][0]
    arrays["ssm_z"] = tiled(w[:, :SSM_INNER], GW)
    arrays["ssm_xbc"] = tiled(w[:, SSM_INNER:SSM_INNER + XBC_T * P], P)[order]
    arrays["ssm_dt"] = tiled(w[:, SSM_INNER + XBC_T * P:], SSM_HEADS)[0]
    arrays["ssm_out"] = a["ssm_w_out"][0].reshape(SSM_G, GW // P, P, D).transpose(0, 2, 1, 3).reshape(SSM_G, P, -1)
    nc = bacc.Bacc("TRN2", target_bir_lowering=False, num_devices=1)
    arrays = {f"in_{k}": np.ascontiguousarray(v) for k, v in arrays.items()}
    ins = {k[3:]: nc.dram_tensor(k, v.shape, mb.dt.from_np(v.dtype), kind="ExternalInput").ap() for k, v in arrays.items()}
    out = nc.dram_tensor("out_0", (1, SEQ, D), mb.dt.float32, kind="ExternalOutput").ap()
    build(nc, ins, out, STAGES)
    return run(nc, [arrays], core_ids=[0]).results[0]["out_0"]
```

```python
import concourse.bass as bass
from concourse import mybir
from contextlib import ExitStack

P = 128
SEQ = 1024
D = 1024
DEPTH = 2
NT = SEQ // P
KD = D // P
HALF = 512
N_MOD = 6
EPS = 1e-6
HEADS = 8
HD = 64
ATT_W = HEADS * HD
PAIRS = ATT_W // P
CONV_CH = D // 2
CT = CONV_CH // P
CONV_W = 31
NEG = -1e30
SSM_INNER = 2 * D
SSM_HEADS = 32
SSM_HEAD_DIM = SSM_INNER // SSM_HEADS
SSM_G = 4
HPG = SSM_HEADS // SSM_G
GW = SSM_INNER // SSM_G
NST = 128
SCONV = 4
CHUNK = 256
NCH = SEQ // CHUNK
E = 16
G = 4
J = E // G
FF = 512
FT = FF // P
TOPK = 2
SLOTS = (SEQ * TOPK) // P + E

CONST = {}
_at = 0
for _name, _n in (("ident", P), ("tri_strict", P), ("tri_inc", P), ("ones", P), ("tri_inc2", P), ("maskneg", P),
                  ("before4", J * J), ("group_key", G), ("step128", NT), ("before16", E * E),
                  ("chunk_end", SLOTS), ("iota_chunk", SLOTS), ("iota128", P), ("token_id", NT),
                  ("eps", 1)):
    CONST[_name] = (_at, _n)
    _at += _n
NCONST = _at
PCOL = {}
_at = 0
for _name, _n in (("c", KD), ("ada_b", N_MOD * KD), ("norm0", KD), ("norm1", KD)):
    PCOL[_name] = (_at, _n)
    _at += _n
NPCOL = _at
MIX0 = {"gq": (0, 1), "gk": (1, 1), "dw_b": (2, CT), "ln_g": (2 + CT, CT), "ln_b": (2 + 2 * CT, CT),
        "dw_w": (2 + 3 * CT, CT * CONV_W)}
NMIX0 = 2 + 3 * CT + CT * CONV_W
XBC_T = (SSM_INNER + 2 * SSM_G * NST) // P
MIX1 = {"conv_b": (0, XBC_T), "norm": (XBC_T, SSM_INNER // P),
        "conv_w": (XBC_T + SSM_INNER // P, XBC_T * SCONV)}
NMIX1 = XBC_T + SSM_INNER // P + XBC_T * SCONV
ROWS = {"rbias": (0, E), "dt_bias": (E, SSM_HEADS), "a_log": (E + SSM_HEADS, SSM_HEADS),
        "ssm_d": (E + 2 * SSM_HEADS, SSM_HEADS)}
NROWS = E + 3 * SSM_HEADS


def bc(ap, axis, n):
    ap = ap.unsqueeze(axis)
    shape = list(ap.shape)
    shape[axis] = n
    return ap.to_broadcast(shape)


class Steps:

    def __init__(self, eng, sem, base=0, turn=None, per=0):
        self.eng, self.sem, self.n, self.base, self.turn, self.per = eng, sem, 0, base, turn, per

    def did(self, ins):
        ins.then_inc(self.sem, 1)
        self.n += 1
        return ins

    def wait(self):
        at = self.base + self.n
        self.eng.wait_ge(self.sem, at if self.turn is None else self.turn * self.per + at)

    def link(self, ins):
        self.did(ins)
        self.wait()

    def end(self):
        assert self.turn is None or self.n == self.per, (self.n, self.per)


def build(nc, ins, out, stages):
    f32 = mybir.dt.float32
    f32r = mybir.dt.float32r
    i32 = mybir.dt.int32
    u32 = mybir.dt.uint32
    ALU = mybir.AluOpType
    ACT = mybir.ActivationFunctionType
    X = mybir.AxisListType.X
    ctx = ExitStack()
    uid = [0]
    live = []

    def sb(name, shape, dt=f32):
        return ctx.enter_context(nc.sbuf_tensor(name, shape, dt))

    def sem(name):
        uid[0] += 1
        live.append(nc.alloc_semaphore(name=f"{name}_{uid[0]}"))
        return live[-1]

    def clear_sems():
        nc.clear_and_free_semaphores(live[:])
        live.clear()
        nc.all_engine_barrier()

    with ctx:
        ctx.enter_context(nc.allow_non_contiguous_dma(reason="parameter columns"))
        x = sb("x", [P, NT, D])
        cst = sb("cst", [P, NCONST])
        pcol = sb("pcol", [P, DEPTH, NPCOL])
        mix0 = sb("mix0", [P, NMIX0])
        mix1 = sb("mix1", [P, NMIX1])
        rows = sb("rows", [P, NROWS])
        gate = sb("gate", [P, 2, D])
        modc = sb("modc", [P, DEPTH, 2, 2, KD])
        small = sb("small", [P, 256])
        WORK, HTW = 32640, KD * SEQ
        base_ = -(-nc.sbuf_base // 32) * 32
        work = sb("work", [P, WORK + HTW])
        hT = work[:, WORK:WORK + HTW].rearrange("p (k n) -> p k n", n=SEQ)
        ps = ctx.enter_context(nc.psum_tensor("ps", [P, 8, HALF], f32))
        hrows = nc.dram_tensor("hrows", [SEQ, D], f32, kind="Internal").ap()
        yrows = nc.dram_tensor("yrows", [(SLOTS + NT) * P, D], f32, kind="Internal").ap()
        y_filled = nc.alloc_semaphore(name="y_rows_filled")
        acs_rows = nc.dram_tensor("acs_rows", [SSM_HEADS, SEQ], f32, kind="Internal").ap()

        def const(name):
            at, n = CONST[name]
            return cst[:, at:at + n]

        def place(name, at, shape, dtype):
            n = 1
            for s in shape:
                n *= s
            assert at + n <= WORK + HTW, (at, n)
            uid[0] += 1
            t = nc.alloc_sbuf_tensor_at(f"{name}_{uid[0]}", [P, *shape], dtype, offset=base_ + 4 * at)
            return t[(slice(None),) * (1 + len(shape))], at + n

        def view(at, shape, limit=WORK):
            n = 1
            for s in shape:
                n *= s
            assert at + n <= limit, (at, n)
            v = work[:, at:at + n]
            if len(shape) == 2:
                v = v.rearrange("p (a b) -> p a b", b=shape[1])
            elif len(shape) == 3:
                v = v.rearrange("p (a b c) -> p a b c", b=shape[1], c=shape[2])
            return v, at + n

        ident, ones = const("ident"), const("ones")
        eps = const("eps")

        with nc.Block() as block:
            s_in = sem("inputs_loaded")
            s_cond = sem("cond_ready")
            s_x = sem("x_loaded")

            @block.sync
            def _(sp):
                sp.dma_start(cst[:, :], ins["consts"]).then_inc(s_in, 16)
                sp.dma_start(pcol[:, :, :], ins["pcols"]).then_inc(s_in, 16)
                sp.dma_start(mix0[:, :], ins["mix0"]).then_inc(s_in, 16)
                sp.dma_start(mix1[:, :], ins["mix1"]).then_inc(s_in, 16)
                sp.dma_start(rows[:, :], ins["rows"]).then_inc(s_in, 16)
                sp.wait_ge(s_in, 80)

            @block.scalar
            def _(act):
                act.wait_ge(s_in, 80)
                nc.scalar.activation(pcol[:, 0, 0:KD], pcol[:, 0, 0:KD], ACT.Silu).then_inc(s_cond, 1)

        def ada_phase(layer):
            wv, at = view(0, (3, KD, D))
            acc = hT[:, 0:3, :]
            w_src = ins["ada_w"][layer].rearrange("c p (k n) -> c p k n", n=D)
            loaded = [sem(f"ada_w_loaded{q}") for q in range(3)]
            bias_loaded = sem("gate_bias_loaded")
            acc_ready = sem("ada_acc_ready")
            summed = sem("ada_summed")
            chain = sem("ada_chain")
            with nc.Block() as block:
                @block.sync
                def _(sp):
                    sp.dma_start(gate[:, :, :], ins["gate_bias"][layer]).then_inc(bias_loaded, 16)
                    with sp.Fori(0, 2) as i:
                        for q in range(3):
                            sp.wait_ge(acc_ready, i * 3 + q + 1)
                            sp.dma_start(wv[:, q], w_src[bass.ds(i * 3 + q, 1)].rearrange("c p k n -> p (c k) n")).then_inc(loaded[q], 16)
                    if layer == 0:
                        sp.dma_start(x[:, :, :], ins["x"].rearrange("(t p) d -> p t d", p=P)).then_inc(s_x, 16)
                        sp.wait_ge(s_x, 16)

                @block.vector
                def _(dve):
                    dve.sem_inc(acc_ready, 3)
                    with dve.Fori(0, 2) as i:
                        st = Steps(dve, chain, turn=i, per=3 * (KD - 1))
                        for q in range(3):
                            dve.wait_ge(loaded[q], i * 16 + 16)
                            dve.wait_ge(summed, i * 3 + 3)
                            for k in range(KD):
                                ck = pcol[:, 0, k:k + 1]
                                if k == 0:
                                    op = nc.vector.tensor_scalar(acc[:, q], wv[:, q, k], ck, None, ALU.mult)
                                else:
                                    st.wait()
                                    op = nc.vector.scalar_tensor_tensor(acc[:, q], wv[:, q, k], ck, acc[:, q], ALU.mult, ALU.add)
                                if k < KD - 1:
                                    st.did(op)
                                else:
                                    op.then_inc(acc_ready, 1)
                        st.end()
                    dve.wait_ge(bias_loaded, 16)
                    dve.wait_ge(summed, 9)
                    ab = pcol[:, layer, PCOL["ada_b"][0]:PCOL["ada_b"][0] + N_MOD * KD].rearrange("p (h q k) -> p h q k", h=2, q=3)
                    sums = ps[:, 0, 0:2 * 2 * KD].rearrange("p (h q k) -> p h q k", h=2, q=2)
                    st = Steps(dve, chain, base=2 * 3 * (KD - 1))
                    st.did(nc.vector.tensor_tensor(modc[:, layer], sums, ab[:, :, 0:2], ALU.add))
                    nc.vector.tensor_tensor(gate[:, :, :], ps[:, 1:5, :].rearrange("p (h a) n -> p h (a n)", h=2), gate[:, :, :], ALU.add)
                    st.wait()
                    nrm = pcol[:, layer, PCOL["norm0"][0]:PCOL["norm0"][0] + 2 * KD].rearrange("p (h k) -> p h k", h=2)
                    for h in range(2):
                        nc.vector.scalar_tensor_tensor(modc[:, layer, h, 1], modc[:, layer, h, 1], 1.0, nrm[:, h], ALU.add, ALU.mult)

                @block.tensor
                def _(pe):
                    pe.sem_inc(summed, 3)
                    with pe.Fori(0, 2) as i:
                        for q in range(3):
                            pe.wait_ge(acc_ready, i * 3 + q + 4)
                            if q == 2:
                                for h in range(2):
                                    last = nc.tensor.matmul(ps[:, bass.ds(i * 2 + 1 + h, 1), :].rearrange("p a n -> p (a n)"), ones, acc[:, q, h * HALF:(h + 1) * HALF], start=True, stop=True)
                            else:
                                for k in range(KD):
                                    last = nc.tensor.matmul(ps[:, 0, bass.ds((i * 2 + q) * KD + k, 1)], acc[:, q, k * P:(k + 1) * P], ones[:, 0:1], start=True, stop=True)
                            last.then_inc(summed, 1)

        def norm_phase(layer, sub, rows_out):
            xn, at = view(0, (4, D))
            junk, at = view(at, (D,))
            squares = sem("squares_summed")
            rms = sem("rms_ready")
            rstd_ready = sem("rstd_ready")
            xn_ready = sem("xn_ready")
            turned = sem("transposed")
            by_act = sem("evacuated_by_scalar")
            by_dve = sem("evacuated_by_vector")
            stored = sem("rows_stored")
            ss, rstd = small[:, 0:NT], small[:, NT:2 * NT]
            shift, scale = modc[:, layer, sub, 0], modc[:, layer, sub, 1]
            with nc.Block() as block:
                @block.scalar
                def _(act):
                    act.sem_inc(by_act, 2)
                    act.sem_inc(squares, 1)
                    with act.Fori(0, NT) as t:
                        act.wait_ge(squares, t + 1)
                        nc.scalar.activation(junk, x[:, bass.ds(t, 1), :].rearrange("p a d -> p (a d)"), ACT.Square, accum_out=ss[:, bass.ds(t, 1)]).then_inc(squares, 1)
                    act.wait_ge(squares, NT + 1)
                    nc.scalar.activation(rstd, ss, ACT.Sqrt, bias=eps, scale=1.0 / D).then_inc(rms, 1)
                    with act.Fori(0, 2) as h:
                        for d in range(0, KD, 2):
                            act.wait_ge(turned, h * KD + d + KD + 1)
                            nc.scalar.activation(hT[:, d, bass.ds(h * HALF, HALF)], ps[:, d % 4], ACT.Identity, bias=shift[:, d:d + 1], scale=scale[:, d:d + 1]).then_inc(by_act, 1)

                @block.vector
                def _(dve):
                    dve.sem_inc(by_dve, 2)
                    dve.wait_ge(rms, 1)
                    nc.vector.reciprocal(rstd, rstd).then_inc(rstd_ready, 1)
                    dve.wait_ge(rstd_ready, 1)
                    with dve.Fori(0, 2) as h:
                        dve.wait_ge(turned, h * KD + KD)
                        if rows_out:
                            dve.wait_ge(stored, h * 16 + 16)
                        for u in range(4):
                            nc.vector.tensor_scalar(xn[:, u], x[:, bass.ds(h * 4 + u, 1), :].rearrange("p a d -> p (a d)"), rstd[:, bass.ds(h * 4 + u, 1)], None, ALU.mult).then_inc(xn_ready, 1)
                        for d in range(1, KD, 2):
                            dve.wait_ge(turned, h * KD + d + KD + 1)
                            nc.vector.tensor_scalar(hT[:, d, bass.ds(h * HALF, HALF)], ps[:, d % 4], scale[:, d:d + 1], shift[:, d:d + 1], ALU.mult, ALU.add).then_inc(by_dve, 1)

                @block.tensor
                def _(pe):
                    pe.sem_inc(turned, KD)
                    with pe.Fori(0, 2) as h:
                        pe.wait_ge(xn_ready, h * 4 + 4)
                        for d in range(KD):
                            pe.wait_ge(by_dve if d % 2 else by_act, h * 4 + d // 2 + 1)
                            for u in range(4):
                                last = nc.tensor.transpose(ps[:, d % 4, u * P:(u + 1) * P], xn[:, u, d * P:(d + 1) * P], ident)
                            last.then_inc(turned, 1)

                if layer == 0 and sub == 0:
                    @block.gpsimd
                    def _(pool):
                        for c in range(SEQ * TOPK // P, SLOTS, NT):
                            pool.dma_start(yrows[c * P:(c + NT) * P, :], ins["x"]).then_inc(y_filled, 16)

                if rows_out:
                    @block.sync
                    def _(sp):
                        sp.sem_inc(stored, 16)
                        with sp.Fori(0, 2) as h:
                            sp.wait_ge(xn_ready, h * 4 + 4)
                            sp.dma_start(hrows[bass.ds(h * HALF, HALF), :].rearrange("(u p) d -> p u d", p=P), xn).then_inc(stored, 16)
                        sp.wait_ge(stored, 48)

        def moe_phase(layer, last_layer):
            sub = 1
            rw, at = view(0, (KD, E))
            score, at = view(at, (NT, E))
            aff, at = view(at, (NT, E))
            cmpa, at = view(at, (NT * G, J, J))
            cmpb, at = view(at, (NT * G, J, J))
            rank, at = view(at, (NT * G, J))
            sel, at = view(at, (NT * G, J))
            gs, at = view(at, (NT, G))
            gsel, at = view(at, (NT, G))
            gmax, at = view(at, (NT,))
            oh, at = view(at, (2, NT, E))
            both, at = view(at, (NT, E))
            off, at = view(at, (NT + 1, E))
            pos, at = view(at, (NT, E))
            nch_c, at = view(at, (E, NT))
            nch, at = view(at, (E,))
            st16, at = view(at, (E, E))
            first, at = view(at, (E,))
            prod, at = view(at, (2, NT, E))
            dest, at = view(at, (2 * NT,))
            ge, at = view(at, (2 * NT, SLOTS))
            hi, at = view(at, (2 * NT,))
            lo, at = view(at, (2 * NT,))
            tv, at = view(at, (2 * NT, SLOTS))
            oh_lo, at = view(at, (2 * NT, P))
            wsel = small[:, 16:32]
            dest_i = small[:, 32:48].bitcast(u32)
            slot_i = small[:, 48:48 + SLOTS + NT + 1].bitcast(u32)
            nch_i = small[:, 96:96 + E].bitcast(i32)
            first_i = small[:, 96 + E:96 + 2 * E].bitcast(i32)
            wsum = small[:, 130:138]
            rw_loaded = sem("router_w_loaded")
            logits = sem("router_logits")
            affs = sem("affinities")
            routed = sem("routed")
            counted = sem("counted")
            placed = sem("slots_placed")
            tabled = sem("slot_table")
            chain = sem("route_chain")
            with nc.Block() as block:
                @block.sync
                def _(sp):
                    sp.dma_start(rw, ins["router_w"].rearrange("(k p) e -> p k e", p=P)).then_inc(rw_loaded, 16)

                @block.tensor
                def _(pe):
                    pe.wait_ge(rw_loaded, 16)
                    for t in range(NT):
                        for k in range(KD):
                            last = nc.tensor.matmul(ps[:, 0, t * E:(t + 1) * E], hT[:, k, t * P:(t + 1) * P], rw[:, k], start=(k == 0), stop=(k == KD - 1))
                    last.then_inc(logits, 1)
                    pe.wait_ge(routed, 1)
                    bf = both.rearrange("p t e -> p (t e)")
                    nc.tensor.matmul(ps[:, 1, 0:P], const("tri_strict"), bf, start=True, stop=True)
                    nc.tensor.matmul(ps[:, 2, 0:P], ones, bf, start=True, stop=True).then_inc(counted, 1)
                    pe.wait_ge(placed, 1)
                    for n in range(2 * NT):
                        last = nc.tensor.matmul(ps[:, 3, 0:SLOTS], oh_lo[:, n], tv[:, n], start=(n == 0), stop=(n == 2 * NT - 1))
                    last.then_inc(tabled, 1)

                @block.scalar
                def _(act):
                    act.wait_ge(logits, 1)
                    nc.scalar.activation(aff.rearrange("p t e -> p (t e)"), ps[:, 0, 0:NT * E], ACT.Sigmoid).then_inc(affs, 1)

                @block.vector
                def _(dve):
                    v = nc.vector
                    st = Steps(dve, chain)
                    dve.wait_ge(affs, 1)
                    st.link(v.tensor_tensor(score, aff, bc(rows[:, 0:E], 1, NT), ALU.add))
                    sg = score.rearrange("p t (g j) -> p (t g) j", g=G)
                    st.did(v.tensor_tensor(cmpa, bc(sg, 2, J), bc(sg, 3, J), ALU.is_gt))
                    st.link(v.tensor_tensor(cmpb, bc(sg, 2, J), bc(sg, 3, J), ALU.is_equal))
                    st.link(v.tensor_tensor(cmpb, cmpb, bc(const("before4").rearrange("p (a b) -> p a b", b=J), 1, NT * G), ALU.mult))
                    st.link(v.tensor_tensor(cmpa, cmpa, cmpb, ALU.add))
                    st.link(v.tensor_reduce(rank, cmpa, X, ALU.add))
                    st.link(v.scalar_tensor_tensor(sel, rank, float(TOPK), sg, ALU.is_lt, ALU.mult))
                    st.link(v.tensor_reduce(gs, sel.rearrange("p (t g) j -> p t g j", g=G), X, ALU.add))
                    st.link(v.tensor_reduce(gmax, gs, X, ALU.max))
                    st.link(v.tensor_tensor(gsel, gs, bc(gmax, 2, G), ALU.is_equal))
                    gk = bc(const("group_key"), 1, NT)
                    st.link(v.tensor_tensor(gsel, gsel, gk, ALU.mult))
                    st.link(v.tensor_reduce(gmax, gsel, X, ALU.max))
                    st.link(v.tensor_tensor(gsel, gk, bc(gmax, 2, G), ALU.is_equal))
                    gflat = bc(gsel.rearrange("p t g -> p (t g)"), 2, J)
                    for k in range(2):
                        st.did(v.scalar_tensor_tensor(oh[:, k].rearrange("p t (g j) -> p (t g) j", g=G), rank, float(k), gflat, ALU.is_equal, ALU.mult))
                    st.wait()
                    v.tensor_tensor(both, oh[:, 0], oh[:, 1], ALU.add).then_inc(routed, 1)
                    st.link(v.tensor_tensor(prod, oh, bc(aff, 1, 2), ALU.mult))
                    w2 = wsel.rearrange("p (k t) -> p k t", k=2)
                    st.link(v.tensor_reduce(w2, prod, X, ALU.add))
                    st.link(v.tensor_tensor(wsum, w2[:, 0], w2[:, 1], ALU.add))
                    st.link(v.reciprocal(wsum, wsum))
                    st.link(v.tensor_tensor(w2, w2, bc(wsum, 1, 2), ALU.mult))
                    dve.wait_ge(counted, 1)
                    tot = ps[:, 2, 0:P].rearrange("p (t e) -> p t e", e=E)
                    st.link(v.memset(off[:, 0], 0.0))
                    for t in range(NT):
                        st.link(v.tensor_tensor(off[:, t + 1], tot[:, t], off[:, t], ALU.add))
                    st.link(v.tensor_tensor(nch_c, bc(off[:, NT], 2, NT), bc(const("step128"), 1, E), ALU.is_gt))
                    st.link(v.tensor_reduce(nch, nch_c, X, ALU.add))
                    st.link(v.tensor_scalar(nch, nch, 1.0, None, ALU.max))
                    st.link(v.tensor_tensor(st16, const("before16").rearrange("p (a b) -> p a b", b=E), bc(nch, 1, E), ALU.mult))
                    st.link(v.tensor_reduce(first, st16, X, ALU.add))
                    st.link(v.tensor_tensor(pos, ps[:, 1, 0:P].rearrange("p (t e) -> p t e", e=E), off[:, 0:NT], ALU.add))
                    st.link(v.scalar_tensor_tensor(pos, bc(first, 1, NT), float(P), pos, ALU.mult, ALU.add))
                    st.link(v.tensor_tensor(prod, oh, bc(pos, 1, 2), ALU.mult))
                    st.link(v.tensor_reduce(dest.rearrange("p (k t) -> p k t", k=2), prod, X, ALU.add))
                    st.did(v.tensor_copy(dest_i, dest))
                    st.link(v.tensor_tensor(ge, bc(dest, 2, SLOTS), bc(const("chunk_end"), 1, 2 * NT), ALU.is_ge))
                    st.link(v.tensor_reduce(hi, ge, X, ALU.add))
                    st.link(v.scalar_tensor_tensor(lo, hi, -float(P), dest, ALU.mult, ALU.add))
                    st.did(v.tensor_tensor(tv, bc(hi, 2, SLOTS), bc(const("iota_chunk"), 1, 2 * NT), ALU.is_equal))
                    st.link(v.tensor_tensor(oh_lo, bc(lo, 2, P), bc(const("iota128"), 1, 2 * NT), ALU.is_equal))
                    tid = bc(bc(const("token_id"), 1, 2), 3, SLOTS)
                    v.tensor_tensor(tv.rearrange("p (k t) c -> p k t c", k=2), tv.rearrange("p (k t) c -> p k t c", k=2), tid, ALU.mult).then_inc(placed, 1)
                    st.did(v.tensor_copy(nch_i, nch))
                    st.did(v.tensor_copy(first_i, first))
                    st.did(v.memset(slot_i[:, SLOTS:SLOTS + NT + 1], 0))
                    dve.wait_ge(tabled, 1)
                    st.did(v.tensor_copy(slot_i[:, 0:SLOTS], ps[:, 3, 0:SLOTS]))

            FH = FF // 2
            PW = KD * FH
            NP, NR = 6, 4
            slot = [0, 1, 2, 3, 1, 2]
            ALL = WORK + HTW
            whi, at = place("w_high", 0, (NP, PW), f32r)
            wlo, at = place("w_low", at, (NP, PW), f32r)
            xhi, at = place("x_high", at, (KD, P), f32r)
            xlo, at = place("x_low", at, (KD, P), f32r)
            ahi, at = place("hidden_high", at, (FT, P), f32r)
            alo, at = place("hidden_low", at, (FT, P), f32r)
            raw, at = place("w_raw", at, (NR, PW), f32)
            xg, at = view(at, (D,), ALL)
            h32, at = place("x_gathered", at, (KD, P), f32)
            sg_, at = view(at, (2, FH), ALL)
            a_, at = view(at, (2, FH), ALL)
            ysb, at = view(at, (D,), ALL)
            idx = small[:, 140:141].bitcast(u32)
            shift, scale = modc[:, layer, sub, 0], modc[:, layer, sub, 1]
            loaded = [sem(f"piece_loaded{q}") for q in range(NR)]
            hi_done, lo_done, lo_pool = sem("piece_hi"), sem("piece_lo"), sem("first_piece_lo")
            NV = NP - 1
            gd, ud = [sem("gate0_done"), sem("gate1_done")], [sem("up0_done"), sem("up1_done")]
            d_done = sem("down_done")
            idx_ready, idx_seen, gathered = sem("index_ready"), sem("index_seen"), sem("gathered")
            rows_seen, y_free = sem("rows_seen"), sem("y_rows_free")
            turned = sem("gathered_transposed")
            h_act, h_dve = sem("h_by_scalar"), sem("h_by_vector")
            xhi_ready, xlo_ready = sem("x_hi_ready"), sem("x_lo_ready")
            silu_done, a_ready = sem("silu_done"), sem("hidden_ready")
            ta = [sem("hidden0_transposed"), sem("hidden1_transposed")]
            ahi_ready, alo_ready = sem("hidden_hi_ready"), sem("hidden_lo_ready")
            y_act, y_dve, y_stored = sem("y_by_scalar"), sem("y_by_vector"), sem("y_stored")
            skips = {k.engine: sem("no_split") for k in (nc.scalar, nc.vector, nc.gpsimd)}

            def chunks(eng, body):
                def where_none(n, steps):
                    with eng.If(n):
                        eng.sem_inc(skips[eng.engine], 1)
                    with eng.Else():
                        steps()

                def expert(e, ahead):
                    at_ = bass.ds(e, 1)
                    n = eng.value_load(nch_i[0:1, at_], min_val=1, max_val=NT)
                    b = eng.value_load(first_i[0:1, at_], min_val=0, max_val=SLOTS - 1)
                    with eng.Fori(0, n) as c:
                        body(e, b + c, lambda steps: where_none(c, steps), lambda steps: ahead(n - 1 - c, steps))

                with eng.Fori(0, E - 1) as e:
                    expert(e, where_none)
                expert(E - 1, lambda left, steps: None)

            with nc.Block() as block:
                def wait_lo(eng, e, q):
                    if q == 0:
                        eng.wait_ge(lo_pool, e + 1)
                    else:
                        eng.wait_ge(lo_done, e * NV + q)

                @block.sync
                def _(sp):
                    def load(e, q):
                        if q >= NR:
                            wait_lo(sp, e, slot[q])
                        elif type(e) is not int:
                            wait_lo(sp, e - 1, NP - 1 - slot[::-1].index(q))
                        src = ins["experts"][bass.ds((e + layer * E) * NP + q, 1)].rearrange("c p n -> p (c n)")
                        sp.dma_start(raw[:, slot[q]], src).then_inc(loaded[slot[q]], 16)

                    for q in range(NP):
                        load(0, q)
                    with sp.Fori(1, E) as e:
                        for q in (0, 3, 1, 2, 4, 5):
                            load(e, q)
                    for q in range(NR):
                        sp.wait_ge(loaded[q], 16 * E * slot.count(q))

                @block.gpsimd
                def _(pool):
                    def gather(j):
                        nc.gpsimd.tensor_copy(idx, slot_i[:, bass.ds(j, 1)]).then_inc(idx_ready, 1)
                        pool.wait_ge(idx_ready, j + 1)
                        pool.sem_inc(idx_seen, 1)
                        nc.gpsimd.indirect_dma_start(out=xg, out_offset=None, in_=hrows[:, :],
                                                     in_offset=bass.IndirectOffsetOnAxis(ap=idx, axis=0)).then_inc(gathered, 16)

                    gather(0)
                    pool.wait_ge(hi_done, 1)
                    nc.gpsimd.tensor_tensor(wlo[:, 0], raw[:, 0], whi[:, 0].bitcast(f32), ALU.subtract).then_inc(lo_pool, 1)
                    pool.wait_ge(turned, 1)
                    gather(1)
                    pool.wait_ge(y_filled, (SLOTS - SEQ * TOPK // P) // NT * 16)

                    def first_lo(e):
                        pool.wait_ge(hi_done, e * NP + 1)
                        nc.gpsimd.tensor_tensor(wlo[:, 0], raw[:, 0], whi[:, 0].bitcast(f32), ALU.subtract).then_inc(lo_pool, 1)

                    def body(e, j, first, ahead):
                        ahead(lambda: first_lo(e + 1))
                        pool.wait_ge(y_act, j + 2)
                        pool.wait_ge(y_dve, j + 2)
                        pool.sem_inc(rows_seen, 1)
                        pool.dma_start(yrows[bass.ds(j * P, P), :], ysb).then_inc(y_stored, 16)
                        pool.wait_ge(turned, j + 2)
                        gather(j + 2)
                        pool.wait_ge(y_stored, j * 16 + 16)
                        pool.sem_inc(y_free, 1)

                    chunks(pool, body)

                @block.tensor
                def _(pe):
                    def transpose_rows(j):
                        pe.wait_ge(gathered, j * 16 + 16)
                        for k in range(KD):
                            last = nc.tensor.transpose(ps[:, k // 4, (k % 4) * P:(k % 4 + 1) * P], xg[:, k * P:(k + 1) * P], ident)
                        last.then_inc(turned, 1)

                    def three(out_, lh, ll, rh, rl, start, stop):
                        nc.tensor.matmul(out_, lh, rl, start=start, stop=False)
                        nc.tensor.matmul(out_, ll, rh, start=False, stop=False)
                        return nc.tensor.matmul(out_, lh, rh, start=False, stop=stop)

                    def hidden(j, e, q, done, ks=range(KD)):
                        if ks[0] == 0:
                            wait_lo(pe, e, q)
                        for k in ks:
                            w = slice(k * FH, (k + 1) * FH)
                            last = three(ps[:, q, 0:FH], xhi[:, k], xlo[:, k], whi[:, q, w], wlo[:, q, w], k == 0, k == KD - 1)
                        if ks[-1] == KD - 1:
                            last.then_inc(done, 1)

                    def transpose_hidden(j, h):
                        pe.wait_ge(a_ready, j * 2 + h + 1)
                        for f in range(2):
                            last = nc.tensor.transpose(ps[:, 4 + h, f * P:(f + 1) * P], a_[:, h, f * P:(f + 1) * P], ident)
                        last.then_inc(ta[h], 1)

                    def down(e, h, col):
                        for f in range(2):
                            w = slice(f * D + col * HALF, f * D + (col + 1) * HALF)
                            last = three(ps[:, 6 + col], ahi[:, 2 * h + f], alo[:, 2 * h + f], whi[:, 4 + h, w], wlo[:, 4 + h, w],
                                         h == 0 and f == 0, h == 1 and f == 1)
                        return last

                    transpose_rows(0)

                    def body(e, j, first, ahead):
                        pe.wait_ge(xlo_ready, j + 1)
                        hidden(j, e, 0, gd[0])
                        hidden(j, e, 1, ud[0])
                        hidden(j, e, 2, gd[1])
                        hidden(j, e, 3, ud[1], range(KD // 2))
                        transpose_hidden(j, 0)
                        hidden(j, e, 3, ud[1], range(KD // 2, KD))
                        pe.wait_ge(alo_ready, j * 2 + 1)
                        wait_lo(pe, e, 4)
                        pe.wait_ge(y_act, j + 1)
                        pe.wait_ge(y_dve, j + 1)
                        down(e, 0, 0)
                        transpose_hidden(j, 1)
                        transpose_rows(j + 1)
                        down(e, 0, 1)
                        pe.wait_ge(alo_ready, j * 2 + 2)
                        wait_lo(pe, e, 5)
                        down(e, 1, 0)
                        down(e, 1, 1).then_inc(d_done, 1)

                    chunks(pe, body)

                used = [gd[0], ud[0], gd[1], ud[1], d_done, d_done]

                @block.scalar
                def _(act):
                    def split_hi(e, q, uses):
                        act.wait_ge(loaded[slot[q]], (e * slot.count(slot[q]) + q // NR) * 16 + 16)
                        if uses is not None:
                            act.wait_ge(used[q], uses)
                        nc.scalar.copy(whi[:, q], raw[:, slot[q]]).then_inc(hi_done, 1)

                    def h_part(j):
                        act.wait_ge(turned, j + 1)
                        for k in range(4):
                            last = nc.scalar.activation(h32[:, k], ps[:, 0, k * P:(k + 1) * P], ACT.Identity, bias=shift[:, k:k + 1], scale=scale[:, k:k + 1])
                        last.then_inc(h_act, 1)

                    def x_hi(j):
                        act.wait_ge(h_act, j + 1)
                        act.wait_ge(h_dve, j + 1)
                        nc.scalar.copy(xhi, h32).then_inc(xhi_ready, 1)

                    def silu(j, h):
                        act.wait_ge(gd[h], j + 1)
                        nc.scalar.activation(sg_[:, h], ps[:, 2 * h, 0:FH], ACT.Silu).then_inc(silu_done, 1)

                    def a_hi(j, h):
                        act.wait_ge(ta[h], j + 1)
                        nc.scalar.copy(ahi[:, 2 * h:2 * h + 2].rearrange("p f n -> p (f n)"), ps[:, 4 + h, 0:2 * P]).then_inc(ahi_ready, 1)

                    nc.scalar.activation(sg_[:, 0, 0:1], eps, ACT.Silu)
                    act.sem_inc(y_act, 1)
                    act.sem_inc(y_free, 1)
                    split_hi(0, 0, None)
                    split_hi(0, 1, None)
                    h_part(0)
                    x_hi(0)
                    for q in (2, 3, 4):
                        split_hi(0, q, None)

                    def body(e, j, first, ahead):
                        silu(j, 0)
                        silu(j, 1)
                        a_hi(j, 0)
                        first(lambda: split_hi(e, 5, None))
                        ahead(lambda: split_hi(e + 1, 0, j + 1))
                        a_hi(j, 1)
                        h_part(j + 1)
                        x_hi(j + 1)
                        ahead(lambda: split_hi(e + 1, 1, j + 1))
                        act.wait_ge(d_done, j + 1)
                        act.wait_ge(y_free, j + 1)
                        nc.scalar.copy(ysb[:, 0:HALF], ps[:, 6]).then_inc(y_act, 1)
                        ahead(lambda: [split_hi(e + 1, q, j + 1) for q in (2, 3, 4)])

                    chunks(act, body)

                @block.vector
                def _(dve):
                    def split_lo(e, q):
                        dve.wait_ge(hi_done, e * NP + q + 1)
                        nc.vector.tensor_tensor(wlo[:, q], raw[:, slot[q]], whi[:, q].bitcast(f32), ALU.subtract).then_inc(lo_done, 1)

                    def h_part(j):
                        dve.wait_ge(turned, j + 1)
                        for k in range(4, KD):
                            last = nc.vector.tensor_scalar(h32[:, k], ps[:, 1, (k - 4) * P:(k - 3) * P], scale[:, k:k + 1], shift[:, k:k + 1], ALU.mult, ALU.add)
                        last.then_inc(h_dve, 1)

                    def x_lo(j):
                        dve.wait_ge(xhi_ready, j + 1)
                        nc.vector.tensor_tensor(xlo, h32, xhi.bitcast(f32), ALU.subtract).then_inc(xlo_ready, 1)

                    def gated(j, h):
                        dve.wait_ge(ud[h], j + 1)
                        dve.wait_ge(silu_done, j * 2 + h + 1)
                        nc.vector.tensor_tensor(a_[:, h], ps[:, 2 * h + 1, 0:FH], sg_[:, h], ALU.mult).then_inc(a_ready, 1)

                    def a_lo(j, h):
                        dve.wait_ge(ahi_ready, j * 2 + h + 1)
                        f = "p f n -> p (f n)"
                        nc.vector.tensor_tensor(alo[:, 2 * h:2 * h + 2].rearrange(f), ps[:, 4 + h, 0:2 * P], ahi[:, 2 * h:2 * h + 2].rearrange(f).bitcast(f32), ALU.subtract).then_inc(alo_ready, 1)

                    dve.sem_inc(y_dve, 1)
                    split_lo(0, 1)
                    h_part(0)
                    x_lo(0)
                    split_lo(0, 2)
                    split_lo(0, 3)

                    def body(e, j, first, ahead):
                        gated(j, 0)
                        first(lambda: split_lo(e, 4))
                        a_lo(j, 0)
                        gated(j, 1)
                        first(lambda: split_lo(e, 5))
                        a_lo(j, 1)
                        h_part(j + 1)
                        x_lo(j + 1)
                        dve.wait_ge(d_done, j + 1)
                        dve.wait_ge(y_free, j + 1)
                        nc.vector.tensor_copy(ysb[:, HALF:D], ps[:, 7]).then_inc(y_dve, 1)
                        ahead(lambda: [split_lo(e + 1, q) for q in (1, 2, 3)])

                    chunks(dve, body)

            y0, at = view(0, (2, D))
            y1, at = view(at, (2, D))
            ta, at = view(at, (2, D))
            idxs = small[:, 142:146].bitcast(u32)
            idx2_ready = sem("index2_ready")
            idx2_seen = sem("index2_seen")
            got = [sem("y_gathered0"), sem("y_gathered1")]
            w0_done, x_done = sem("y0_weighted"), sem("x_updated")
            chain2 = sem("combine_chain")
            o_stored = sem("out_stored")
            with nc.Block() as block:
                @block.gpsimd
                def _(pool):
                    with pool.Fori(0, NT // 2) as i:
                        for s in range(2):
                            t = i * 2 + s
                            pool.wait_ge(x_done, i * 2 + 2)
                            for k in range(2):
                                nc.gpsimd.tensor_copy(idxs[:, 2 * s + k:2 * s + k + 1], dest_i[:, bass.ds(t + k * NT, 1)]).then_inc(idx2_ready, 1)
                            pool.wait_ge(idx2_ready, t * 2 + 2)
                            pool.sem_inc(idx2_seen, 1)
                            for k, y in enumerate((y0, y1)):
                                nc.gpsimd.indirect_dma_start(out=y[:, s], out_offset=None, in_=yrows[0:SLOTS * P, :],
                                                             in_offset=bass.IndirectOffsetOnAxis(ap=idxs[:, 2 * s + k:2 * s + k + 1], axis=0)).then_inc(got[s], 16)

                @block.scalar
                def _(act):
                    with act.Fori(0, NT // 2) as i:
                        for s in range(2):
                            act.wait_ge(got[s], i * 32 + 32)
                            act.wait_ge(x_done, i * 2 + 2)
                            nc.scalar.activation(ta[:, s], y0[:, s], ACT.Copy, scale=wsel[:, bass.ds(i * 2 + s, 1)]).then_inc(w0_done, 1)

                @block.vector
                def _(dve):
                    dve.sem_inc(x_done, 2)
                    with dve.Fori(0, NT // 2) as i:
                        st = Steps(dve, chain2, turn=i, per=4)
                        for s in range(2):
                            dve.wait_ge(got[s], i * 32 + 32)
                            dve.wait_ge(w0_done, i * 2 + s + 1)
                            xt = x[:, bass.ds(i * 2 + s, 1), :].rearrange("p a d -> p (a d)")
                            st.link(nc.vector.scalar_tensor_tensor(ta[:, s], y1[:, s], wsel[:, bass.ds(i * 2 + s + NT, 1)], ta[:, s], ALU.mult, ALU.add))
                            st.link(nc.vector.tensor_tensor(ta[:, s], ta[:, s], gate[:, 1], ALU.mult))
                            nc.vector.tensor_tensor(xt, xt, ta[:, s], ALU.add).then_inc(x_done, 1)
                        st.end()

                if last_layer:
                    @block.sync
                    def _(sp):
                        with sp.Fori(0, NT) as t:
                            sp.wait_ge(x_done, t + 3)
                            sp.dma_start(out[0, bass.ds(t * P, P), :], x[:, bass.ds(t, 1), :].rearrange("p a d -> p (a d)")).then_inc(o_stored, 16)
                        sp.wait_ge(o_stored, NT * 16)

        def hybrid_phase(layer):
            QW = 2 * P
            qkv, at = view(0, (3, NT, ATT_W))
            upad, at = view(at, (CT, SEQ + CONV_W - 1))
            conv, at = view(at, (CT, SEQ))
            wring, at = view(at, (2, KD * QW))
            sgm, at = view(at, (2, HALF))
            par = {k: mix0[:, v[0]:v[0] + v[1]] for k, v in MIX0.items()}
            dw = par["dw_w"].rearrange("p (c j) -> p c j", j=CONV_W)
            w_loaded = [sem("w_in_loaded0"), sem("w_in_loaded1")]
            w_used = sem("w_in_used")
            u_done = sem("conv_product_done")
            sig_done, a_done = sem("sigmoid_done"), sem("a_copied")
            glu_done = sem("glu_done")
            qkv_done, qkv_out = sem("qkv_block_done"), sem("qkv_evacuated")
            padded = sem("pad_zeroed")
            chain = sem("conv_chain")
            NU, NB = CT, 3 * ATT_W // QW
            with nc.Block() as block:
                @block.sync
                def _(sp):
                    with sp.Fori(0, (NU + NB) // 2) as i:
                        for s in range(2):
                            sp.wait_ge(w_used, i * 2 + s + 1)
                            sp.dma_start(wring[:, s], ins["hy_in"][bass.ds(i * 2 + s, 1)].rearrange("c p n -> p (c n)")).then_inc(w_loaded[s], 16)

                @block.tensor
                def _(pe):
                    pe.sem_inc(w_used, 2)
                    with pe.Fori(0, NU // 2) as i:
                        for s in range(2):
                            w = wring[:, s].rearrange("p (k n) -> p k n", n=QW)
                            pe.wait_ge(w_loaded[s], i * 16 + 16)
                            pe.wait_ge(sig_done, i * 4 + 4)
                            pe.wait_ge(a_done, i * 4 + 4)
                            for h in range(2):
                                for q in range(2):
                                    for k in range(KD):
                                        last = nc.tensor.matmul(ps[:, s * 4 + h * 2 + q], w[:, k, q * P:(q + 1) * P], hT[:, k, h * HALF:(h + 1) * HALF], start=(k == 0), stop=(k == KD - 1))
                                last.then_inc(u_done, 1)
                            pe.wait_ge(u_done, i * 4 + s * 2 + 2)
                            pe.sem_inc(w_used, 1)
                    pe.wait_ge(sig_done, NU * 2 + 4)
                    pe.wait_ge(a_done, NU * 2 + 4)
                    with pe.Fori(0, NB // 2) as i:
                        for s in range(2):
                            w = wring[:, s].rearrange("p (k n) -> p k n", n=QW)
                            pe.wait_ge(w_loaded[s], i * 16 + 16 * (NU // 2 + 1))
                            for t in range(NT):
                                pe.wait_ge(qkv_out, i * 2 * NT + s * NT + t + 1)
                                for k in range(KD):
                                    last = nc.tensor.matmul(ps[:, t, 0:QW], hT[:, k, t * P:(t + 1) * P], w[:, k], start=(k == 0), stop=(k == KD - 1))
                                last.then_inc(qkv_done, 1)
                            pe.wait_ge(qkv_done, i * 2 * NT + (s + 1) * NT)
                            pe.sem_inc(w_used, 1)

                @block.scalar
                def _(act):
                    act.sem_inc(qkv_out, NT)
                    act.sem_inc(sig_done, 4)
                    act.sem_inc(a_done, 4)
                    with act.Fori(0, NU // 2) as i:
                        for s in range(2):
                            for h in range(2):
                                n = i * 4 + s * 2 + h
                                act.wait_ge(u_done, n + 1)
                                act.wait_ge(glu_done, i * 4 + s * 2 + 2)
                                nc.scalar.activation(sgm[:, h], ps[:, s * 4 + h * 2 + 1], ACT.Sigmoid).then_inc(sig_done, 1)
                                nc.scalar.copy(upad[:, bass.ds(i * 2 + s, 1), CONV_W - 1 + h * HALF:CONV_W - 1 + (h + 1) * HALF].rearrange("p a n -> p (a n)"), ps[:, s * 4 + h * 2]).then_inc(a_done, 1)
                    with act.Fori(0, NB // 2) as i:
                        for s in range(2):
                            for t in range(NT):
                                act.wait_ge(qkv_done, i * 2 * NT + s * NT + t + 1)
                                nc.scalar.copy(qkv[:, bass.ds(i, 1), t, s * QW:(s + 1) * QW].rearrange("p a n -> p (a n)"), ps[:, t, 0:QW]).then_inc(qkv_out, 1)

                @block.gpsimd
                def _(pool):
                    pool.sem_inc(glu_done, 2)
                    with pool.Fori(0, NU) as c:
                        for h in range(2):
                            pool.wait_ge(sig_done, c * 2 + h + 5)
                            pool.wait_ge(a_done, c * 2 + h + 5)
                            u = upad[:, bass.ds(c, 1), CONV_W - 1 + h * HALF:CONV_W - 1 + (h + 1) * HALF].rearrange("p a n -> p (a n)")
                            nc.gpsimd.tensor_tensor(u, u, sgm[:, h], ALU.mult).then_inc(glu_done, 1)

                @block.vector
                def _(dve):
                    nc.vector.memset(upad[:, :, 0:CONV_W - 1], 0.0).then_inc(padded, 1)
                    dve.wait_ge(padded, 1)
                    with dve.Fori(0, CT) as c:
                        dve.wait_ge(glu_done, c * 2 + 4)
                        st = Steps(dve, chain, turn=c, per=CONV_W)
                        y = conv[:, bass.ds(c, 1), :].rearrange("p a n -> p (a n)")
                        for j in range(CONV_W):
                            u = upad[:, bass.ds(c, 1), j:j + SEQ].rearrange("p a n -> p (a n)")
                            w = dw[:, bass.ds(c, 1), j]
                            if j == 0:
                                st.link(nc.vector.tensor_scalar(y, u, w, par["dw_b"][:, bass.ds(c, 1)], ALU.mult, ALU.add))
                            else:
                                st.link(nc.vector.scalar_tensor_tensor(y, u, w, y, ALU.mult, ALU.add))
                        st.end()

            sq, _ = view(at - 2 * HALF - 2 * KD * QW, (CT, HALF))
            mu = hT[:, 0, 0:HALF]
            sd = hT[:, 1, 0:HALF]
            qsq = hT[:, 2:6, :].rearrange("p a b -> p (a b)")
            rqk = small[:, 16:16 + 2 * NT * HEADS]
            gq8 = small[:, 150:151]
            summed, centred, sq_done, var_sum = sem("ln_summed"), sem("centred"), sem("ln_squared"), sem("ln_var_summed")
            sd_done, normed = sem("ln_sd"), sem("ln_normed")
            qsq_done, qss_done, qrms = sem("qk_squared"), sem("qk_summed"), sem("qk_rms")
            chain = sem("ln_chain")
            wo_loaded = sem("w_out_loaded")
            with nc.Block() as block:
                @block.tensor
                def _(pe):
                    for h in range(2):
                        cols = slice(h * HALF, (h + 1) * HALF)
                        for c in range(CT):
                            last = nc.tensor.matmul(ps[:, h], ones, conv[:, c, cols], start=(c == 0), stop=(c == CT - 1))
                        last.then_inc(summed, 1)
                        pe.wait_ge(sq_done, h + 1)
                        for c in range(CT):
                            last = nc.tensor.matmul(ps[:, 2 + h], ones, sq[:, c], start=(c == 0), stop=(c == CT - 1))
                        last.then_inc(var_sum, 1)

                @block.vector
                def _(dve):
                    st = Steps(dve, chain)
                    for h in range(2):
                        y = conv[:, :, h * HALF:(h + 1) * HALF]
                        dve.wait_ge(summed, h + 1)
                        st.link(nc.vector.tensor_scalar(mu, ps[:, h], 1.0 / CONV_CH, None, ALU.mult))
                        nc.vector.tensor_tensor(y, y, bc(mu, 1, CT), ALU.subtract).then_inc(centred, 1)
                        dve.wait_ge(centred, h + 1)
                        dve.wait_ge(sd_done, h + 1)
                        st.link(nc.vector.reciprocal(sd, sd))
                        nc.vector.tensor_tensor(y, y, bc(sd, 1, CT), ALU.mult).then_inc(normed, 1)
                        dve.wait_ge(normed, h + 1)
                    for n in range(2):
                        dve.wait_ge(qsq_done, n + 1)
                        nc.vector.tensor_reduce(rqk[:, n * NT * HEADS:(n + 1) * NT * HEADS], qsq.rearrange("p (a d) -> p a d", d=HD), X, ALU.add).then_inc(qss_done, 1)
                    dve.wait_ge(qrms, 1)
                    st.did(nc.vector.reciprocal(rqk, rqk))
                    st.did(nc.vector.tensor_scalar(gq8, par["gq"], float(HD) ** -0.5, None, ALU.mult))

                @block.scalar
                def _(act):
                    for h in range(2):
                        act.wait_ge(centred, h + 1)
                        if h:
                            act.wait_ge(var_sum, h)
                        nc.scalar.activation(sq, conv[:, :, h * HALF:(h + 1) * HALF], ACT.Square).then_inc(sq_done, 1)
                        act.wait_ge(var_sum, h + 1)
                        if h:
                            act.wait_ge(normed, h)
                        nc.scalar.activation(sd, ps[:, 2 + h], ACT.Sqrt, bias=eps, scale=1.0 / CONV_CH).then_inc(sd_done, 1)
                    act.wait_ge(normed, 2)
                    for c in range(CT):
                        nc.scalar.activation(conv[:, c], conv[:, c], ACT.Silu, bias=par["ln_b"][:, c:c + 1], scale=par["ln_g"][:, c:c + 1])
                    for n in range(2):
                        if n:
                            act.wait_ge(qss_done, n)
                        nc.scalar.activation(qsq, qkv[:, n].rearrange("p t d -> p (t d)"), ACT.Square).then_inc(qsq_done, 1)
                    act.wait_ge(qss_done, 2)
                    nc.scalar.activation(rqk, rqk, ACT.Sqrt, bias=eps, scale=1.0 / HD).then_inc(qrms, 1)

            at = NT * ATT_W * 3
            attT, at = view(at, (PAIRS, SEQ))
            at = NT * ATT_W * 3 + CT * (SEQ + CONV_W - 1) + CT * SEQ
            qn, at = view(at, (NT, P))
            kn, at = view(at, (NT, P))
            qT, at = view(at, (SEQ,))
            kT, at = view(at, (SEQ,))
            pr, at = view(at, (2, SEQ))
            pT, at = view(at, (2, SEQ))
            att, at = view(at, (NT, P))
            nmax = small[:, 152:154]
            rsum = small[:, 156:160]
            U = 2 * NT
            qk_ready, qk_turned = sem("qk_normed"), sem("qk_transposed")
            qT_ready, kT_ready = sem("qT_ready"), sem("kT_ready")
            s_done, m_done, p_done = sem("scores_ready"), sem("max_ready"), sem("probs_ready")
            t_done, pa, pb = sem("probs_transposed"), sem("pT_by_vector"), sem("pT_by_scalar")
            o_done, o_out = sem("pv_ready"), sem("out_normed")
            att_turned, att_out = sem("att_transposed"), sem("attT_ready")
            chain = sem("attention_chain")
            with nc.Block() as block:
                @block.sync
                def _(sp):
                    sp.dma_start(hT[:, :, :].rearrange("p k n -> p (k n)"), ins["hy_out"]).then_inc(wo_loaded, 16)
                    sp.wait_ge(wo_loaded, 16)

                @block.gpsimd
                def _(pool):
                    def norm_qk(i):
                        for n, dst in enumerate((qn, kn)):
                            r = rqk[:, n * NT * HEADS:(n + 1) * NT * HEADS].rearrange("p (t h) -> p t h", h=HEADS)
                            for hh in range(2):
                                src = qkv[:, n, :, bass.ds(i * P + hh * HD, HD)]
                                nc.gpsimd.tensor_tensor(dst[:, :, hh * HD:(hh + 1) * HD], src, r[:, :, bass.ds(i * 2 + hh, 1)].to_broadcast([P, NT, HD]), ALU.mult).then_inc(qk_ready, 1)

                    norm_qk(0)
                    with pool.Fori(1, PAIRS) as i:
                        pool.wait_ge(qk_turned, i * 2)
                        norm_qk(i)

                @block.tensor
                def _(pe):
                    with pe.Fori(0, PAIRS) as i:
                        for n, src in enumerate((qn, kn)):
                            pe.wait_ge(qk_ready, i * 4 + 2 * n + 2)
                            for t in range(NT):
                                last = nc.tensor.transpose(ps[:, 4 + 2 * n + t // 4, (t % 4) * P:(t % 4 + 1) * P], src[:, t], ident)
                            last.then_inc(qk_turned, 1)
                        pe.wait_ge(qT_ready, i + 1)
                        pe.wait_ge(kT_ready, i + 1)

                        def scores(u):
                            head, qt = divmod(u, NT)
                            rows_ = slice(head * HD, (head + 1) * HD)
                            b = (u % 2) * 2
                            if u >= 2:
                                pe.wait_ge(p_done, i * U + u - 1)
                            for h in range(0, (qt + 1) * P, HALF):
                                n = min(HALF, (qt + 1) * P - h)
                                diag = h + n == (qt + 1) * P
                                last = nc.tensor.matmul(ps[:, b + h // HALF, 0:n], qT[rows_, qt * P:(qt + 1) * P], kT[rows_, h:h + n], start=True, stop=True)
                                if diag:
                                    last = nc.tensor.matmul(ps[:, b + h // HALF, n - P:n], ident, const("maskneg"), start=False, stop=True, skip_group_check=True)
                            last.then_inc(s_done, 1)

                        def turn(u):
                            qt = u % NT
                            pe.wait_ge(p_done, i * U + u + 1)
                            if u:
                                pe.wait_ge(pa, i * U + u)
                                pe.wait_ge(pb, i * U + u)
                            for k in range(qt + 1):
                                last = nc.tensor.transpose(ps[:, 4 + k // 4, (k % 4) * P:(k % 4 + 1) * P], pr[:, u % 2, k * P:(k + 1) * P], ident)
                            last.then_inc(t_done, 1)

                        def values(u):
                            head, qt = divmod(u, NT)
                            pe.wait_ge(pa, i * U + u + 1)
                            pe.wait_ge(pb, i * U + u + 1)
                            if u >= 2:
                                pe.wait_ge(o_out, i * U + u - 1)
                            for k in range(qt + 1):
                                last = nc.tensor.matmul(ps[:, 6 + u % 2, 0:HD], pT[:, u % 2, k * P:(k + 1) * P], qkv[:, 2, k, bass.ds(i * P + head * HD, HD)], start=(k == 0), stop=(k == qt))
                            last.then_inc(o_done, 1)

                        scores(0)
                        scores(1)
                        for u in range(U):
                            turn(u)
                            if u + 2 < U:
                                scores(u + 2)
                            if u:
                                values(u - 1)
                        values(U - 1)
                        pe.wait_ge(o_out, i * U + U)
                        for t in range(NT):
                            last = nc.tensor.transpose(ps[:, 4 + t // 4, (t % 4) * P:(t % 4 + 1) * P], att[:, t], ident)
                        last.then_inc(att_turned, 1)
                        pe.wait_ge(att_out, i + 2)

                @block.scalar
                def _(act):
                    with act.Fori(0, PAIRS) as i:
                        act.wait_ge(qk_turned, i * 2 + 1)
                        nc.scalar.activation(qT, ps[:, 4:6].rearrange("p a n -> p (a n)"), ACT.Copy, scale=gq8).then_inc(qT_ready, 1)

                        def probs(u):
                            n = (u % NT + 1) * P
                            act.wait_ge(m_done, i * U + u + 1)
                            if u >= 2:
                                act.wait_ge(t_done, i * U + u - 1)
                            if u >= 4:
                                act.wait_ge(o_out, i * U + u - 3)
                            b = (u % 2) * 2
                            nc.scalar.activation(pr[:, u % 2, 0:n], ps[:, b:b + 2].rearrange("p a n -> p (a n)")[:, 0:n], ACT.Exp, bias=nmax[:, u % 2:u % 2 + 1], accum_out=rsum[:, u % 4:u % 4 + 1]).then_inc(p_done, 1)

                        probs(0)
                        for u in range(U):
                            if u + 1 < U:
                                probs(u + 1)
                            act.wait_ge(t_done, i * U + u + 1)
                            n = (u % NT + 1) * P
                            if n > HALF:
                                if u >= 2:
                                    act.wait_ge(o_done, i * U + u - 1)
                                nc.scalar.copy(pT[:, u % 2, HALF:n], ps[:, 5, 0:n - HALF]).then_inc(pb, 1)
                            else:
                                act.sem_inc(pb, 1)
                        act.wait_ge(att_out, i + 2)

                @block.vector
                def _(dve):
                    dve.sem_inc(att_out, 1)
                    with dve.Fori(0, PAIRS) as i:
                        st = Steps(dve, chain, turn=i, per=U)
                        dve.wait_ge(qk_turned, i * 2 + 2)
                        nc.vector.tensor_scalar(kT, ps[:, 6:8].rearrange("p a n -> p (a n)"), par["gk"], None, ALU.mult).then_inc(kT_ready, 1)

                        def maxes(u):
                            n = (u % NT + 1) * P
                            b = (u % 2) * 2
                            dve.wait_ge(s_done, i * U + u + 1)
                            if u >= 2:
                                dve.wait_ge(p_done, i * U + u - 1)
                            nc.vector.tensor_reduce(nmax[:, u % 2:u % 2 + 1], ps[:, b:b + 2].rearrange("p a n -> p (a n)")[:, 0:n], X, ALU.max, negate=True).then_inc(m_done, 1)

                        def normed(u):
                            head, qt = divmod(u, NT)
                            dve.wait_ge(p_done, i * U + u + 1)
                            r = rsum[:, u % 4:u % 4 + 1]
                            st.link(nc.vector.reciprocal(rinv, r))
                            dve.wait_ge(o_done, i * U + u + 1)
                            nc.vector.tensor_scalar(att[:, qt, head * HD:(head + 1) * HD], ps[:, 6 + u % 2, 0:HD], rinv, None, ALU.mult).then_inc(o_out, 1)
                            dve.wait_ge(o_out, i * U + u + 1)

                        rinv = small[:, 154:155]
                        maxes(0)
                        maxes(1)
                        for u in range(U):
                            dve.wait_ge(t_done, i * U + u + 1)
                            n = min((u % NT + 1) * P, HALF)
                            if u >= 2:
                                dve.wait_ge(o_done, i * U + u - 1)
                            nc.vector.tensor_copy(pT[:, u % 2, 0:n], ps[:, 4, 0:n]).then_inc(pa, 1)
                            if u + 2 < U:
                                maxes(u + 2)
                            if u:
                                normed(u - 1)
                        normed(U - 1)
                        st.end()
                        dve.wait_ge(att_turned, i + 1)
                        nc.vector.tensor_copy(attT[:, bass.ds(i, 1), :].rearrange("p a n -> p (a n)"), ps[:, 4:6].rearrange("p a n -> p (a n)")).then_inc(att_out, 1)
                        dve.wait_ge(att_out, i + 2)

            tmp, at = view(at - NT * P, (2, HALF))
            done, updated = sem("out_product"), sem("x_updated")
            chain = sem("out_chain")
            with nc.Block() as block:
                @block.tensor
                def _(pe):
                    with pe.Fori(0, 2) as h:
                        for t in range(NT):
                            pe.wait_ge(updated, h * NT + NT)
                            for k in range(KD):
                                src = attT[:, k] if k < PAIRS else conv[:, k - PAIRS]
                                last = nc.tensor.matmul(ps[:, t], src[:, t * P:(t + 1) * P], hT[:, k, bass.ds(h * HALF, HALF)], start=(k == 0), stop=(k == KD - 1))
                            last.then_inc(done, 1)

                @block.vector
                def _(dve):
                    dve.sem_inc(updated, NT)
                    with dve.Fori(0, 2) as h:
                        st = Steps(dve, chain, turn=h, per=NT)
                        for t in range(NT):
                            dve.wait_ge(done, h * NT + t + 1)
                            st.link(nc.vector.tensor_tensor(tmp[:, t % 2], ps[:, t], gate[:, 0, bass.ds(h * HALF, HALF)], ALU.mult))
                            xt = x[:, t, bass.ds(h * HALF, HALF)]
                            nc.vector.tensor_tensor(xt, xt, tmp[:, t % 2], ALU.add).then_inc(updated, 1)
                            dve.wait_ge(updated, h * NT + t + NT + 1)
                        st.end()

        def ssm_phase(layer):
            TPC = CHUNK // P
            GT = GW // P
            CTG = GT + 2
            H, DH = SSM_HEADS, SSM_HEAD_DIM
            LC = CHUNK + P
            par = {k: mix1[:, v[0]:v[0] + v[1]] for k, v in MIX1.items()}
            cw = par["conv_w"].rearrange("p (c j) -> p c j", j=SCONV)
            row = {k: rows[:, v[0]:v[0] + v[1]] for k, v in ROWS.items()}
            dt, at = view(0, (NT, H))
            acs, at = view(at, (NT, H))
            eacs, at = view(at, (NT, H))
            dst, at = view(at, (NT, H))
            cdec, at = view(at, (NCH, H))
            base = at
            wdt, at = view(at, (KD, H))
            t0_, at = view(at, (NT, H))
            t1_, at = view(at, (NT, H))
            t2_, at = view(at, (NT, H))
            da, at = view(at, (NT, H))
            nega, at = view(at, (H,))
            arow, at = view(at, (SEQ,))
            wdt_loaded, dt_raw, chain = sem("dt_w_loaded"), sem("dt_product"), sem("dt_chain")
            exp_done, ln_done, a_done = sem("dt_exp"), sem("dt_ln"), sem("a_exp")
            abs_done, u_done2 = sem("dt_abs"), sem("dt_one_plus")
            da_ready, cums, e_done, arow_out = sem("da_ready"), sem("cumsums"), sem("decays"), sem("acs_row_ready")
            cum_out, dec_in = sem("acs_ready"), sem("decay_in_ready")
            arow_stored = sem("acs_rows_stored")
            with nc.Block() as block:
                @block.sync
                def _(sp):
                    sp.dma_start(wdt.rearrange("p k n -> p (k n)"), ins["ssm_dt"]).then_inc(wdt_loaded, 16)
                    sp.wait_ge(arow_out, 1)
                    sp.dma_start(acs_rows[:, :], arow[0:H, :]).then_inc(arow_stored, 16)
                    sp.wait_ge(arow_stored, 16)

                @block.tensor
                def _(pe):
                    pe.wait_ge(wdt_loaded, 16)
                    for t in range(NT):
                        for k in range(KD):
                            last = nc.tensor.matmul(ps[:, 0, t * H:(t + 1) * H], hT[:, k, t * P:(t + 1) * P], wdt[:, k], start=(k == 0), stop=(k == KD - 1))
                    last.then_inc(dt_raw, 1)
                    pe.wait_ge(da_ready, 1)
                    for c in range(NCH):
                        a, b = 2 * c, 2 * c + 1
                        nc.tensor.matmul(ps[:, 1, a * H:(a + 1) * H], const("tri_inc"), da[:, a], start=True, stop=True)
                        nc.tensor.matmul(ps[:, 1, b * H:(b + 1) * H], const("tri_inc"), da[:, b], start=True, stop=False)
                        nc.tensor.matmul(ps[:, 1, b * H:(b + 1) * H], ones, da[:, a], start=False, stop=True)
                        nc.tensor.matmul(ps[:, 2, c * H:(c + 1) * H], ones, da[:, a], start=True, stop=False)
                        nc.tensor.matmul(ps[:, 2, c * H:(c + 1) * H], ones, da[:, b], start=False, stop=True)
                        r = ps[0:H, 3 + c // 2, (c % 2) * CHUNK:(c % 2 + 1) * CHUNK]
                        at_, n_ = CONST["tri_inc"]
                        nc.tensor.matmul(r, da[:, a], cst[:, at_:at_ + 2 * P], start=True, stop=True)
                        last = nc.tensor.matmul(r[:, P:2 * P], da[:, b], const("tri_inc"), start=False, stop=True, skip_group_check=True)
                    last.then_inc(cums, 1)

                @block.scalar
                def _(act):
                    nc.scalar.activation(nega, row["a_log"], ACT.Exp).then_inc(a_done, 1)
                    act.wait_ge(abs_done, 1)
                    f = lambda v: v.rearrange("p t h -> p (t h)")
                    nc.scalar.activation(f(t1_), f(t1_), ACT.Exp, scale=-1.0).then_inc(exp_done, 1)
                    act.wait_ge(u_done2, 1)
                    nc.scalar.activation(f(da), f(t2_), ACT.Ln).then_inc(ln_done, 1)
                    act.wait_ge(dec_in, 1)
                    nc.scalar.activation(f(eacs), f(acs), ACT.Exp)
                    nc.scalar.activation(f(dst), f(dst), ACT.Exp)
                    nc.scalar.activation(f(cdec), f(cdec), ACT.Exp).then_inc(e_done, 1)
                    act.wait_ge(cums, 1)
                    nc.scalar.copy(arow[0:H, :], ps[0:H, 3:5].rearrange("p a n -> p (a n)")).then_inc(arow_out, 1)

                @block.vector
                def _(dve):
                    v = nc.vector
                    st = Steps(dve, chain)
                    dve.wait_ge(dt_raw, 1)
                    st.link(v.tensor_tensor(t0_, ps[:, 0, 0:NT * H].rearrange("p (t h) -> p t h", h=H), bc(row["dt_bias"], 1, NT), ALU.add))
                    st.link(v.tensor_scalar(t1_, t0_, -1.0, None, ALU.mult))
                    v.tensor_tensor(t1_, t0_, t1_, ALU.max).then_inc(abs_done, 1)
                    dve.wait_ge(exp_done, 1)
                    v.tensor_scalar(t2_, t1_, 1.0, None, ALU.add).then_inc(u_done2, 1)
                    dve.wait_ge(u_done2, 1)
                    dve.wait_ge(ln_done, 1)
                    st.link(v.tensor_scalar(t2_, t2_, 1.0, None, ALU.subtract))
                    st.link(v.tensor_scalar(dt, t2_, 0.0, None, ALU.is_equal))
                    st.did(v.tensor_tensor(da, da, dt, ALU.add))
                    st.link(v.tensor_tensor(t2_, t2_, dt, ALU.add))
                    st.link(v.reciprocal(t2_, t2_))
                    st.link(v.tensor_tensor(da, da, t1_, ALU.mult))
                    st.link(v.tensor_tensor(da, da, t2_, ALU.mult))
                    st.link(v.scalar_tensor_tensor(dt, t0_, 0.0, da, ALU.max, ALU.add))
                    dve.wait_ge(a_done, 1)
                    st.link(v.tensor_scalar(nega, nega, -1.0, None, ALU.mult))
                    v.tensor_tensor(da, dt, bc(nega, 1, NT), ALU.mult).then_inc(da_ready, 1)
                    dve.wait_ge(cums, 1)
                    st.link(v.tensor_copy(acs.rearrange("p t h -> p (t h)"), ps[:, 1, 0:NT * H]))
                    st.link(v.tensor_copy(cdec.rearrange("p t h -> p (t h)"), ps[:, 2, 0:NCH * H]))
                    v.tensor_tensor(dst.rearrange("p (c a) h -> p c a h", a=TPC), bc(cdec, 2, TPC), acs.rearrange("p (c a) h -> p c a h", a=TPC), ALU.subtract).then_inc(dec_in, 1)

            HB = 2
            NBAT = HPG // HB
            at = base
            xw, at = view(at, (2, KD * P))
            zw, at = view(at, (KD, GW))
            ow, at = view(at, (GT, D))
            raw, at = view(at, (2, SEQ + SCONV))
            cv_at = at
            cv, at = view(at, (2, SEQ))
            BT, at = view(at, (SEQ,))
            CTt, at = view(at, (SEQ,))
            xs, at = view(at, (NT, GW))
            Btok, at = view(at, (NT, P))
            rbc, at = view(at, (HPG, CHUNK))
            cbt, at = view(at, (LC,))
            mt01, at = view(at, (2, HB, LC))
            assert NBAT == 4 and 2 * HB * LC <= 2 * SEQ
            mt23, _ = view(cv_at, (2, HB, LC))
            mt = [mt01[:, 0], mt01[:, 1], mt23[:, 0], mt23[:, 1]]
            xdt, at = view(at, (TPC, GW))
            xdec, at = view(at, (TPC, GW))
            state, at = view(at, (GW,))
            zs, at = view(at, (TPC, GW))
            y, at = view(at, (TPC, GW))
            tq, at = view(at, (GW,))
            gT, at = view(at, (GT, P))
            acg = small[:, 16:16 + NT * HPG].rearrange("p (t h) -> p t h", h=HPG)
            normg = small[:, 96:96 + GT]
            ssq = small[:, 90:92]
            w_xbc = [sem("xbc_w_loaded0"), sem("xbc_w_loaded1")]
            w_z, w_o = sem("z_w_loaded"), sem("out_w_loaded")
            xw_used, z_used, o_used = sem("xbc_w_used"), sem("z_product"), sem("out_product")
            raw_out, zeroed = sem("raw_evacuated"), sem("pads_zeroed")
            convd, cv_ready = sem("convolved"), sem("conv_silu")
            turned, tv, ta = sem("xs_transposed"), sem("xs_by_vector"), sem("xs_by_scalar")
            rb_loaded, acg_ready = sem("acs_broadcast"), sem("acs_group_copied")
            cb_done, cb_out = sem("cb_ready"), sem("cb_masked")
            slot_seen = sem("decay_slot_seen")
            diff, expd, mt_ready = sem("decay_exponent"), sem("decay_exp"), sem("decayed_cb")
            xdt_ready, xdec_ready = sem("xdt_ready"), sem("xdec_ready")
            st_done, st_out = sem("state_product"), sem("state_updated")
            yo_done, yd_done = sem("y_off_ready"), sem("y_diag_ready")
            z_out, y1_, y2_ = sem("z_silu"), sem("y_gated"), sem("y_normed")
            sq_done, rt_done = sem("y_squared"), sem("y_rms")
            g_turned, g_out = sem("y_transposed"), sem("gT_ready")
            o_out = sem("x_updated")
            chain = sem("ssd_chain")
            CPG = NCH * TPC
            with nc.Block() as block:
                @block.sync
                def _(sp):
                    with sp.Fori(0, SSM_G) as g:
                        for c in range(CTG):
                            sp.wait_ge(xw_used, g * CTG + c + 1)
                            sp.dma_start(xw[:, c % 2], ins["ssm_xbc"][bass.ds(g * CTG + c, 1)].rearrange("c p n -> p (c n)")).then_inc(w_xbc[c % 2], 16)
                            if c == 1:
                                sp.wait_ge(z_used, (g + 1) * CPG)
                                sp.dma_start(zw.rearrange("p k n -> p (k n)"), ins["ssm_z"][bass.ds(g, 1)].rearrange("c p n -> p (c n)")).then_inc(w_z, 16)
                            if c == 2:
                                sp.wait_ge(o_used, (g + 1) * 2 * CPG)
                                sp.dma_start(ow.rearrange("p k n -> p (k n)"), ins["ssm_out"][bass.ds(g, 1)].rearrange("c p n -> p (c n)")).then_inc(w_o, 16)
                        for c in range(NCH):
                            sp.wait_ge(diff, (g * NCH + c + 1) * NBAT)
                            sp.dma_start(rbc, acs_rows[bass.ds(g * HPG, HPG), c * CHUNK:(c + 1) * CHUNK].unsqueeze(0).to_broadcast([P, HPG, CHUNK])).then_inc(rb_loaded, 16)

                @block.tensor
                def _(pe):
                    pe.sem_inc(xw_used, 2)
                    pe.sem_inc(z_used, CPG)
                    pe.sem_inc(o_used, 2 * CPG)
                    pe.sem_inc(yd_done, NBAT)
                    with pe.Fori(0, SSM_G) as g:
                        def conv_turn(c):
                            src = cv[:, c % 2] if c < GT else BT
                            pe.wait_ge(cv_ready, g * CTG + c + 1)
                            if c:
                                pe.wait_ge(tv, g * (GT + 1) + c)
                                pe.wait_ge(ta, g * (GT + 1) + c)
                            for t in range(NT):
                                last = nc.tensor.transpose(ps[:, 4 + t // 4, (t % 4) * P:(t % 4 + 1) * P], src[:, t * P:(t + 1) * P], ident)
                            last.then_inc(turned, 1)

                        for c in range(CTG):
                            w = xw[:, c % 2].rearrange("p (k n) -> p k n", n=P)
                            pe.wait_ge(w_xbc[c % 2], g * (CTG // 2 * 16) + 16 * (c // 2 + 1))
                            if c >= 2:
                                pe.wait_ge(raw_out, g * CTG + c - 1)
                            for h in range(2):
                                for k in range(KD):
                                    last = nc.tensor.matmul(ps[:, (c % 2) * 2 + h], w[:, k], hT[:, k, h * HALF:(h + 1) * HALF], start=(k == 0), stop=(k == KD - 1))
                            last.then_inc(xw_used, 1)
                            if 1 <= c <= GT + 1:
                                conv_turn(c - 1)

                        def z_product(c, a):
                            t = c * TPC + a
                            if t == 0:
                                pe.wait_ge(w_z, g * 16 + 16)
                                pe.wait_ge(raw_out, g * CTG + CTG)
                            if t >= TPC:
                                pe.wait_ge(z_out, g * CPG + t - TPC + 1)
                            for k in range(KD):
                                last = nc.tensor.matmul(ps[:, 1 + a], hT[:, k, t * P:(t + 1) * P], zw[:, k], start=(k == 0), stop=(k == KD - 1))
                            last.then_inc(z_used, 1)

                        def cb_product(c):
                            if c == 0:
                                pe.wait_ge(cv_ready, g * CTG + CTG)
                                pe.wait_ge(raw_out, g * CTG + CTG)
                            else:
                                pe.wait_ge(cb_out, g * NCH + c)
                            l0 = c * CHUNK
                            nc.tensor.matmul(ps[:, 0, 0:CHUNK], BT[:, l0:l0 + P], CTt[:, l0:l0 + CHUNK], start=True, stop=True)
                            nc.tensor.matmul(ps[:, 0, CHUNK:LC], BT[:, l0 + P:l0 + CHUNK], CTt[:, l0 + P:l0 + CHUNK], start=True, stop=True).then_inc(cb_done, 1)

                        def out_product(c, a):
                            t = c * TPC + a
                            pe.wait_ge(y2_, g * CPG + t + 1)
                            if t:
                                pe.wait_ge(g_out, g * CPG + t)
                            for k in range(GT):
                                last = nc.tensor.transpose(ps[:, 5, k * P:(k + 1) * P], y[:, a, k * P:(k + 1) * P], ident)
                            last.then_inc(g_turned, 1)
                            pe.wait_ge(g_out, g * CPG + t + 1)
                            if t == 0:
                                pe.wait_ge(w_o, g * 16 + 16)
                            for h in range(2):
                                if t:
                                    pe.wait_ge(o_out, (g * CPG + t) * 2 + h - 1)
                                for k in range(GT):
                                    last = nc.tensor.matmul(ps[:, 6 + h], gT[:, k], ow[:, k, h * HALF:(h + 1) * HALF], start=(k == 0), stop=(k == GT - 1))
                                last.then_inc(o_used, 1)

                        for c in range(NCH):
                            cb_product(c)
                            for a in range(TPC):
                                z_product(c, a)
                            if c:
                                for a in range(TPC):
                                    out_product(c - 1, a)
                            if c:
                                pe.wait_ge(st_out, g * (NCH - 1) + c)
                                for a in range(TPC):
                                    t = c * TPC + a
                                    last = nc.tensor.matmul(ps[:, 3 + a], CTt[:, t * P:(t + 1) * P], state, start=True, stop=True)
                                last.then_inc(yo_done, 1)
                            if c < NCH - 1:
                                pe.wait_ge(xdec_ready, g * (NCH - 1) + c + 1)
                                if c == 0:
                                    pe.wait_ge(tv, (g + 1) * (GT + 1))
                                    pe.wait_ge(ta, (g + 1) * (GT + 1))
                                for a in range(TPC):
                                    last = nc.tensor.matmul(ps[:, 5], Btok[:, c * TPC + a], xdec[:, a], start=(a == 0), stop=(a == TPC - 1))
                                last.then_inc(st_done, 1)
                            pe.wait_ge(xdt_ready, g * NCH + c + 1)
                            if c:
                                pe.wait_ge(o_out, (g * CPG + c * TPC) * 2)
                            for b in range(NBAT):
                                pe.wait_ge(mt_ready, (g * NCH + c) * NBAT + b + 1)
                                for hh in range(HB):
                                    hd = b * HB + hh
                                    cols = slice(hd * DH, (hd + 1) * DH)
                                    m = mt[b][:, hh]
                                    nc.tensor.matmul(ps[:, 6, cols], m[:, 0:P], xdt[:, 0, cols], start=True, stop=True)
                                    nc.tensor.matmul(ps[:, 7, cols], m[:, P:2 * P], xdt[:, 0, cols], start=True, stop=False)
                                    last = nc.tensor.matmul(ps[:, 7, cols], m[:, 2 * P:3 * P], xdt[:, 1, cols], start=False, stop=True)
                                last.then_inc(yd_done, 1)
                        for a in range(TPC):
                            out_product(NCH - 1, a)
                        pe.wait_ge(o_out, (g + 1) * 2 * CPG)

                @block.gpsimd
                def _(pool):
                    pool.sem_inc(diff, NBAT)
                    with pool.Fori(0, SSM_G) as g:
                        nc.gpsimd.tensor_copy(acg, acs[:, :, bass.ds(g * HPG, HPG)])
                        nc.gpsimd.tensor_copy(normg, par["norm"][:, bass.ds(g * GT, GT)]).then_inc(acg_ready, 1)
                        pool.wait_ge(acg_ready, g + 1)
                        for c in range(NCH):
                            pool.wait_ge(rb_loaded, (g * NCH + c) * 16 + 16)
                            for b in range(NBAT):
                                if c == 0 and b == 2:
                                    pool.wait_ge(cv_ready, (g + 1) * CTG)
                                    pool.wait_ge(turned, g * (GT + 1) + GT)
                                pool.wait_ge(yd_done, (g * NCH + c) * NBAT + b + 1)
                                pool.sem_inc(slot_seen, 1)
                                for hh in range(HB):
                                    hd = b * HB + hh
                                    nc.gpsimd.tensor_scalar(mt[b][:, hh, 0:CHUNK], rbc[:, hd], acg[:, c * TPC, hd:hd + 1], 0.0, ALU.subtract, ALU.min)
                                    last = nc.gpsimd.tensor_scalar(mt[b][:, hh, CHUNK:LC], rbc[:, hd, P:CHUNK], acg[:, c * TPC + 1, hd:hd + 1], 0.0, ALU.subtract, ALU.min)
                                last.then_inc(diff, 1)
                        pool.wait_ge(o_out, (g + 1) * 2 * CPG)

                @block.scalar
                def _(act):
                    with act.Fori(0, SSM_G) as g:
                        def silu(c):
                            dst = BT if c == GT else CTt if c == GT + 1 else cv[:, c % 2]
                            act.wait_ge(convd, g * CTG + c + 1)
                            nc.scalar.activation(dst, cv[:, c % 2], ACT.Silu).then_inc(cv_ready, 1)

                        def turn_evac(c):
                            act.wait_ge(turned, g * (GT + 1) + c + 1)
                            dst = xs[:, 4:8, c * P:(c + 1) * P] if c < GT else Btok[:, 4:8]
                            nc.scalar.copy(dst, ps[:, 5].rearrange("p (t n) -> p t n", n=P)).then_inc(ta, 1)

                        act.wait_ge(zeroed, 1)
                        for c in range(CTG):
                            if c >= 1:
                                silu(c - 1)
                            if c >= 2:
                                turn_evac(c - 2)
                            act.wait_ge(xw_used, g * CTG + c + 3)
                            if c >= 2:
                                act.wait_ge(convd, g * CTG + c - 1)
                            nc.scalar.copy(raw[:, c % 2, SCONV - 1:SCONV - 1 + SEQ], ps[:, (c % 2) * 2:(c % 2) * 2 + 2].rearrange("p a n -> p (a n)")).then_inc(raw_out, 1)
                        silu(CTG - 1)
                        turn_evac(GT)

                        def tail(c, a):
                            t = c * TPC + a
                            act.wait_ge(y1_, g * CPG + t + 1)
                            nc.scalar.activation(zs[:, a], y[:, a], ACT.Square, accum_out=ssq[:, a:a + 1]).then_inc(sq_done, 1)
                            act.wait_ge(sq_done, g * CPG + t + 1)
                            nc.scalar.activation(ssq[:, a:a + 1], ssq[:, a:a + 1], ACT.Sqrt, bias=eps, scale=1.0 / GW).then_inc(rt_done, 1)

                        def evac_gT(c, a):
                            t = c * TPC + a
                            act.wait_ge(acg_ready, g + 1)
                            act.wait_ge(g_turned, g * CPG + t + 1)
                            if t:
                                act.wait_ge(o_used, ((g + 1) * CPG + t) * 2)
                            for k in range(GT):
                                last = nc.scalar.activation(gT[:, k], ps[:, 5, k * P:(k + 1) * P], ACT.Copy, scale=normg[:, k:k + 1])
                            last.then_inc(g_out, 1)

                        def silu_z(c, a):
                            t = c * TPC + a
                            act.wait_ge(z_used, (g + 1) * CPG + t + 1)
                            if t >= TPC:
                                act.wait_ge(y1_, g * CPG + t - TPC + 1)
                            nc.scalar.activation(zs[:, a], ps[:, 1 + a], ACT.Silu).then_inc(z_out, 1)

                        def decays(c, b):
                            act.wait_ge(diff, (g * NCH + c + 1) * NBAT + b + 1)
                            nc.scalar.activation(mt[b], mt[b], ACT.Exp).then_inc(expd, 1)

                        for c in range(NCH):
                            decays(c, 0)
                            silu_z(c, 0)
                            decays(c, 1)
                            decays(c, 2)
                            silu_z(c, 1)
                            if c:
                                evac_gT(c - 1, 0)
                            decays(c, 3)
                            if c:
                                evac_gT(c - 1, 1)
                            for a in range(TPC):
                                tail(c, a)
                        for a in range(TPC):
                            evac_gT(NCH - 1, a)
                        act.wait_ge(o_out, (g + 1) * 2 * CPG)

                @block.vector
                def _(dve):
                    v = nc.vector
                    nc.vector.memset(raw[:, :, 0:SCONV - 1], 0.0).then_inc(zeroed, 1)
                    dve.wait_ge(zeroed, 1)
                    with dve.Fori(0, SSM_G) as g:
                        st = Steps(dve, chain, turn=g, per=CTG * (SCONV - 1) + (NCH - 2) + TPC * (2 + 4 * (NCH - 1)) + 3 * CPG)

                        def turn_evac(c):
                            dve.wait_ge(turned, g * (GT + 1) + c + 1)
                            dst = xs[:, 0:4, c * P:(c + 1) * P] if c < GT else Btok[:, 0:4]
                            v.tensor_copy(dst, ps[:, 4].rearrange("p (t n) -> p t n", n=P)).then_inc(tv, 1)

                        for c in range(CTG):
                            if c >= 2:
                                turn_evac(c - 2)
                            dve.wait_ge(raw_out, g * CTG + c + 1)
                            if c >= 2:
                                dve.wait_ge(cv_ready, g * CTG + c - 1)
                                dve.wait_ge(turned, g * (GT + 1) + c - 1)
                            yv = cv[:, c % 2]
                            for j in range(SCONV):
                                u = raw[:, c % 2, j:j + SEQ]
                                w = cw[:, bass.ds(g * CTG + c, 1), j]
                                if j == 0:
                                    st.link(v.tensor_scalar(yv, u, w, par["conv_b"][:, bass.ds(g * CTG + c, 1)], ALU.mult, ALU.add))
                                elif j < SCONV - 1:
                                    st.link(v.scalar_tensor_tensor(yv, u, w, yv, ALU.mult, ALU.add))
                                else:
                                    v.scalar_tensor_tensor(yv, u, w, yv, ALU.mult, ALU.add).then_inc(convd, 1)
                        turn_evac(GT)
                        dve.wait_ge(tv, (g + 1) * (GT + 1))
                        dve.wait_ge(ta, (g + 1) * (GT + 1))

                        def heads(ap):
                            return ap.rearrange("p (h d) -> p h d", d=DH)

                        def out_add(c, a):
                            t = c * TPC + a
                            for h in range(2):
                                dve.wait_ge(o_used, ((g + 1) * CPG + t) * 2 + h + 1)
                                st.link(v.tensor_tensor(tq, ps[:, 6 + h], gate[:, 0, h * HALF:(h + 1) * HALF], ALU.mult))
                                xt = x[:, t, h * HALF:(h + 1) * HALF]
                                v.tensor_tensor(xt, xt, tq, ALU.add).then_inc(o_out, 1)
                                dve.wait_ge(o_out, (g * CPG + t) * 2 + h + 1)

                        for c in range(NCH):
                            hs = bass.ds(g * HPG, HPG)
                            t0, t1 = c * TPC, (c + 1) * TPC
                            for a in range(TPC):
                                last = v.tensor_tensor(heads(xdt[:, a]), heads(xs[:, t0 + a]), dt[:, t0 + a, hs].unsqueeze(2).to_broadcast([P, HPG, DH]), ALU.mult)
                            last.then_inc(xdt_ready, 1)
                            dve.wait_ge(xdt_ready, g * NCH + c + 1)
                            if c < NCH - 1:
                                for a in range(TPC):
                                    last = v.tensor_tensor(heads(xdec[:, a]), heads(xdt[:, a]), dst[:, t0 + a, hs].unsqueeze(2).to_broadcast([P, HPG, DH]), ALU.mult)
                                last.then_inc(xdec_ready, 1)
                            dve.wait_ge(cb_done, g * NCH + c + 1)
                            at_, n_ = CONST["tri_inc"]
                            v.tensor_tensor(cbt, ps[:, 0, 0:LC], cst[:, at_:at_ + LC], ALU.mult).then_inc(cb_out, 1)
                            dve.wait_ge(cb_out, g * NCH + c + 1)
                            for b in range(NBAT):
                                if c and b >= 2:
                                    out_add(c - 1, b - 2)
                                dve.wait_ge(expd, (g * NCH + c) * NBAT + b + 1)
                                v.tensor_tensor(mt[b], mt[b], bc(cbt, 1, HB), ALU.mult).then_inc(mt_ready, 1)
                            if c:
                                dve.wait_ge(yo_done, g * (NCH - 1) + c)
                                for a in range(TPC):
                                    last = st.did(v.tensor_tensor(heads(y[:, a]), heads(ps[:, 3 + a]), eacs[:, t0 + a, hs].unsqueeze(2).to_broadcast([P, HPG, DH]), ALU.mult))
                            if c < NCH - 1:
                                dve.wait_ge(st_done, g * (NCH - 1) + c + 1)
                                if c == 0:
                                    v.tensor_copy(state, ps[:, 5]).then_inc(st_out, 1)
                                else:
                                    st.link(v.tensor_tensor(heads(state), heads(state), cdec[:, c, hs].unsqueeze(2).to_broadcast([P, HPG, DH]), ALU.mult))
                                    v.tensor_tensor(state, state, ps[:, 5], ALU.add).then_inc(st_out, 1)
                                dve.wait_ge(st_out, g * (NCH - 1) + c + 1)
                            dve.wait_ge(yd_done, (g * NCH + c + 2) * NBAT)
                            for a in range(TPC):
                                t = t0 + a
                                st.link(v.tensor_tensor(heads(tq), heads(xs[:, t]), bc(row["ssm_d"][:, hs], 2, DH), ALU.mult))
                                if c:
                                    st.link(v.tensor_tensor(y[:, a], y[:, a], ps[:, 6 + a], ALU.add))
                                    st.link(v.tensor_tensor(y[:, a], y[:, a], tq, ALU.add))
                                else:
                                    st.link(v.tensor_tensor(y[:, a], tq, ps[:, 6 + a], ALU.add))
                                dve.wait_ge(z_out, g * CPG + t + 1)
                                v.tensor_tensor(y[:, a], y[:, a], zs[:, a], ALU.mult).then_inc(y1_, 1)
                            for a in range(TPC):
                                t = t0 + a
                                dve.wait_ge(rt_done, g * CPG + t + 1)
                                st.link(v.reciprocal(ssq[:, a:a + 1], ssq[:, a:a + 1]))
                                v.tensor_scalar(y[:, a], y[:, a], ssq[:, a:a + 1], None, ALU.mult).then_inc(y2_, 1)
                        for a in range(TPC):
                            out_add(NCH - 1, a)
                        st.end()


        for layer in range(DEPTH):
            if f"ada{layer}" in stages:
                ada_phase(layer)
            if f"mix{layer}" in stages:
                norm_phase(layer, 0, False)
                (hybrid_phase if layer % 2 == 0 else ssm_phase)(layer)
                clear_sems()
            if f"moe{layer}" in stages:
                norm_phase(layer, 1, True)
                moe_phase(layer, layer == DEPTH - 1)
                if layer < DEPTH - 1:
                    clear_sems()
        if "dump" in stages:
            o_stored = sem("dumped")
            with nc.Block() as block:
                @block.sync
                def _(sp):
                    sp.dma_start(out[0].rearrange("(t p) d -> p t d", p=P), x[:, :, :]).then_inc(o_stored, 16)
                    sp.wait_ge(o_stored, 16)


STAGES = ("ada0", "mix0", "moe0", "ada1", "mix1", "moe1")


def kernel(**inputs):
    import numpy as np
    import concourse.bacc as bacc
    from concourse import mybir as mb
    from concourse.bass_utils import run_bass_kernel_spmd as run

    a = {k: np.asarray(v) for k, v in inputs.items()}
    f = np.float32
    p = np.arange(P)
    parts = {
        "ident": np.eye(P, dtype=f),
        "tri_strict": (p[:, None] < p[None]).astype(f),
        "tri_inc": (p[:, None] <= p[None]).astype(f),
        "ones": np.ones((P, P), f),
        "tri_inc2": (p[:, None] <= p[None]).astype(f),
        "maskneg": np.where(p[:, None] >= p[None], 0.0, NEG).astype(f),
        "before4": np.broadcast_to((np.arange(J)[None] < np.arange(J)[:, None]).astype(f).reshape(1, -1), (P, J * J)),
        "group_key": np.broadcast_to((G - np.arange(G)).astype(f)[None], (P, G)),
        "step128": np.broadcast_to((P * np.arange(NT)).astype(f)[None], (P, NT)),
        "before16": np.broadcast_to((np.arange(E)[None] < np.arange(E)[:, None]).astype(f).reshape(1, -1), (P, E * E)),
        "chunk_end": np.broadcast_to((P * (1 + np.arange(SLOTS))).astype(f)[None], (P, SLOTS)),
        "iota_chunk": np.broadcast_to(np.arange(SLOTS).astype(f)[None], (P, SLOTS)),
        "iota128": np.broadcast_to(p.astype(f)[None], (P, P)),
        "token_id": (p[:, None] + P * np.arange(NT)[None]).astype(f),
        "eps": np.full((P, 1), EPS, f),
    }
    arrays = {}
    arrays["consts"] = np.concatenate([parts[n] for n in CONST], axis=1)

    def cols(v):
        return v.reshape(-1, P).T

    arrays["pcols"] = np.stack([np.concatenate([cols(a["c"][0]), cols(a["ada_b"][l]), cols(a["norm_mix"][l]), cols(a["norm_ffn"][l])], axis=1)
                                for l in range(DEPTH)], axis=1)
    arrays["mix0"] = np.concatenate([np.tile(a["hy_q_norm"][0], 2)[:, None], np.tile(a["hy_k_norm"][0], 2)[:, None],
                                     cols(a["hy_dw_b"][0]), cols(a["hy_ln_g"][0]), cols(a["hy_ln_b"][0]),
                                     a["hy_dw_w"][0].reshape(CONV_W, CT, P).transpose(2, 1, 0).reshape(P, -1)], axis=1)
    order = [i for g in range(SSM_G) for i in [*range(g * GW // P, (g + 1) * GW // P), SSM_INNER // P + g, SSM_INNER // P + SSM_G + g]]
    arrays["mix1"] = np.concatenate([cols(a["ssm_conv_b"][0])[:, order], cols(a["ssm_norm"][0]),
                                     a["ssm_conv_w"][0].reshape(SCONV, XBC_T, P).transpose(2, 1, 0)[:, order].reshape(P, -1)], axis=1)
    arrays["rows"] = np.broadcast_to(np.concatenate([a["router_bias"], a["ssm_dt_bias"][0], a["ssm_a_log"][0], a["ssm_d"][0]])[None], (P, NROWS))
    ab = a["ada_b"].reshape(DEPTH, N_MOD, D)[:, [2, 5]]
    arrays["gate_bias"] = np.broadcast_to(ab[:, None], (DEPTH, P, 2, D))
    arrays["x"] = a["x"][0]
    arrays["router_w"] = a["router_w"]

    def tiled(w, n):
        k, m = w.shape
        return w.reshape(k // P, P, m // n, n).transpose(2, 1, 0, 3).reshape(m // n, P, -1)

    arrays["ada_w"] = np.stack([tiled(a["ada_w"][l], D) for l in range(DEPTH)])
    ex = np.empty((DEPTH * E * 6, P, KD * FF // 2), f)
    pieces = ex.reshape(DEPTH, E, 6, P, -1)
    for q, key in enumerate(("exp_w_gate", "exp_w_up")):
        w = a[key].reshape(DEPTH, E, KD, P, 2, FF // 2).transpose(0, 1, 4, 3, 2, 5).reshape(DEPTH, E, 2, P, -1)
        pieces[:, :, q], pieces[:, :, 2 + q] = w[:, :, 0], w[:, :, 1]
    pieces[:, :, 4:] = a["exp_w_down"].reshape(DEPTH, E, 2, FT // 2, P, D).transpose(0, 1, 2, 4, 3, 5).reshape(DEPTH, E, 2, P, -1)
    arrays["experts"] = ex
    w = a["hy_w_in"][0]
    u = w[:, 3 * ATT_W:].reshape(D, 2, CT, P).transpose(0, 2, 1, 3).reshape(D, -1)
    arrays["hy_in"] = tiled(np.concatenate([u, w[:, :3 * ATT_W]], axis=1), 2 * P)
    arrays["hy_out"] = tiled(a["hy_w_out"][0], D)[0]
    w = a["ssm_w_in"][0]
    arrays["ssm_z"] = tiled(w[:, :SSM_INNER], GW)
    arrays["ssm_xbc"] = tiled(w[:, SSM_INNER:SSM_INNER + XBC_T * P], P)[order]
    arrays["ssm_dt"] = tiled(w[:, SSM_INNER + XBC_T * P:], SSM_HEADS)[0]
    arrays["ssm_out"] = a["ssm_w_out"][0].reshape(SSM_G, GW // P, P, D).transpose(0, 2, 1, 3).reshape(SSM_G, P, -1)
    nc = bacc.Bacc("TRN2", target_bir_lowering=False, num_devices=1)
    arrays = {f"in_{k}": np.ascontiguousarray(v) for k, v in arrays.items()}
    ins = {k[3:]: nc.dram_tensor(k, v.shape, mb.dt.from_np(v.dtype), kind="ExternalInput").ap() for k, v in arrays.items()}
    out = nc.dram_tensor("out_0", (1, SEQ, D), mb.dt.float32, kind="ExternalOutput").ap()
    build(nc, ins, out, STAGES)
    return run(nc, [arrays], core_ids=[0]).results[0]["out_0"]
```

```python
import concourse.bass as bass
from concourse import mybir
from contextlib import ExitStack

P = 128
SEQ = 1024
D = 1024
DEPTH = 2
NT = SEQ // P
KD = D // P
HALF = 512
N_MOD = 6
EPS = 1e-6
HEADS = 8
HD = 64
ATT_W = HEADS * HD
PAIRS = ATT_W // P
CONV_CH = D // 2
CT = CONV_CH // P
CONV_W = 31
NEG = -1e30
SSM_INNER = 2 * D
SSM_HEADS = 32
SSM_HEAD_DIM = SSM_INNER // SSM_HEADS
SSM_G = 4
HPG = SSM_HEADS // SSM_G
GW = SSM_INNER // SSM_G
NST = 128
SCONV = 4
CHUNK = 256
NCH = SEQ // CHUNK
E = 16
G = 4
J = E // G
FF = 512
FT = FF // P
TOPK = 2
SLOTS = (SEQ * TOPK) // P + E

CONST = {}
_at = 0
for _name, _n in (("ident", P), ("tri_strict", P), ("tri_inc", P), ("ones", P), ("tri_inc2", P), ("maskneg", P),
                  ("before4", J * J), ("group_key", G), ("step128", NT), ("before16", E * E),
                  ("chunk_end", SLOTS), ("iota_chunk", SLOTS), ("iota128", P), ("token_id", NT),
                  ("eps", 1)):
    CONST[_name] = (_at, _n)
    _at += _n
NCONST = _at
PCOL = {}
_at = 0
for _name, _n in (("c", KD), ("ada_b", N_MOD * KD), ("norm0", KD), ("norm1", KD)):
    PCOL[_name] = (_at, _n)
    _at += _n
NPCOL = _at
MIX0 = {"gq": (0, 1), "gk": (1, 1), "dw_b": (2, CT), "ln_g": (2 + CT, CT), "ln_b": (2 + 2 * CT, CT),
        "dw_w": (2 + 3 * CT, CT * CONV_W)}
NMIX0 = 2 + 3 * CT + CT * CONV_W
XBC_T = (SSM_INNER + 2 * SSM_G * NST) // P
MIX1 = {"conv_b": (0, XBC_T), "norm": (XBC_T, SSM_INNER // P),
        "conv_w": (XBC_T + SSM_INNER // P, XBC_T * SCONV)}
NMIX1 = XBC_T + SSM_INNER // P + XBC_T * SCONV
ROWS = {"rbias": (0, E), "dt_bias": (E, SSM_HEADS), "a_log": (E + SSM_HEADS, SSM_HEADS),
        "ssm_d": (E + 2 * SSM_HEADS, SSM_HEADS)}
NROWS = E + 3 * SSM_HEADS


def bc(ap, axis, n):
    ap = ap.unsqueeze(axis)
    shape = list(ap.shape)
    shape[axis] = n
    return ap.to_broadcast(shape)


class Steps:

    def __init__(self, eng, sem, base=0, turn=None, per=0):
        self.eng, self.sem, self.n, self.base, self.turn, self.per = eng, sem, 0, base, turn, per

    def did(self, ins):
        ins.then_inc(self.sem, 1)
        self.n += 1
        return ins

    def wait(self):
        at = self.base + self.n
        self.eng.wait_ge(self.sem, at if self.turn is None else self.turn * self.per + at)

    def link(self, ins):
        self.did(ins)
        self.wait()

    def end(self):
        assert self.turn is None or self.n == self.per, (self.n, self.per)


def build(nc, ins, out):
    f32 = mybir.dt.float32
    f32r = mybir.dt.float32r
    i32 = mybir.dt.int32
    u32 = mybir.dt.uint32
    ALU = mybir.AluOpType
    ACT = mybir.ActivationFunctionType
    X = mybir.AxisListType.X
    ctx = ExitStack()
    uid = [0]
    live = []

    def sb(name, shape, dt=f32):
        return ctx.enter_context(nc.sbuf_tensor(name, shape, dt))

    def sem(name):
        uid[0] += 1
        live.append(nc.alloc_semaphore(name=f"{name}_{uid[0]}"))
        return live[-1]

    def clear_sems():
        nc.clear_and_free_semaphores(live[:])
        live.clear()
        nc.all_engine_barrier()

    with ctx:
        ctx.enter_context(nc.allow_non_contiguous_dma(reason="parameter columns"))
        x_base = -(-nc.sbuf_base // 32) * 32
        x = sb("x", [P, NT, D])
        cst = sb("cst", [P, NCONST])
        pcol = sb("pcol", [P, DEPTH, NPCOL])
        mix0 = sb("mix0", [P, NMIX0])
        mix1 = sb("mix1", [P, NMIX1])
        rows = sb("rows", [P, NROWS])
        gate = sb("gate", [P, 2, D])
        modc = sb("modc", [P, DEPTH, 2, 2, KD])
        small = sb("small", [P, 256])
        WORK, HTW = 32640, KD * SEQ
        base_ = -(-nc.sbuf_base // 32) * 32
        work = sb("work", [P, WORK + HTW])
        hT = work[:, WORK:WORK + HTW].rearrange("p (k n) -> p k n", n=SEQ)
        ps = ctx.enter_context(nc.psum_tensor("ps", [P, 8, HALF], f32))
        hrows = nc.dram_tensor("hrows", [SEQ, D], f32, kind="Internal").ap()
        yrows = nc.dram_tensor("yrows", [(SLOTS + NT) * P, D], f32, kind="Internal").ap()
        ada_sums = nc.dram_tensor("ada_sums", [2 * N_MOD, P, HALF], f32, kind="Internal").ap()
        sums_loaded = nc.alloc_semaphore(name="ada_sums_loaded")
        y_filled = nc.alloc_semaphore(name="y_rows_filled")
        acs_rows = nc.dram_tensor("acs_rows", [SSM_HEADS, SEQ], f32, kind="Internal").ap()

        def const(name):
            at, n = CONST[name]
            return cst[:, at:at + n]

        def place(name, at, shape, dtype):
            n = 1
            for s in shape:
                n *= s
            assert at + n <= WORK + HTW, (at, n)
            uid[0] += 1
            t = nc.alloc_sbuf_tensor_at(f"{name}_{uid[0]}", [P, *shape], dtype, offset=base_ + 4 * at)
            return t[(slice(None),) * (1 + len(shape))], at + n

        def view(at, shape, limit=WORK):
            n = 1
            for s in shape:
                n *= s
            assert at + n <= limit, (at, n)
            v = work[:, at:at + n]
            if len(shape) == 2:
                v = v.rearrange("p (a b) -> p a b", b=shape[1])
            elif len(shape) == 3:
                v = v.rearrange("p (a b c) -> p a b c", b=shape[1], c=shape[2])
            return v, at + n

        ident, ones = const("ident"), const("ones")
        eps = const("eps")

        def three_passes(out_, lh, ll, rh, rl, start, stop):
            nc.tensor.matmul(out_, lh, rl, start=start, stop=False)
            nc.tensor.matmul(out_, ll, rh, start=False, stop=False)
            return nc.tensor.matmul(out_, lh, rh, start=False, stop=stop)

        with nc.Block() as block:
            s_in = sem("inputs_loaded")
            s_x = sem("x_loaded")

            @block.sync
            def _(sp):
                sp.dma_start(cst[:, :], ins["consts"]).then_inc(s_in, 16)
                sp.dma_start(pcol[:, :, :], ins["pcols"]).then_inc(s_in, 16)
                sp.dma_start(mix0[:, :], ins["mix0"]).then_inc(s_in, 16)
                sp.dma_start(mix1[:, :], ins["mix1"]).then_inc(s_in, 16)
                sp.dma_start(rows[:, :], ins["rows"]).then_inc(s_in, 16)
                sp.wait_ge(s_in, 80)

            @block.scalar
            def _(act):
                act.wait_ge(s_in, 80)
                nc.scalar.activation(pcol[:, 0, 0:KD], pcol[:, 0, 0:KD], ACT.Silu)

        def modulation(dve, layer, bias_loaded, chain, steps):
            dve.wait_ge(bias_loaded, 16)
            ab = pcol[:, layer, PCOL["ada_b"][0]:PCOL["ada_b"][0] + N_MOD * KD].rearrange("p (h q k) -> p h q k", h=2, q=3)
            sums = ps[:, 0, 0:2 * 2 * KD].rearrange("p (h q k) -> p h q k", h=2, q=2)
            st = Steps(dve, chain, base=steps)
            st.did(nc.vector.tensor_tensor(modc[:, layer], sums, ab[:, :, 0:2], ALU.add))
            nc.vector.tensor_tensor(gate[:, :, :], ps[:, 1:5, :].rearrange("p (h a) n -> p h (a n)", h=2), gate[:, :, :], ALU.add)
            st.wait()
            nrm = pcol[:, layer, PCOL["norm0"][0]:PCOL["norm0"][0] + 2 * KD].rearrange("p (h k) -> p h k", h=2)
            for h in range(2):
                nc.vector.scalar_tensor_tensor(modc[:, layer, h, 1], modc[:, layer, h, 1], 1.0, nrm[:, h], ALU.add, ALU.mult)

        def ada_acc():
            return view(3 * NT // 2 * D, (2 * N_MOD, HALF))[0]

        def ada_from_sums(layer):
            acc = ada_acc()
            bias_loaded = sem("gate_bias_loaded")
            summed, chain = sem("ada_summed"), sem("ada_chain")
            with nc.Block() as block:
                @block.sync
                def _(sp):
                    sp.dma_start(gate[:, :, :], ins["gate_bias"][layer]).then_inc(bias_loaded, 16)

                @block.tensor
                def _(pe):
                    pe.wait_ge(sums_loaded, 16)
                    for i in range(2):
                        for h in range(2):
                            nc.tensor.matmul(ps[:, i * 2 + 1 + h], ones, acc[:, (i * 3 + 2) * 2 + h], start=True, stop=True)
                        for q in range(2):
                            for k in range(KD):
                                src = acc[:, (i * 3 + q) * 2 + k // 4, (k % 4) * P:(k % 4 + 1) * P]
                                last = nc.tensor.matmul(ps[:, 0, (i * 2 + q) * KD + k:(i * 2 + q) * KD + k + 1], src, ones[:, 0:1], start=True, stop=True)
                    last.then_inc(summed, 1)

                @block.vector
                def _(dve):
                    dve.wait_ge(summed, 1)
                    modulation(dve, layer, bias_loaded, chain, 0)

        def ada_phase(layer):
            wv, at = view(0, (3, KD, D))
            acc = hT[:, 0:3, :]
            w_src = ins["ada_w0"].rearrange("c p (k n) -> c p k n", n=D)
            loaded = [sem(f"ada_w_loaded{q}") for q in range(3)]
            bias_loaded = sem("gate_bias_loaded")
            acc_ready = sem("ada_acc_ready")
            summed = sem("ada_summed")
            chain = sem("ada_chain")
            with nc.Block() as block:
                @block.sync
                def _(sp):
                    sp.dma_start(gate[:, :, :], ins["gate_bias"][layer]).then_inc(bias_loaded, 16)
                    with sp.Fori(0, 2) as i:
                        for q in range(3):
                            sp.wait_ge(acc_ready, i * 3 + q + 1)
                            sp.dma_start(wv[:, q], w_src[bass.ds(i * 3 + q, 1)].rearrange("c p k n -> p (c k) n")).then_inc(loaded[q], 16)
                    if layer == 0:
                        sp.dma_start(x[:, :, :], ins["x"].rearrange("(t p) d -> p t d", p=P)).then_inc(s_x, 16)
                        sp.wait_ge(s_x, 16)

                @block.vector
                def _(dve):
                    dve.sem_inc(acc_ready, 3)
                    with dve.Fori(0, 2) as i:
                        st = Steps(dve, chain, turn=i, per=3 * (KD - 1))
                        for q in range(3):
                            dve.wait_ge(loaded[q], i * 16 + 16)
                            dve.wait_ge(summed, i * 3 + 3)
                            for k in range(KD):
                                ck = pcol[:, 0, k:k + 1]
                                if k == 0:
                                    op = nc.vector.tensor_scalar(acc[:, q], wv[:, q, k], ck, None, ALU.mult)
                                else:
                                    st.wait()
                                    op = nc.vector.scalar_tensor_tensor(acc[:, q], wv[:, q, k], ck, acc[:, q], ALU.mult, ALU.add)
                                if k < KD - 1:
                                    st.did(op)
                                else:
                                    op.then_inc(acc_ready, 1)
                        st.end()
                    dve.wait_ge(summed, 9)
                    modulation(dve, layer, bias_loaded, chain, 2 * 3 * (KD - 1))

                @block.tensor
                def _(pe):
                    pe.sem_inc(summed, 3)
                    with pe.Fori(0, 2) as i:
                        for q in range(3):
                            pe.wait_ge(acc_ready, i * 3 + q + 4)
                            if q == 2:
                                for h in range(2):
                                    last = nc.tensor.matmul(ps[:, bass.ds(i * 2 + 1 + h, 1), :].rearrange("p a n -> p (a n)"), ones, acc[:, q, h * HALF:(h + 1) * HALF], start=True, stop=True)
                            else:
                                for k in range(KD):
                                    last = nc.tensor.matmul(ps[:, 0, bass.ds((i * 2 + q) * KD + k, 1)], acc[:, q, k * P:(k + 1) * P], ones[:, 0:1], start=True, stop=True)
                            last.then_inc(summed, 1)

        def norm_phase(layer, sub, rows_out):
            xn, at = view(0, (4, D))
            junk, at = view(at, (D,))
            junk2, at = view(at, (D,))
            NSQ = 5
            squares, squares_dve, sq_chain = sem("squares_summed"), sem("squares_by_vector"), sem("square_chain")
            xn_seen = sem("xn_slots_seen")
            rms = sem("rms_ready")
            rstd_ready = sem("rstd_ready")
            xn_ready = sem("xn_ready")
            turned = sem("transposed")
            by_act = sem("evacuated_by_scalar")
            by_dve = sem("evacuated_by_vector")
            stored = sem("rows_stored")
            ss, rstd = small[:, 0:NT], small[:, NT:2 * NT]
            shift, scale = modc[:, layer, sub, 0], modc[:, layer, sub, 1]
            with nc.Block() as block:
                @block.scalar
                def _(act):
                    act.sem_inc(by_act, 2)
                    act.sem_inc(squares, 1)
                    with act.Fori(0, NSQ) as t:
                        act.wait_ge(squares, t + 1)
                        nc.scalar.activation(junk, x[:, bass.ds(t, 1), :].rearrange("p a d -> p (a d)"), ACT.Square, accum_out=ss[:, bass.ds(t, 1)]).then_inc(squares, 1)
                    act.wait_ge(squares, NSQ + 1)
                    act.wait_ge(squares_dve, NT - NSQ)
                    nc.scalar.activation(rstd, ss, ACT.Sqrt, bias=eps, scale=1.0 / D).then_inc(rms, 1)
                    act.wait_ge(rstd_ready, 1)
                    with act.Fori(0, 2) as h:
                        act.wait_ge(turned, h * KD + KD)
                        if rows_out:
                            act.wait_ge(stored, h * 16 + 16)
                        act.sem_inc(xn_seen, 1)
                        for u in range(2):
                            nc.scalar.activation(xn[:, u], x[:, bass.ds(h * 4 + u, 1), :].rearrange("p a d -> p (a d)"), ACT.Copy, scale=rstd[:, bass.ds(h * 4 + u, 1)]).then_inc(xn_ready, 1)
                        for d in range(0, KD, 2):
                            act.wait_ge(turned, h * KD + d + KD + 1)
                            nc.scalar.activation(hT[:, d, bass.ds(h * HALF, HALF)], ps[:, d % 4], ACT.Identity, bias=shift[:, d:d + 1], scale=scale[:, d:d + 1]).then_inc(by_act, 1)

                @block.vector
                def _(dve):
                    dve.sem_inc(by_dve, 2)
                    st = Steps(dve, sq_chain)
                    for t in range(NSQ, NT):
                        st.link(nc.vector.tensor_tensor(junk2, x[:, t], x[:, t], ALU.mult))
                        nc.vector.tensor_reduce(ss[:, t:t + 1], junk2, X, ALU.add).then_inc(squares_dve, 1)
                        dve.wait_ge(squares_dve, t - NSQ + 1)
                    dve.wait_ge(rms, 1)
                    nc.vector.reciprocal(rstd, rstd).then_inc(rstd_ready, 1)
                    dve.wait_ge(rstd_ready, 1)
                    with dve.Fori(0, 2) as h:
                        dve.wait_ge(turned, h * KD + KD)
                        if rows_out:
                            dve.wait_ge(stored, h * 16 + 16)
                        for u in range(2, 4):
                            nc.vector.tensor_scalar(xn[:, u], x[:, bass.ds(h * 4 + u, 1), :].rearrange("p a d -> p (a d)"), rstd[:, bass.ds(h * 4 + u, 1)], None, ALU.mult).then_inc(xn_ready, 1)
                        for d in range(1, KD, 2):
                            dve.wait_ge(turned, h * KD + d + KD + 1)
                            nc.vector.tensor_scalar(hT[:, d, bass.ds(h * HALF, HALF)], ps[:, d % 4], scale[:, d:d + 1], shift[:, d:d + 1], ALU.mult, ALU.add).then_inc(by_dve, 1)

                @block.tensor
                def _(pe):
                    pe.sem_inc(turned, KD)
                    with pe.Fori(0, 2) as h:
                        pe.wait_ge(xn_ready, h * 4 + 4)
                        for d in range(KD):
                            pe.wait_ge(by_dve if d % 2 else by_act, h * 4 + d // 2 + 1)
                            for u in range(4):
                                last = nc.tensor.transpose(ps[:, d % 4, u * P:(u + 1) * P], xn[:, u, d * P:(d + 1) * P], ident)
                            last.then_inc(turned, 1)

                if layer == 0 and sub == 0:
                    @block.gpsimd
                    def _(pool):
                        for c in range(SEQ * TOPK // P, SLOTS, NT):
                            pool.dma_start(yrows[c * P:(c + NT) * P, :], ins["x"]).then_inc(y_filled, 16)

                if rows_out:
                    @block.sync
                    def _(sp):
                        sp.sem_inc(stored, 16)
                        with sp.Fori(0, 2) as h:
                            sp.wait_ge(xn_ready, h * 4 + 4)
                            sp.dma_start(hrows[bass.ds(h * HALF, HALF), :].rearrange("(u p) d -> p u d", p=P), xn).then_inc(stored, 16)
                        sp.wait_ge(stored, 48)

        def moe_phase(layer, last_layer):
            sub = 1
            rw, at = view(0, (KD, E))
            score, at = view(at, (NT, E))
            aff, at = view(at, (NT, E))
            cmpa, at = view(at, (NT * G, J, J))
            cmpb, at = view(at, (NT * G, J, J))
            rank, at = view(at, (NT * G, J))
            sel, at = view(at, (NT * G, J))
            gs, at = view(at, (NT, G))
            gsel, at = view(at, (NT, G))
            gmax, at = view(at, (NT,))
            oh, at = view(at, (2, NT, E))
            both, at = view(at, (NT, E))
            off, at = view(at, (NT + 1, E))
            pos, at = view(at, (NT, E))
            nch_c, at = view(at, (E, NT))
            nch, at = view(at, (E,))
            st16, at = view(at, (E, E))
            first, at = view(at, (E,))
            prod, at = view(at, (2, NT, E))
            dest, at = view(at, (2 * NT,))
            ge, at = view(at, (2 * NT, SLOTS))
            hi, at = view(at, (2 * NT,))
            lo, at = view(at, (2 * NT,))
            tv, at = view(at, (2 * NT, SLOTS))
            oh_lo, at = view(at, (2 * NT, P))
            wsel = small[:, 16:32]
            dest_i = small[:, 32:48].bitcast(u32)
            slot_i = small[:, 48:48 + SLOTS + NT + 1].bitcast(u32)
            nch_i = small[:, 96:96 + E].bitcast(i32)
            first_i = small[:, 96 + E:96 + 2 * E].bitcast(i32)
            wsum = small[:, 130:138]
            rw_loaded = sem("router_w_loaded")
            logits = sem("router_logits")
            affs = sem("affinities")
            routed = sem("routed")
            counted = sem("counted")
            placed = sem("slots_placed")
            tabled = sem("slot_table")
            chain = sem("route_chain")
            with nc.Block() as block:
                @block.sync
                def _(sp):
                    sp.dma_start(rw, ins["router_w"].rearrange("(k p) e -> p k e", p=P)).then_inc(rw_loaded, 16)

                @block.tensor
                def _(pe):
                    pe.wait_ge(rw_loaded, 16)
                    for t in range(NT):
                        for k in range(KD):
                            last = nc.tensor.matmul(ps[:, 0, t * E:(t + 1) * E], hT[:, k, t * P:(t + 1) * P], rw[:, k], start=(k == 0), stop=(k == KD - 1))
                    last.then_inc(logits, 1)
                    pe.wait_ge(routed, 1)
                    bf = both.rearrange("p t e -> p (t e)")
                    nc.tensor.matmul(ps[:, 1, 0:P], const("tri_strict"), bf, start=True, stop=True)
                    nc.tensor.matmul(ps[:, 2, 0:P], ones, bf, start=True, stop=True).then_inc(counted, 1)
                    pe.wait_ge(placed, 1)
                    for n in range(2 * NT):
                        last = nc.tensor.matmul(ps[:, 3, 0:SLOTS], oh_lo[:, n], tv[:, n], start=(n == 0), stop=(n == 2 * NT - 1))
                    last.then_inc(tabled, 1)

                @block.scalar
                def _(act):
                    act.wait_ge(logits, 1)
                    nc.scalar.activation(aff.rearrange("p t e -> p (t e)"), ps[:, 0, 0:NT * E], ACT.Sigmoid).then_inc(affs, 1)

                @block.vector
                def _(dve):
                    v = nc.vector
                    st = Steps(dve, chain)
                    dve.wait_ge(affs, 1)
                    st.link(v.tensor_tensor(score, aff, bc(rows[:, 0:E], 1, NT), ALU.add))
                    sg = score.rearrange("p t (g j) -> p (t g) j", g=G)
                    st.did(v.tensor_tensor(cmpa, bc(sg, 2, J), bc(sg, 3, J), ALU.is_gt))
                    st.link(v.tensor_tensor(cmpb, bc(sg, 2, J), bc(sg, 3, J), ALU.is_equal))
                    st.link(v.tensor_tensor(cmpb, cmpb, bc(const("before4").rearrange("p (a b) -> p a b", b=J), 1, NT * G), ALU.mult))
                    st.link(v.tensor_tensor(cmpa, cmpa, cmpb, ALU.add))
                    st.link(v.tensor_reduce(rank, cmpa, X, ALU.add))
                    st.link(v.scalar_tensor_tensor(sel, rank, float(TOPK), sg, ALU.is_lt, ALU.mult))
                    st.link(v.tensor_reduce(gs, sel.rearrange("p (t g) j -> p t g j", g=G), X, ALU.add))
                    st.link(v.tensor_reduce(gmax, gs, X, ALU.max))
                    st.link(v.tensor_tensor(gsel, gs, bc(gmax, 2, G), ALU.is_equal))
                    gk = bc(const("group_key"), 1, NT)
                    st.link(v.tensor_tensor(gsel, gsel, gk, ALU.mult))
                    st.link(v.tensor_reduce(gmax, gsel, X, ALU.max))
                    st.link(v.tensor_tensor(gsel, gk, bc(gmax, 2, G), ALU.is_equal))
                    gflat = bc(gsel.rearrange("p t g -> p (t g)"), 2, J)
                    for k in range(2):
                        st.did(v.scalar_tensor_tensor(oh[:, k].rearrange("p t (g j) -> p (t g) j", g=G), rank, float(k), gflat, ALU.is_equal, ALU.mult))
                    st.wait()
                    v.tensor_tensor(both, oh[:, 0], oh[:, 1], ALU.add).then_inc(routed, 1)
                    st.link(v.tensor_tensor(prod, oh, bc(aff, 1, 2), ALU.mult))
                    w2 = wsel.rearrange("p (k t) -> p k t", k=2)
                    st.link(v.tensor_reduce(w2, prod, X, ALU.add))
                    st.link(v.tensor_tensor(wsum, w2[:, 0], w2[:, 1], ALU.add))
                    st.link(v.reciprocal(wsum, wsum))
                    st.link(v.tensor_tensor(w2, w2, bc(wsum, 1, 2), ALU.mult))
                    dve.wait_ge(counted, 1)
                    tot = ps[:, 2, 0:P].rearrange("p (t e) -> p t e", e=E)
                    st.link(v.memset(off[:, 0], 0.0))
                    for t in range(NT):
                        st.link(v.tensor_tensor(off[:, t + 1], tot[:, t], off[:, t], ALU.add))
                    st.link(v.tensor_tensor(nch_c, bc(off[:, NT], 2, NT), bc(const("step128"), 1, E), ALU.is_gt))
                    st.link(v.tensor_reduce(nch, nch_c, X, ALU.add))
                    st.link(v.tensor_scalar(nch, nch, 1.0, None, ALU.max))
                    st.link(v.tensor_tensor(st16, const("before16").rearrange("p (a b) -> p a b", b=E), bc(nch, 1, E), ALU.mult))
                    st.link(v.tensor_reduce(first, st16, X, ALU.add))
                    st.link(v.tensor_tensor(pos, ps[:, 1, 0:P].rearrange("p (t e) -> p t e", e=E), off[:, 0:NT], ALU.add))
                    st.link(v.scalar_tensor_tensor(pos, bc(first, 1, NT), float(P), pos, ALU.mult, ALU.add))
                    st.link(v.tensor_tensor(prod, oh, bc(pos, 1, 2), ALU.mult))
                    st.link(v.tensor_reduce(dest.rearrange("p (k t) -> p k t", k=2), prod, X, ALU.add))
                    st.did(v.tensor_copy(dest_i, dest))
                    st.link(v.tensor_tensor(ge, bc(dest, 2, SLOTS), bc(const("chunk_end"), 1, 2 * NT), ALU.is_ge))
                    st.link(v.tensor_reduce(hi, ge, X, ALU.add))
                    st.link(v.scalar_tensor_tensor(lo, hi, -float(P), dest, ALU.mult, ALU.add))
                    st.did(v.tensor_tensor(tv, bc(hi, 2, SLOTS), bc(const("iota_chunk"), 1, 2 * NT), ALU.is_equal))
                    st.link(v.tensor_tensor(oh_lo, bc(lo, 2, P), bc(const("iota128"), 1, 2 * NT), ALU.is_equal))
                    tid = bc(bc(const("token_id"), 1, 2), 3, SLOTS)
                    v.tensor_tensor(tv.rearrange("p (k t) c -> p k t c", k=2), tv.rearrange("p (k t) c -> p k t c", k=2), tid, ALU.mult).then_inc(placed, 1)
                    st.did(v.tensor_copy(nch_i, nch))
                    st.did(v.tensor_copy(first_i, first))
                    st.did(v.memset(slot_i[:, SLOTS:SLOTS + NT + 1], 0))
                    dve.wait_ge(tabled, 1)
                    st.did(v.tensor_copy(slot_i[:, 0:SLOTS], ps[:, 3, 0:SLOTS]))

            FH = FF // 2
            PW = KD * FH
            NP, NR = 6, 4
            slot = [0, 1, 2, 3, 1, 2]
            ALL = WORK + HTW
            whi, at = place("w_high", 0, (NP, PW), f32r)
            wlo, at = place("w_low", at, (NP, PW), f32r)
            xhi, at = place("x_high", at, (KD, P), f32r)
            xlo, at = place("x_low", at, (KD, P), f32r)
            ahi, at = place("hidden_high", at, (FT, P), f32r)
            alo, at = place("hidden_low", at, (FT, P), f32r)
            raw, at = place("w_raw", at, (NR, PW), f32)
            xg, at = view(at, (D,), ALL)
            h32, at = place("x_gathered", at, (KD, P), f32)
            sg_, at = view(at, (2, FH), ALL)
            a_, at = view(at, (2, FH), ALL)
            ysb, at = view(at, (D,), ALL)
            idx = small[:, 140:141].bitcast(u32)
            shift, scale = modc[:, layer, sub, 0], modc[:, layer, sub, 1]
            loaded = [sem(f"piece_loaded{q}") for q in range(NR)]
            hi_done, hi_first, hi_last = sem("piece_hi"), sem("first_piece_hi"), sem("last_piece_hi")
            lo_done, lo_pool = sem("piece_lo"), sem("first_piece_lo")
            NV = NP - 1
            gd, ud = [sem("gate0_done"), sem("gate1_done")], [sem("up0_done"), sem("up1_done")]
            d_done = sem("down_done")
            idx_ready, idx_seen, gathered = sem("index_ready"), sem("index_seen"), sem("gathered")
            rows_seen, y_free = sem("rows_seen"), sem("y_rows_free")
            turned = sem("gathered_transposed")
            h_act, h_dve = sem("h_by_scalar"), sem("h_by_vector")
            xhi_ready, xlo_ready = sem("x_hi_ready"), sem("x_lo_ready")
            silu_done, a_ready = sem("silu_done"), sem("hidden_ready")
            ta = [sem("hidden0_transposed"), sem("hidden1_transposed")]
            ahi_ready, alo_ready = sem("hidden_hi_ready"), sem("hidden_lo_ready")
            y_act, y_dve, y_stored = sem("y_by_scalar"), sem("y_by_vector"), sem("y_stored")
            skips = {k.engine: sem("no_split") for k in (nc.scalar, nc.vector, nc.gpsimd)}

            def chunks(eng, body):
                def where_none(n, steps):
                    with eng.If(n):
                        eng.sem_inc(skips[eng.engine], 1)
                    with eng.Else():
                        steps()

                def expert(e, ahead):
                    at_ = bass.ds(e, 1)
                    n = eng.value_load(nch_i[0:1, at_], min_val=1, max_val=NT)
                    b = eng.value_load(first_i[0:1, at_], min_val=0, max_val=SLOTS - 1)
                    with eng.Fori(0, n) as c:
                        body(e, b + c, lambda steps: where_none(c, steps), lambda steps: ahead(n - 1 - c, steps))

                with eng.Fori(0, E - 1) as e:
                    expert(e, where_none)
                expert(E - 1, lambda left, steps: None)

            with nc.Block() as block:
                def wait_lo(eng, e, q):
                    if q == 0:
                        eng.wait_ge(lo_pool, e + 1)
                    else:
                        eng.wait_ge(lo_done, e * NV + q)

                @block.sync
                def _(sp):
                    def load(e, q):
                        if q >= NR:
                            wait_lo(sp, e, slot[q])
                        elif not isinstance(e, int):
                            wait_lo(sp, e - 1, NP - 1 - slot[::-1].index(q))
                        src = ins["experts"][bass.ds((e + layer * E) * NP + q, 1)].rearrange("c p n -> p (c n)")
                        sp.dma_start(raw[:, slot[q]], src).then_inc(loaded[slot[q]], 16)

                    for q in range(NR):
                        load(0, q)
                    with sp.Fori(1, E) as e:
                        load(e, 0)
                        load(e - 1, 4)
                        load(e - 1, 5)
                        for q in (3, 1, 2):
                            load(e, q)
                    load(E - 1, 4)
                    load(E - 1, 5)
                    for q in range(NR):
                        sp.wait_ge(loaded[q], 16 * E * slot.count(q))

                @block.gpsimd
                def _(pool):
                    def gather(j):
                        nc.gpsimd.tensor_copy(idx, slot_i[:, bass.ds(j, 1)]).then_inc(idx_ready, 1)
                        pool.wait_ge(idx_ready, j + 1)
                        pool.sem_inc(idx_seen, 1)
                        nc.gpsimd.indirect_dma_start(out=xg, out_offset=None, in_=hrows[:, :],
                                                     in_offset=bass.IndirectOffsetOnAxis(ap=idx, axis=0)).then_inc(gathered, 16)

                    gather(0)
                    pool.wait_ge(hi_first, 1)
                    nc.gpsimd.tensor_tensor(wlo[:, 0], raw[:, 0], whi[:, 0].bitcast(f32), ALU.subtract).then_inc(lo_pool, 1)
                    pool.wait_ge(turned, 1)
                    gather(1)
                    pool.wait_ge(y_filled, (SLOTS - SEQ * TOPK // P) // NT * 16)

                    def first_lo(e):
                        pool.wait_ge(hi_first, e + 1)
                        nc.gpsimd.tensor_tensor(wlo[:, 0], raw[:, 0], whi[:, 0].bitcast(f32), ALU.subtract).then_inc(lo_pool, 1)

                    def body(e, j, first, ahead):
                        ahead(lambda: first_lo(e + 1))
                        pool.wait_ge(y_act, j + 2)
                        pool.wait_ge(y_dve, j + 2)
                        pool.sem_inc(rows_seen, 1)
                        pool.dma_start(yrows[bass.ds(j * P, P), :], ysb).then_inc(y_stored, 16)
                        pool.wait_ge(turned, j + 2)
                        gather(j + 2)
                        pool.wait_ge(y_stored, j * 16 + 16)
                        pool.sem_inc(y_free, 1)

                    chunks(pool, body)

                @block.tensor
                def _(pe):
                    def transpose_rows(j):
                        pe.wait_ge(gathered, j * 16 + 16)
                        for k in range(KD):
                            last = nc.tensor.transpose(ps[:, k // 4, (k % 4) * P:(k % 4 + 1) * P], xg[:, k * P:(k + 1) * P], ident)
                        last.then_inc(turned, 1)

                    def hidden(j, e, q, done, ks=range(KD)):
                        if ks[0] == 0:
                            wait_lo(pe, e, q)
                        for k in ks:
                            w = slice(k * FH, (k + 1) * FH)
                            last = three_passes(ps[:, q, 0:FH], xhi[:, k], xlo[:, k], whi[:, q, w], wlo[:, q, w], k == 0, k == KD - 1)
                        if ks[-1] == KD - 1:
                            last.then_inc(done, 1)

                    def transpose_hidden(j, h):
                        pe.wait_ge(a_ready, j * 2 + h + 1)
                        for f in range(2):
                            last = nc.tensor.transpose(ps[:, 4 + h, f * P:(f + 1) * P], a_[:, h, f * P:(f + 1) * P], ident)
                        last.then_inc(ta[h], 1)

                    def down(e, h, col):
                        for f in range(2):
                            w = slice(f * D + col * HALF, f * D + (col + 1) * HALF)
                            last = three_passes(ps[:, 6 + col], ahi[:, 2 * h + f], alo[:, 2 * h + f], whi[:, 4 + h, w], wlo[:, 4 + h, w],
                                         h == 0 and f == 0, h == 1 and f == 1)
                        return last

                    transpose_rows(0)

                    def body(e, j, first, ahead):
                        pe.wait_ge(xlo_ready, j + 1)
                        hidden(j, e, 0, gd[0])
                        hidden(j, e, 1, ud[0])
                        hidden(j, e, 2, gd[1])
                        hidden(j, e, 3, ud[1], range(KD // 2))
                        transpose_hidden(j, 0)
                        hidden(j, e, 3, ud[1], range(KD // 2, KD))
                        pe.wait_ge(alo_ready, j * 2 + 1)
                        wait_lo(pe, e, 4)
                        pe.wait_ge(y_act, j + 1)
                        pe.wait_ge(y_dve, j + 1)
                        down(e, 0, 0)
                        transpose_hidden(j, 1)
                        transpose_rows(j + 1)
                        down(e, 0, 1)
                        pe.wait_ge(alo_ready, j * 2 + 2)
                        wait_lo(pe, e, 5)
                        down(e, 1, 0)
                        down(e, 1, 1).then_inc(d_done, 1)

                    chunks(pe, body)

                used = [gd[0], ud[0], gd[1], ud[1], d_done, d_done]

                @block.scalar
                def _(act):
                    def split_hi(e, q, uses):
                        act.wait_ge(loaded[slot[q]], (e * slot.count(slot[q]) + q // NR) * 16 + 16)
                        if uses is not None:
                            act.wait_ge(used[q], uses)
                        nc.scalar.copy(whi[:, q], raw[:, slot[q]]).then_inc(hi_first if q == 0 else hi_last if q == 5 else hi_done, 1)

                    def h_part(j):
                        act.wait_ge(turned, j + 1)
                        for k in range(4):
                            last = nc.scalar.activation(h32[:, k], ps[:, 0, k * P:(k + 1) * P], ACT.Identity, bias=shift[:, k:k + 1], scale=scale[:, k:k + 1])
                        last.then_inc(h_act, 1)

                    def x_hi(j):
                        act.wait_ge(h_act, j + 1)
                        act.wait_ge(h_dve, j + 1)
                        nc.scalar.copy(xhi, h32).then_inc(xhi_ready, 1)

                    def silu(j, h):
                        act.wait_ge(gd[h], j + 1)
                        nc.scalar.activation(sg_[:, h], ps[:, 2 * h, 0:FH], ACT.Silu).then_inc(silu_done, 1)

                    def a_hi(j, h):
                        act.wait_ge(ta[h], j + 1)
                        nc.scalar.copy(ahi[:, 2 * h:2 * h + 2].rearrange("p f n -> p (f n)"), ps[:, 4 + h, 0:2 * P]).then_inc(ahi_ready, 1)

                    nc.scalar.activation(sg_[:, 0, 0:1], eps, ACT.Silu)
                    act.sem_inc(y_act, 1)
                    act.sem_inc(y_free, 1)
                    split_hi(0, 0, None)
                    split_hi(0, 1, None)
                    h_part(0)
                    x_hi(0)
                    for q in (2, 3, 4):
                        split_hi(0, q, None)

                    def body(e, j, first, ahead):
                        silu(j, 0)
                        silu(j, 1)
                        ahead(lambda: split_hi(e + 1, 0, j + 1))
                        a_hi(j, 0)
                        first(lambda: split_hi(e, 5, None))
                        a_hi(j, 1)
                        h_part(j + 1)
                        x_hi(j + 1)
                        ahead(lambda: split_hi(e + 1, 1, j + 1))
                        act.wait_ge(d_done, j + 1)
                        act.wait_ge(y_free, j + 1)
                        nc.scalar.copy(ysb[:, 0:HALF], ps[:, 6]).then_inc(y_act, 1)
                        ahead(lambda: [split_hi(e + 1, q, j + 1) for q in (2, 3, 4)])

                    chunks(act, body)

                @block.vector
                def _(dve):
                    def split_lo(e, q):
                        if q == 5:
                            dve.wait_ge(hi_last, e + 1)
                        else:
                            dve.wait_ge(hi_done, e * 4 + q)
                        nc.vector.tensor_tensor(wlo[:, q], raw[:, slot[q]], whi[:, q].bitcast(f32), ALU.subtract).then_inc(lo_done, 1)

                    def h_part(j):
                        dve.wait_ge(turned, j + 1)
                        for k in range(4, KD):
                            last = nc.vector.tensor_scalar(h32[:, k], ps[:, 1, (k - 4) * P:(k - 3) * P], scale[:, k:k + 1], shift[:, k:k + 1], ALU.mult, ALU.add)
                        last.then_inc(h_dve, 1)

                    def x_lo(j):
                        dve.wait_ge(xhi_ready, j + 1)
                        nc.vector.tensor_tensor(xlo, h32, xhi.bitcast(f32), ALU.subtract).then_inc(xlo_ready, 1)

                    def gated(j, h):
                        dve.wait_ge(ud[h], j + 1)
                        dve.wait_ge(silu_done, j * 2 + h + 1)
                        nc.vector.tensor_tensor(a_[:, h], ps[:, 2 * h + 1, 0:FH], sg_[:, h], ALU.mult).then_inc(a_ready, 1)

                    def a_lo(j, h):
                        dve.wait_ge(ahi_ready, j * 2 + h + 1)
                        f = "p f n -> p (f n)"
                        nc.vector.tensor_tensor(alo[:, 2 * h:2 * h + 2].rearrange(f), ps[:, 4 + h, 0:2 * P], ahi[:, 2 * h:2 * h + 2].rearrange(f).bitcast(f32), ALU.subtract).then_inc(alo_ready, 1)

                    dve.sem_inc(y_dve, 1)
                    split_lo(0, 1)
                    h_part(0)
                    x_lo(0)
                    split_lo(0, 2)
                    split_lo(0, 3)

                    def body(e, j, first, ahead):
                        gated(j, 0)
                        first(lambda: split_lo(e, 4))
                        a_lo(j, 0)
                        gated(j, 1)
                        first(lambda: split_lo(e, 5))
                        a_lo(j, 1)
                        h_part(j + 1)
                        x_lo(j + 1)
                        dve.wait_ge(d_done, j + 1)
                        dve.wait_ge(y_free, j + 1)
                        nc.vector.tensor_copy(ysb[:, HALF:D], ps[:, 7]).then_inc(y_dve, 1)
                        ahead(lambda: [split_lo(e + 1, q) for q in (1, 2, 3)])

                    chunks(dve, body)

            NS = 4
            y0, at = view(0, (NS, D))
            y1, at = view(at, (NS, D))
            ta, at = view(at, (NS, D))
            idxs = small[:, 142:142 + 2 * NS].bitcast(u32)
            idx2_ready = sem("index2_ready")
            idx2_seen = sem("index2_seen")
            got = [sem(f"y_gathered{s_}") for s_ in range(NS)]
            w0_done, x_done = sem("y0_weighted"), sem("x_updated")
            chain2 = sem("combine_chain")
            o_stored = sem("out_stored")
            with nc.Block() as block:
                @block.gpsimd
                def _(pool):
                    with pool.Fori(0, NT // NS) as i:
                        for s in range(NS):
                            t = i * NS + s
                            pool.wait_ge(x_done, t + 1)
                            for k in range(2):
                                nc.gpsimd.tensor_copy(idxs[:, 2 * s + k:2 * s + k + 1], dest_i[:, bass.ds(t + k * NT, 1)]).then_inc(idx2_ready, 1)
                            pool.wait_ge(idx2_ready, t * 2 + 2)
                            pool.sem_inc(idx2_seen, 1)
                            for k, y in enumerate((y0, y1)):
                                nc.gpsimd.indirect_dma_start(out=y[:, s], out_offset=None, in_=yrows[0:SLOTS * P, :],
                                                             in_offset=bass.IndirectOffsetOnAxis(ap=idxs[:, 2 * s + k:2 * s + k + 1], axis=0)).then_inc(got[s], 16)

                @block.scalar
                def _(act):
                    with act.Fori(0, NT // NS) as i:
                        for s in range(NS):
                            act.wait_ge(got[s], i * 32 + 32)
                            act.wait_ge(x_done, i * NS + s + 1)
                            nc.scalar.activation(ta[:, s], y0[:, s], ACT.Copy, scale=wsel[:, bass.ds(i * NS + s, 1)]).then_inc(w0_done, 1)

                @block.vector
                def _(dve):
                    dve.sem_inc(x_done, NS)
                    with dve.Fori(0, NT // NS) as i:
                        st = Steps(dve, chain2, turn=i, per=2 * NS)
                        for s in range(NS):
                            dve.wait_ge(got[s], i * 32 + 32)
                            dve.wait_ge(w0_done, i * NS + s + 1)
                            xt = x[:, bass.ds(i * NS + s, 1), :].rearrange("p a d -> p (a d)")
                            st.link(nc.vector.scalar_tensor_tensor(ta[:, s], y1[:, s], wsel[:, bass.ds(i * NS + s + NT, 1)], ta[:, s], ALU.mult, ALU.add))
                            st.link(nc.vector.tensor_tensor(ta[:, s], ta[:, s], gate[:, 1], ALU.mult))
                            nc.vector.tensor_tensor(xt, xt, ta[:, s], ALU.add).then_inc(x_done, 1)
                        st.end()

                assert at <= 3 * NT // 2 * D
                if not last_layer:
                    @block.sync
                    def _(sp):
                        sp.dma_start(ada_acc(), ada_sums.rearrange("c p n -> p c n")).then_inc(sums_loaded, 16)
                        sp.wait_ge(sums_loaded, 16)

                if last_layer:
                    @block.sync
                    def _(sp):
                        with sp.Fori(0, NT) as t:
                            sp.wait_ge(x_done, t + NS + 1)
                            sp.dma_start(out[0, bass.ds(t * P, P), :], x[:, bass.ds(t, 1), :].rearrange("p a d -> p (a d)")).then_inc(o_stored, 16)
                        sp.wait_ge(o_stored, NT * 16)

        def hybrid_phase(layer):
            QW = 2 * P
            qkv, at = view(0, (3, NT, ATT_W))
            upad, at = view(at, (CT, SEQ + CONV_W - 1))
            conv, at = view(at, (CT, SEQ))
            w_at = at
            wraw, at = view(at, (KD * QW,))
            sgm, at = view(at, (2, HALF))
            xhi = nc.alloc_sbuf_tensor_at("in_x_high", [P, KD, SEQ], f32r, offset=x_base)[:, :, :]
            xlo, _ = place("in_x_low", WORK, (KD, SEQ), f32r)
            whi, hi_at = place("in_w_high", at, (2, KD * QW), f32r)
            wlo, _ = place("in_w_low", hi_at, (2, KD * QW), f32r)
            x_hi, x_lo, w_hi, w_lo = sem("x_high"), sem("x_low"), sem("w_high"), sem("w_low")
            par = {k: mix0[:, v[0]:v[0] + v[1]] for k, v in MIX0.items()}
            dw = par["dw_w"].rearrange("p (c j) -> p c j", j=CONV_W)
            w_loaded, w_used = sem("w_in_loaded"), sem("w_in_used")
            u_done = sem("conv_product_done")
            sig_done, a_done = sem("sigmoid_done"), sem("a_copied")
            glu_done = sem("glu_done")
            qkv_done, qkv_out = sem("qkv_block_done"), sem("qkv_evacuated")
            padded = sem("pad_zeroed")
            chain = sem("conv_chain")
            NU, NB = CT, 3 * ATT_W // QW
            with nc.Block() as block:
                @block.sync
                def _(sp):
                    sp.dma_start(wraw, ins["hy_in"][0]).then_inc(w_loaded, 16)
                    with sp.Fori(1, NU + NB + 1) as b:
                        sp.wait_ge(w_lo, b)
                        sp.dma_start(wraw, ins["hy_in"][bass.ds(b, 1)].rearrange("c p n -> p (c n)")).then_inc(w_loaded, 16)

                @block.tensor
                def _(pe):
                    pe.sem_inc(w_used, 2)
                    pe.wait_ge(x_lo, KD)
                    with pe.Fori(0, NU // 2) as i:
                        for s in range(2):
                            wh, wl = (v_[:, s].rearrange("p (k n) -> p k n", n=QW) for v_ in (whi, wlo))
                            pe.wait_ge(w_lo, i * 2 + s + 1)
                            pe.wait_ge(sig_done, i * 4 + 4)
                            pe.wait_ge(a_done, i * 4 + 4)
                            for h in range(2):
                                for q in range(2):
                                    for k in range(KD):
                                        c_, n_ = slice(q * P, (q + 1) * P), slice(h * HALF, (h + 1) * HALF)
                                        last = three_passes(ps[:, s * 4 + h * 2 + q], wh[:, k, c_], wl[:, k, c_], xhi[:, k, n_], xlo[:, k, n_], k == 0, k == KD - 1)
                                last.then_inc(u_done, 1)
                            pe.wait_ge(u_done, i * 4 + s * 2 + 2)
                            pe.sem_inc(w_used, 1)
                    pe.wait_ge(sig_done, NU * 2 + 4)
                    pe.wait_ge(a_done, NU * 2 + 4)
                    with pe.Fori(0, NB // 2) as i:
                        for s in range(2):
                            wh, wl = (v_[:, s].rearrange("p (k n) -> p k n", n=QW) for v_ in (whi, wlo))
                            pe.wait_ge(w_lo, NU + i * 2 + s + 1)
                            for t in range(NT):
                                pe.wait_ge(qkv_out, i * 2 * NT + s * NT + t + 1)
                                for k in range(KD):
                                    n_ = slice(t * P, (t + 1) * P)
                                    last = three_passes(ps[:, t, 0:QW], xhi[:, k, n_], xlo[:, k, n_], wh[:, k], wl[:, k], k == 0, k == KD - 1)
                                last.then_inc(qkv_done, 1)
                            pe.wait_ge(qkv_done, i * 2 * NT + (s + 1) * NT)
                            pe.sem_inc(w_used, 1)

                @block.scalar
                def _(act):
                    act.sem_inc(qkv_out, NT)
                    act.sem_inc(sig_done, 4)
                    act.sem_inc(a_done, 4)

                    def w_high(b, s):
                        act.wait_ge(w_loaded, b * 16 + 16)
                        act.wait_ge(w_used, b + 1)
                        nc.scalar.copy(whi[:, s], wraw).then_inc(w_hi, 1)

                    for k in range(KD // 2):
                        nc.scalar.copy(xhi[:, k], hT[:, k]).then_inc(x_hi, 1)
                    w_high(0, 0)
                    for k in range(KD // 2, KD):
                        nc.scalar.copy(xhi[:, k], hT[:, k]).then_inc(x_hi, 1)
                    with act.Fori(0, NU // 2) as i:
                        for s in range(2):
                            w_high(i * 2 + s + 1, 1 - s)
                            for h in range(2):
                                n = i * 4 + s * 2 + h
                                act.wait_ge(u_done, n + 1)
                                act.wait_ge(glu_done, i * 4 + s * 2 + 2)
                                nc.scalar.activation(sgm[:, h], ps[:, s * 4 + h * 2 + 1], ACT.Sigmoid).then_inc(sig_done, 1)
                                nc.scalar.copy(upad[:, bass.ds(i * 2 + s, 1), CONV_W - 1 + h * HALF:CONV_W - 1 + (h + 1) * HALF].rearrange("p a n -> p (a n)"), ps[:, s * 4 + h * 2]).then_inc(a_done, 1)
                    with act.Fori(0, NB // 2) as i:
                        for s in range(2):
                            w_high(NU + i * 2 + s + 1, 1 - s)
                            for t in range(NT):
                                act.wait_ge(qkv_done, i * 2 * NT + s * NT + t + 1)
                                nc.scalar.copy(qkv[:, bass.ds(i, 1), t, s * QW:(s + 1) * QW].rearrange("p a n -> p (a n)"), ps[:, t, 0:QW]).then_inc(qkv_out, 1)

                @block.gpsimd
                def _(pool):
                    pool.sem_inc(glu_done, 2)

                    def w_low(b, s):
                        pool.wait_ge(w_hi, b + 1)
                        nc.gpsimd.tensor_tensor(wlo[:, s], wraw, whi[:, s].bitcast(f32), ALU.subtract).then_inc(w_lo, 1)

                    w_low(0, 0)
                    with pool.Fori(0, NU // 2) as i:
                        for s in range(2):
                            c = i * 2 + s
                            w_low(c + 1, 1 - s)
                            for h in range(2):
                                pool.wait_ge(sig_done, c * 2 + h + 5)
                                pool.wait_ge(a_done, c * 2 + h + 5)
                                u = upad[:, bass.ds(c, 1), CONV_W - 1 + h * HALF:CONV_W - 1 + (h + 1) * HALF].rearrange("p a n -> p (a n)")
                                nc.gpsimd.tensor_tensor(u, u, sgm[:, h], ALU.mult).then_inc(glu_done, 1)
                    with pool.Fori(0, NB // 2) as i:
                        for s in range(2):
                            w_low(NU + i * 2 + s + 1, 1 - s)

                @block.vector
                def _(dve):
                    for k in range(KD):
                        dve.wait_ge(x_hi, k + 1)
                        nc.vector.tensor_tensor(xlo[:, k], hT[:, k], xhi[:, k].bitcast(f32), ALU.subtract).then_inc(x_lo, 1)
                    nc.vector.memset(upad[:, :, 0:CONV_W - 1], 0.0).then_inc(padded, 1)
                    dve.wait_ge(padded, 1)
                    with dve.Fori(0, CT) as c:
                        dve.wait_ge(glu_done, c * 2 + 4)
                        st = Steps(dve, chain, turn=c, per=CONV_W)
                        y = conv[:, bass.ds(c, 1), :].rearrange("p a n -> p (a n)")
                        for j in range(CONV_W):
                            u = upad[:, bass.ds(c, 1), j:j + SEQ].rearrange("p a n -> p (a n)")
                            w = dw[:, bass.ds(c, 1), j]
                            if j == 0:
                                st.link(nc.vector.tensor_scalar(y, u, w, par["dw_b"][:, bass.ds(c, 1)], ALU.mult, ALU.add))
                            else:
                                st.link(nc.vector.scalar_tensor_tensor(y, u, w, y, ALU.mult, ALU.add))
                        st.end()

            sq, _ = view(w_at, (CT, HALF))
            mu = hT[:, 0, 0:HALF]
            sd = hT[:, 1, 0:HALF]
            qsq = hT[:, 2:6, :].rearrange("p a b -> p (a b)")
            rqk = small[:, 16:16 + 2 * NT * HEADS]
            gq8 = small[:, 150:151]
            summed, centred, sq_done, var_sum = sem("ln_summed"), sem("centred"), sem("ln_squared"), sem("ln_var_summed")
            sd_done, normed = sem("ln_sd"), sem("ln_normed")
            qsq_done, qss_done, qrms = sem("qk_squared"), sem("qk_summed"), sem("qk_rms")
            chain = sem("ln_chain")
            wo_loaded, x_again = sem("w_out_loaded"), sem("x_loaded_again")
            with nc.Block() as block:
                @block.tensor
                def _(pe):
                    for h in range(2):
                        cols = slice(h * HALF, (h + 1) * HALF)
                        for c in range(CT):
                            last = nc.tensor.matmul(ps[:, h], ones, conv[:, c, cols], start=(c == 0), stop=(c == CT - 1))
                        last.then_inc(summed, 1)
                        pe.wait_ge(sq_done, h + 1)
                        for c in range(CT):
                            last = nc.tensor.matmul(ps[:, 2 + h], ones, sq[:, c], start=(c == 0), stop=(c == CT - 1))
                        last.then_inc(var_sum, 1)

                @block.vector
                def _(dve):
                    st = Steps(dve, chain)
                    for h in range(2):
                        y = conv[:, :, h * HALF:(h + 1) * HALF]
                        dve.wait_ge(summed, h + 1)
                        st.link(nc.vector.tensor_scalar(mu, ps[:, h], 1.0 / CONV_CH, None, ALU.mult))
                        nc.vector.tensor_tensor(y, y, bc(mu, 1, CT), ALU.subtract).then_inc(centred, 1)
                        dve.wait_ge(centred, h + 1)
                        dve.wait_ge(qsq_done, h + 1)
                        nc.vector.tensor_reduce(rqk[:, h * NT * HEADS:(h + 1) * NT * HEADS], qsq.rearrange("p (a d) -> p a d", d=HD), X, ALU.add).then_inc(qss_done, 1)
                        dve.wait_ge(sd_done, h + 1)
                        st.link(nc.vector.reciprocal(sd, sd))
                        nc.vector.tensor_tensor(y, y, bc(sd, 1, CT), ALU.mult).then_inc(normed, 1)
                        dve.wait_ge(normed, h + 1)
                    dve.wait_ge(qrms, 1)
                    st.did(nc.vector.reciprocal(rqk, rqk))
                    st.did(nc.vector.tensor_scalar(gq8, par["gq"], float(HD) ** -0.5, None, ALU.mult))

                @block.scalar
                def _(act):
                    for h in range(2):
                        if h:
                            act.wait_ge(qss_done, h)
                        nc.scalar.activation(qsq, qkv[:, h].rearrange("p t d -> p (t d)"), ACT.Square).then_inc(qsq_done, 1)
                        act.wait_ge(centred, h + 1)
                        if h:
                            act.wait_ge(var_sum, h)
                        nc.scalar.activation(sq, conv[:, :, h * HALF:(h + 1) * HALF], ACT.Square).then_inc(sq_done, 1)
                        act.wait_ge(var_sum, h + 1)
                        if h:
                            act.wait_ge(normed, h)
                        nc.scalar.activation(sd, ps[:, 2 + h], ACT.Sqrt, bias=eps, scale=1.0 / CONV_CH).then_inc(sd_done, 1)
                    act.wait_ge(qss_done, 2)
                    nc.scalar.activation(rqk, rqk, ACT.Sqrt, bias=eps, scale=1.0 / HD).then_inc(qrms, 1)
                    act.wait_ge(normed, 2)
                    for c in range(CT):
                        nc.scalar.activation(conv[:, c], conv[:, c], ACT.Silu, bias=par["ln_b"][:, c:c + 1], scale=par["ln_g"][:, c:c + 1])

            at = NT * ATT_W * 3
            attT, at = view(at, (PAIRS, SEQ))
            at = NT * ATT_W * 3 + CT * (SEQ + CONV_W - 1) + CT * SEQ
            qn, at = view(at, (NT, P))
            kn, at = view(at, (NT, P))
            qT, at = view(at, (SEQ,))
            kT, at = view(at, (SEQ,))
            pr, at = view(at, (2, SEQ))
            pT, at = view(at, (2, SEQ))
            att, at = view(at, (NT, P))
            aw, at_a = view(at, (4, HALF))
            aacc, _ = view(at_a, (HALF,))
            aw_loaded = [sem(f"ada1_w_loaded{s_}") for s_ in range(4)]
            aw_used, aacc_ready, aacc_stored = sem("ada1_w_used"), sem("ada1_sum_ready"), sem("ada1_sum_stored")
            ada_chain = sem("ada1_chain")
            nmax = small[:, 152:154]
            rsum = small[:, 156:160]
            U = 2 * NT
            qk_ready, qk_turned = sem("qk_normed"), sem("qk_transposed")
            qT_ready, kT_ready = sem("qT_ready"), sem("kT_ready")
            s_done, m_done, p_done = sem("scores_ready"), sem("max_ready"), sem("probs_ready")
            t_done, pa, pb = sem("probs_transposed"), sem("pT_by_vector"), sem("pT_by_scalar")
            o_done, o_out = sem("pv_ready"), sem("out_normed")
            att_turned, att_out = sem("att_transposed"), sem("attT_ready")
            chain = sem("attention_chain")
            NB_A = 2 * N_MOD // PAIRS
            NB_1 = NB_A * (PAIRS - 1)

            def load_tile(sp, n, k):
                sp.dma_start(aw[:, k % 4], ins["ada_w1"][bass.ds(n, 1), :, k * HALF:(k + 1) * HALF].rearrange("c p n -> p (c n)")).then_inc(aw_loaded[k % 4], 16)

            def load_rest(sp, n):
                load_tile(sp, n, 3)
                for k in range(4, KD):
                    sp.wait_ge(aw_used, n * (KD - 1) + k - 3)
                    load_tile(sp, n, k)

            def store_sum(sp, n):
                sp.wait_ge(aacc_ready, n + 1)
                sp.dma_start(ada_sums[bass.ds(n, 1)].rearrange("c p n -> p (c n)"), aacc).then_inc(aacc_stored, 16)

            def ada_turn(sp, n):
                load_rest(sp, n)
                for k in range(3):
                    sp.wait_ge(aw_used, n * (KD - 1) + k + 5)
                    load_tile(sp, n + 1, k)
                store_sum(sp, n)

            def ada_block(pool, n):
                st = Steps(pool, ada_chain, turn=n, per=KD)
                for k in range(KD):
                    w = aw[:, k % 4]
                    pool.wait_ge(aw_loaded[k % 4], n * (KD // 4 * 16) + (k // 4 + 1) * 16)
                    st.link(nc.gpsimd.tensor_tensor(w, w, pcol[:, 0, k:k + 1].to_broadcast([P, HALF]), ALU.mult))
                    if k == 0:
                        continue
                    if k == 1:
                        pool.wait_ge(aacc_stored, n * 16 + 16)
                        nc.gpsimd.tensor_tensor(aacc, w, aw[:, 0], ALU.add).then_inc(aw_used, 2)
                        pool.wait_ge(aw_used, n * (KD - 1) + 2)
                    elif k < KD - 1:
                        nc.gpsimd.tensor_tensor(aacc, aacc, w, ALU.add).then_inc(aw_used, 1)
                        pool.wait_ge(aw_used, n * (KD - 1) + k + 1)
                    else:
                        nc.gpsimd.tensor_tensor(aacc, aacc, w, ALU.add).then_inc(aacc_ready, 1)

            with nc.Block() as block:
                @block.sync
                def _(sp):
                    sp.dma_start(hT[:, :, :].rearrange("p k n -> p (k n)"), ins["hy_out"]).then_inc(wo_loaded, 16)

                    sp.sem_inc(aacc_stored, 16)
                    for k in range(3):
                        load_tile(sp, 0, k)
                    with sp.Fori(0, NB_1) as n:
                        ada_turn(sp, n)
                    sp.wait_ge(wo_loaded, 16)
                    sp.dma_start(x[:, :, :], ins["x"].rearrange("(t p) d -> p t d", p=P)).then_inc(x_again, 16)
                    sp.wait_ge(x_again, 16)

                @block.gpsimd
                def _(pool):
                    def norm_qk(i):
                        for n, dst in enumerate((qn, kn)):
                            r = rqk[:, n * NT * HEADS:(n + 1) * NT * HEADS].rearrange("p (t h) -> p t h", h=HEADS)
                            for hh in range(2):
                                src = qkv[:, n, :, bass.ds(i * P + hh * HD, HD)]
                                nc.gpsimd.tensor_tensor(dst[:, :, hh * HD:(hh + 1) * HD], src, r[:, :, bass.ds(i * 2 + hh, 1)].to_broadcast([P, NT, HD]), ALU.mult).then_inc(qk_ready, 1)

                    norm_qk(0)
                    with pool.Fori(1, PAIRS) as i:
                        pool.wait_ge(qk_turned, i * 2)
                        norm_qk(i)
                        with pool.Fori(0, NB_A) as m:
                            ada_block(pool, (i - 1) * NB_A + m)

                @block.tensor
                def _(pe):
                    with pe.Fori(0, PAIRS) as i:
                        for n, src in enumerate((qn, kn)):
                            pe.wait_ge(qk_ready, i * 4 + 2 * n + 2)
                            for t in range(NT):
                                last = nc.tensor.transpose(ps[:, 4 + 2 * n + t // 4, (t % 4) * P:(t % 4 + 1) * P], src[:, t], ident)
                            last.then_inc(qk_turned, 1)
                        pe.wait_ge(qT_ready, i + 1)
                        pe.wait_ge(kT_ready, i + 1)

                        def scores(u):
                            head, qt = divmod(u, NT)
                            rows_ = slice(head * HD, (head + 1) * HD)
                            b = (u % 2) * 2
                            if u >= 2:
                                pe.wait_ge(p_done, i * U + u - 1)
                            for h in range(0, (qt + 1) * P, HALF):
                                n = min(HALF, (qt + 1) * P - h)
                                diag = h + n == (qt + 1) * P
                                last = nc.tensor.matmul(ps[:, b + h // HALF, 0:n], qT[rows_, qt * P:(qt + 1) * P], kT[rows_, h:h + n], start=True, stop=True)
                                if diag:
                                    last = nc.tensor.matmul(ps[:, b + h // HALF, n - P:n], ident, const("maskneg"), start=False, stop=True, skip_group_check=True)
                            last.then_inc(s_done, 1)

                        def turn(u):
                            qt = u % NT
                            pe.wait_ge(p_done, i * U + u + 1)
                            if u:
                                pe.wait_ge(pa, i * U + u)
                                pe.wait_ge(pb, i * U + u)
                            for k in range(qt + 1):
                                last = nc.tensor.transpose(ps[:, 4 + k // 4, (k % 4) * P:(k % 4 + 1) * P], pr[:, u % 2, k * P:(k + 1) * P], ident)
                            last.then_inc(t_done, 1)

                        def values(u):
                            head, qt = divmod(u, NT)
                            pe.wait_ge(pa, i * U + u + 1)
                            pe.wait_ge(pb, i * U + u + 1)
                            if u >= 2:
                                pe.wait_ge(o_out, i * U + u - 1)
                            for k in range(qt + 1):
                                last = nc.tensor.matmul(ps[:, 6 + u % 2, 0:HD], pT[:, u % 2, k * P:(k + 1) * P], qkv[:, 2, k, bass.ds(i * P + head * HD, HD)], start=(k == 0), stop=(k == qt))
                            last.then_inc(o_done, 1)

                        scores(0)
                        scores(1)
                        for u in range(U):
                            turn(u)
                            if u + 2 < U:
                                scores(u + 2)
                            if u:
                                values(u - 1)
                        values(U - 1)
                        pe.wait_ge(o_out, i * U + U)
                        for t in range(NT):
                            last = nc.tensor.transpose(ps[:, 4 + t // 4, (t % 4) * P:(t % 4 + 1) * P], att[:, t], ident)
                        last.then_inc(att_turned, 1)
                        pe.wait_ge(att_out, i + 2)

                @block.scalar
                def _(act):
                    with act.Fori(0, PAIRS) as i:
                        act.wait_ge(qk_turned, i * 2 + 1)
                        nc.scalar.activation(qT, ps[:, 4:6].rearrange("p a n -> p (a n)"), ACT.Copy, scale=gq8).then_inc(qT_ready, 1)

                        def probs(u):
                            n = (u % NT + 1) * P
                            act.wait_ge(m_done, i * U + u + 1)
                            if u >= 2:
                                act.wait_ge(t_done, i * U + u - 1)
                            if u >= 4:
                                act.wait_ge(o_out, i * U + u - 3)
                            b = (u % 2) * 2
                            nc.scalar.activation(pr[:, u % 2, 0:n], ps[:, b:b + 2].rearrange("p a n -> p (a n)")[:, 0:n], ACT.Exp, bias=nmax[:, u % 2:u % 2 + 1], accum_out=rsum[:, u % 4:u % 4 + 1]).then_inc(p_done, 1)

                        probs(0)
                        for u in range(U):
                            if u + 1 < U:
                                probs(u + 1)
                            act.wait_ge(t_done, i * U + u + 1)
                            n = (u % NT + 1) * P
                            if n > HALF:
                                if u >= 2:
                                    act.wait_ge(o_done, i * U + u - 1)
                                nc.scalar.copy(pT[:, u % 2, HALF:n], ps[:, 5, 0:n - HALF]).then_inc(pb, 1)
                            else:
                                act.sem_inc(pb, 1)
                        act.wait_ge(att_out, i + 2)

                @block.vector
                def _(dve):
                    dve.sem_inc(att_out, 1)
                    with dve.Fori(0, PAIRS) as i:
                        st = Steps(dve, chain, turn=i, per=U)
                        dve.wait_ge(qk_turned, i * 2 + 2)
                        nc.vector.tensor_scalar(kT, ps[:, 6:8].rearrange("p a n -> p (a n)"), par["gk"], None, ALU.mult).then_inc(kT_ready, 1)

                        def maxes(u):
                            n = (u % NT + 1) * P
                            b = (u % 2) * 2
                            dve.wait_ge(s_done, i * U + u + 1)
                            if u >= 2:
                                dve.wait_ge(p_done, i * U + u - 1)
                            nc.vector.tensor_reduce(nmax[:, u % 2:u % 2 + 1], ps[:, b:b + 2].rearrange("p a n -> p (a n)")[:, 0:n], X, ALU.max, negate=True).then_inc(m_done, 1)

                        def normed(u):
                            head, qt = divmod(u, NT)
                            dve.wait_ge(p_done, i * U + u + 1)
                            r = rsum[:, u % 4:u % 4 + 1]
                            st.link(nc.vector.reciprocal(rinv, r))
                            dve.wait_ge(o_done, i * U + u + 1)
                            nc.vector.tensor_scalar(att[:, qt, head * HD:(head + 1) * HD], ps[:, 6 + u % 2, 0:HD], rinv, None, ALU.mult).then_inc(o_out, 1)
                            dve.wait_ge(o_out, i * U + u + 1)

                        rinv = small[:, 154:155]
                        maxes(0)
                        maxes(1)
                        for u in range(U):
                            dve.wait_ge(t_done, i * U + u + 1)
                            n = min((u % NT + 1) * P, HALF)
                            if u >= 2:
                                dve.wait_ge(o_done, i * U + u - 1)
                            nc.vector.tensor_copy(pT[:, u % 2, 0:n], ps[:, 4, 0:n]).then_inc(pa, 1)
                            if u + 2 < U:
                                maxes(u + 2)
                            if u:
                                normed(u - 1)
                        normed(U - 1)
                        st.end()
                        dve.wait_ge(att_turned, i + 1)
                        nc.vector.tensor_copy(attT[:, bass.ds(i, 1), :].rearrange("p a n -> p (a n)"), ps[:, 4:6].rearrange("p a n -> p (a n)")).then_inc(att_out, 1)
                        dve.wait_ge(att_out, i + 2)

            tmp, at = view(at - NT * P, (2, HALF))
            done, updated = sem("out_product"), sem("x_updated")
            chain = sem("out_chain")
            with nc.Block() as block:
                @block.sync
                def _(sp):
                    with sp.Fori(NB_1, 2 * N_MOD - 1) as n:
                        ada_turn(sp, n)
                    load_rest(sp, 2 * N_MOD - 1)
                    store_sum(sp, 2 * N_MOD - 1)
                    sp.wait_ge(aacc_stored, 16 * (2 * N_MOD + 1))

                @block.gpsimd
                def _(pool):
                    with pool.Fori(NB_1, 2 * N_MOD) as n:
                        ada_block(pool, n)

                @block.tensor
                def _(pe):
                    with pe.Fori(0, 2) as h:
                        for t in range(NT):
                            pe.wait_ge(updated, h * NT + NT)
                            for k in range(KD):
                                src = attT[:, k] if k < PAIRS else conv[:, k - PAIRS]
                                last = nc.tensor.matmul(ps[:, t], src[:, t * P:(t + 1) * P], hT[:, k, bass.ds(h * HALF, HALF)], start=(k == 0), stop=(k == KD - 1))
                            last.then_inc(done, 1)

                @block.vector
                def _(dve):
                    dve.sem_inc(updated, NT)
                    with dve.Fori(0, 2) as h:
                        st = Steps(dve, chain, turn=h, per=NT)
                        for t in range(NT):
                            dve.wait_ge(done, h * NT + t + 1)
                            st.link(nc.vector.tensor_tensor(tmp[:, t % 2], ps[:, t], gate[:, 0, bass.ds(h * HALF, HALF)], ALU.mult))
                            xt = x[:, t, bass.ds(h * HALF, HALF)]
                            nc.vector.tensor_tensor(xt, xt, tmp[:, t % 2], ALU.add).then_inc(updated, 1)
                            dve.wait_ge(updated, h * NT + t + NT + 1)
                        st.end()

        def ssm_phase(layer):
            TPC = CHUNK // P
            GT = GW // P
            CTG = GT + 2
            H, DH = SSM_HEADS, SSM_HEAD_DIM
            LC = CHUNK + P
            par = {k: mix1[:, v[0]:v[0] + v[1]] for k, v in MIX1.items()}
            cw = par["conv_w"].rearrange("p (c j) -> p c j", j=SCONV)
            row = {k: rows[:, v[0]:v[0] + v[1]] for k, v in ROWS.items()}
            dt, at = view(0, (NT, H))
            acs, at = view(at, (NT, H))
            eacs, at = view(at, (NT, H))
            dst, at = view(at, (NT, H))
            cdec, at = view(at, (NCH, H))
            base = at
            wdt, at = view(at, (KD, H))
            t0_, at = view(at, (NT, H))
            t1_, at = view(at, (NT, H))
            t2_, at = view(at, (NT, H))
            da, at = view(at, (NT, H))
            nega, at = view(at, (H,))
            arow, at = view(at, (SEQ,))
            wdt_loaded, dt_raw, chain = sem("dt_w_loaded"), sem("dt_product"), sem("dt_chain")
            exp_done, ln_done, a_done = sem("dt_exp"), sem("dt_ln"), sem("a_exp")
            abs_done, u_done2 = sem("dt_abs"), sem("dt_one_plus")
            da_ready, cums, e_done, arow_out = sem("da_ready"), sem("cumsums"), sem("decays"), sem("acs_row_ready")
            cum_out, dec_in = sem("acs_ready"), sem("decay_in_ready")
            arow_stored = sem("acs_rows_stored")
            with nc.Block() as block:
                @block.sync
                def _(sp):
                    sp.dma_start(wdt.rearrange("p k n -> p (k n)"), ins["ssm_dt"]).then_inc(wdt_loaded, 16)
                    sp.wait_ge(arow_out, 1)
                    sp.dma_start(acs_rows[:, :], arow[0:H, :]).then_inc(arow_stored, 16)
                    sp.wait_ge(arow_stored, 16)

                @block.tensor
                def _(pe):
                    pe.wait_ge(wdt_loaded, 16)
                    for t in range(NT):
                        for k in range(KD):
                            last = nc.tensor.matmul(ps[:, 0, t * H:(t + 1) * H], hT[:, k, t * P:(t + 1) * P], wdt[:, k], start=(k == 0), stop=(k == KD - 1))
                    last.then_inc(dt_raw, 1)
                    pe.wait_ge(da_ready, 1)
                    for c in range(NCH):
                        a, b = 2 * c, 2 * c + 1
                        nc.tensor.matmul(ps[:, 1, a * H:(a + 1) * H], const("tri_inc"), da[:, a], start=True, stop=True)
                        nc.tensor.matmul(ps[:, 1, b * H:(b + 1) * H], const("tri_inc"), da[:, b], start=True, stop=False)
                        nc.tensor.matmul(ps[:, 1, b * H:(b + 1) * H], ones, da[:, a], start=False, stop=True)
                        nc.tensor.matmul(ps[:, 2, c * H:(c + 1) * H], ones, da[:, a], start=True, stop=False)
                        nc.tensor.matmul(ps[:, 2, c * H:(c + 1) * H], ones, da[:, b], start=False, stop=True)
                        r = ps[0:H, 3 + c // 2, (c % 2) * CHUNK:(c % 2 + 1) * CHUNK]
                        at_, n_ = CONST["tri_inc"]
                        nc.tensor.matmul(r, da[:, a], cst[:, at_:at_ + 2 * P], start=True, stop=True)
                        last = nc.tensor.matmul(r[:, P:2 * P], da[:, b], const("tri_inc"), start=False, stop=True, skip_group_check=True)
                    last.then_inc(cums, 1)

                @block.scalar
                def _(act):
                    nc.scalar.activation(nega, row["a_log"], ACT.Exp).then_inc(a_done, 1)
                    act.wait_ge(abs_done, 1)
                    f = lambda v: v.rearrange("p t h -> p (t h)")
                    nc.scalar.activation(f(t1_), f(t1_), ACT.Exp, scale=-1.0).then_inc(exp_done, 1)
                    act.wait_ge(u_done2, 1)
                    nc.scalar.activation(f(da), f(t2_), ACT.Ln).then_inc(ln_done, 1)
                    act.wait_ge(dec_in, 1)
                    nc.scalar.activation(f(eacs), f(acs), ACT.Exp)
                    nc.scalar.activation(f(dst), f(dst), ACT.Exp)
                    nc.scalar.activation(f(cdec), f(cdec), ACT.Exp).then_inc(e_done, 1)
                    act.wait_ge(cums, 1)
                    nc.scalar.copy(arow[0:H, :], ps[0:H, 3:5].rearrange("p a n -> p (a n)")).then_inc(arow_out, 1)

                @block.vector
                def _(dve):
                    v = nc.vector
                    st = Steps(dve, chain)
                    dve.wait_ge(dt_raw, 1)
                    st.link(v.tensor_tensor(t0_, ps[:, 0, 0:NT * H].rearrange("p (t h) -> p t h", h=H), bc(row["dt_bias"], 1, NT), ALU.add))
                    st.link(v.tensor_scalar(t1_, t0_, -1.0, None, ALU.mult))
                    v.tensor_tensor(t1_, t0_, t1_, ALU.max).then_inc(abs_done, 1)
                    dve.wait_ge(exp_done, 1)
                    v.tensor_scalar(t2_, t1_, 1.0, None, ALU.add).then_inc(u_done2, 1)
                    dve.wait_ge(u_done2, 1)
                    dve.wait_ge(ln_done, 1)
                    st.link(v.tensor_scalar(t2_, t2_, 1.0, None, ALU.subtract))
                    st.link(v.tensor_scalar(dt, t2_, 0.0, None, ALU.is_equal))
                    st.did(v.tensor_tensor(da, da, dt, ALU.add))
                    st.link(v.tensor_tensor(t2_, t2_, dt, ALU.add))
                    st.link(v.reciprocal(t2_, t2_))
                    st.link(v.tensor_tensor(da, da, t1_, ALU.mult))
                    st.link(v.tensor_tensor(da, da, t2_, ALU.mult))
                    st.link(v.scalar_tensor_tensor(dt, t0_, 0.0, da, ALU.max, ALU.add))
                    dve.wait_ge(a_done, 1)
                    st.link(v.tensor_scalar(nega, nega, -1.0, None, ALU.mult))
                    v.tensor_tensor(da, dt, bc(nega, 1, NT), ALU.mult).then_inc(da_ready, 1)
                    dve.wait_ge(cums, 1)
                    st.link(v.tensor_copy(acs.rearrange("p t h -> p (t h)"), ps[:, 1, 0:NT * H]))
                    st.link(v.tensor_copy(cdec.rearrange("p t h -> p (t h)"), ps[:, 2, 0:NCH * H]))
                    v.tensor_tensor(dst.rearrange("p (c a) h -> p c a h", a=TPC), bc(cdec, 2, TPC), acs.rearrange("p (c a) h -> p c a h", a=TPC), ALU.subtract).then_inc(dec_in, 1)

            HB = 2
            NBAT = HPG // HB
            at = base
            xw, at = view(at, (2, KD * P))
            zw, at = view(at, (KD, GW))
            ow, at = view(at, (GT, D))
            raw, at = view(at, (2, SEQ + SCONV))
            cv_at = at
            cv, at = view(at, (2, SEQ))
            BT, at = view(at, (SEQ,))
            CTt, at = view(at, (SEQ,))
            xs, at = view(at, (NT, GW))
            Btok, at = view(at, (NT, P))
            rbc, at = view(at, (HPG, CHUNK))
            cbt, at = view(at, (LC,))
            mt01, at = view(at, (2, HB, LC))
            assert NBAT == 4 and 2 * HB * LC <= 2 * SEQ
            mt23, _ = view(cv_at, (2, HB, LC))
            mt = [mt01[:, 0], mt01[:, 1], mt23[:, 0], mt23[:, 1]]
            xdt, at = view(at, (TPC, GW))
            xdec, at = view(at, (TPC, GW))
            state, at = view(at, (GW,))
            zs, at = view(at, (TPC, GW))
            y, at = view(at, (TPC, GW))
            tq, at = view(at, (GW,))
            gT0, at = view(at, (GT, P))
            gT1, gT1_end = view(cv_at + 2 * HB * LC, (GT, P))
            assert gT1_end <= cv_at + 2 * SEQ
            gT, g_bank = (gT0, gT1), (5, 4)
            acg = small[:, 16:16 + NT * HPG].rearrange("p (t h) -> p t h", h=HPG)
            normg = small[:, 96:96 + GT]
            ssq = small[:, 90:92]
            w_xbc = [sem("xbc_w_loaded0"), sem("xbc_w_loaded1")]
            w_z, w_o = sem("z_w_loaded"), sem("out_w_loaded")
            xw_used, z_used, o_used = sem("xbc_w_used"), sem("z_product"), sem("out_product")
            raw_out, zeroed = sem("raw_evacuated"), sem("pads_zeroed")
            convd, cv_ready = sem("convolved"), sem("conv_silu")
            turned, tv, ta = sem("xs_transposed"), sem("xs_by_vector"), sem("xs_by_scalar")
            rb_loaded, acg_ready = sem("acs_broadcast"), sem("acs_group_copied")
            cb_done, cb_out = sem("cb_ready"), sem("cb_masked")
            slot_seen = sem("decay_slot_seen")
            diff, expd, mt_ready = sem("decay_exponent"), sem("decay_exp"), sem("decayed_cb")
            xdt_ready, xdec_ready = sem("xdt_ready"), sem("xdec_ready")
            st_done, st_out = sem("state_product"), sem("state_updated")
            yo_done, yd_done = sem("y_off_ready"), sem("y_diag_ready")
            z_out, y1_, y2_ = sem("z_silu"), sem("y_gated"), sem("y_normed")
            sq_done, rt_done = sem("y_squared"), sem("y_rms")
            g_turned, g_out = sem("y_transposed"), sem("gT_ready")
            o_read, o_out = sem("out_product_read"), sem("x_updated")
            chain = sem("ssd_chain")
            CPG = NCH * TPC
            with nc.Block() as block:
                @block.sync
                def _(sp):
                    with sp.Fori(0, SSM_G) as g:
                        for c in range(CTG):
                            sp.wait_ge(xw_used, g * CTG + c + 1)
                            sp.dma_start(xw[:, c % 2], ins["ssm_xbc"][bass.ds(g * CTG + c, 1)].rearrange("c p n -> p (c n)")).then_inc(w_xbc[c % 2], 16)
                            if c == 1:
                                sp.wait_ge(z_used, (g + 1) * CPG)
                                sp.dma_start(zw.rearrange("p k n -> p (k n)"), ins["ssm_z"][bass.ds(g, 1)].rearrange("c p n -> p (c n)")).then_inc(w_z, 16)
                            if c == 2:
                                sp.wait_ge(o_used, (g + 1) * 2 * CPG)
                                sp.dma_start(ow.rearrange("p k n -> p (k n)"), ins["ssm_out"][bass.ds(g, 1)].rearrange("c p n -> p (c n)")).then_inc(w_o, 16)
                        for c in range(NCH):
                            sp.wait_ge(diff, (g * NCH + c + 1) * NBAT)
                            sp.dma_start(rbc, acs_rows[bass.ds(g * HPG, HPG), c * CHUNK:(c + 1) * CHUNK].unsqueeze(0).to_broadcast([P, HPG, CHUNK])).then_inc(rb_loaded, 16)

                @block.tensor
                def _(pe):
                    pe.sem_inc(xw_used, 2)
                    pe.sem_inc(z_used, CPG)
                    pe.sem_inc(o_used, 2 * CPG)
                    pe.sem_inc(yd_done, NBAT)
                    def conv_product(g, c):
                        w = xw[:, c % 2].rearrange("p (k n) -> p k n", n=P)
                        pe.wait_ge(w_xbc[c % 2], g * (CTG // 2 * 16) + 16 * (c // 2 + 1))
                        if c >= 2:
                            pe.wait_ge(raw_out, g * CTG + c - 1)
                        for h in range(2):
                            for k in range(KD):
                                last = nc.tensor.matmul(ps[:, (c % 2) * 2 + h], w[:, k], hT[:, k, h * HALF:(h + 1) * HALF], start=(k == 0), stop=(k == KD - 1))
                        last.then_inc(xw_used, 1)

                    def group(g, more):
                        def conv_turn(c):
                            src = cv[:, c % 2] if c < GT else BT
                            pe.wait_ge(cv_ready, g * CTG + c + 1)
                            if c:
                                pe.wait_ge(tv, g * (GT + 1) + c)
                                pe.wait_ge(ta, g * (GT + 1) + c)
                            for t in range(NT):
                                last = nc.tensor.transpose(ps[:, 4 + t // 4, (t % 4) * P:(t % 4 + 1) * P], src[:, t * P:(t + 1) * P], ident)
                            last.then_inc(turned, 1)

                        for c in range(1, CTG):
                            conv_product(g, c)
                            if c <= GT + 1:
                                conv_turn(c - 1)

                        def z_product(c, a):
                            t = c * TPC + a
                            if t == 0:
                                pe.wait_ge(w_z, g * 16 + 16)
                                pe.wait_ge(raw_out, g * CTG + CTG)
                            if t >= TPC:
                                pe.wait_ge(z_out, g * CPG + t - TPC + 1)
                            for k in range(KD):
                                if k == KD - 2 and c and a == TPC - 1:
                                    for a_ in range(TPC):
                                        out_turn(c - 1, a_)
                                last = nc.tensor.matmul(ps[:, 1 + a], hT[:, k, t * P:(t + 1) * P], zw[:, k], start=(k == 0), stop=(k == KD - 1))
                            last.then_inc(z_used, 1)

                        def cb_product(c):
                            if c == 0:
                                pe.wait_ge(cv_ready, g * CTG + CTG)
                                pe.wait_ge(raw_out, g * CTG + CTG)
                            else:
                                pe.wait_ge(cb_out, g * NCH + c)
                            l0 = c * CHUNK
                            nc.tensor.matmul(ps[:, 0, 0:CHUNK], BT[:, l0:l0 + P], CTt[:, l0:l0 + CHUNK], start=True, stop=True)
                            nc.tensor.matmul(ps[:, 0, CHUNK:LC], BT[:, l0 + P:l0 + CHUNK], CTt[:, l0 + P:l0 + CHUNK], start=True, stop=True).then_inc(cb_done, 1)

                        def out_turn(c, a):
                            pe.wait_ge(y2_, g * CPG + c * TPC + a + 1)
                            for k in range(GT):
                                last = nc.tensor.transpose(ps[:, g_bank[a], k * P:(k + 1) * P], y[:, a, k * P:(k + 1) * P], ident)
                            last.then_inc(g_turned, 1)

                        def out_product(c, a):
                            t = c * TPC + a
                            pe.wait_ge(g_out, g * CPG + t + 1)
                            if t == 0:
                                pe.wait_ge(w_o, g * 16 + 16)
                            for h in range(2):
                                if t:
                                    pe.wait_ge(o_read, (g * CPG + t) * 2 + h - 1)
                                for k in range(GT):
                                    last = nc.tensor.matmul(ps[:, 6 + h], gT[a][:, k], ow[:, k, h * HALF:(h + 1) * HALF], start=(k == 0), stop=(k == GT - 1))
                                last.then_inc(o_used, 1)

                        for c in range(NCH):
                            if c:
                                cb_product(c)
                            z_product(c, 0)
                            if c == 0:
                                cb_product(c)
                            z_product(c, 1)
                            if c:
                                for a in range(TPC):
                                    out_product(c - 1, a)
                            if c:
                                pe.wait_ge(st_out, g * (NCH - 1) + c)
                                for a in range(TPC):
                                    t = c * TPC + a
                                    last = nc.tensor.matmul(ps[:, 3 + a], CTt[:, t * P:(t + 1) * P], state, start=True, stop=True)
                                last.then_inc(yo_done, 1)
                            if c < NCH - 1:
                                pe.wait_ge(xdec_ready, g * (NCH - 1) + c + 1)
                                if c == 0:
                                    pe.wait_ge(tv, (g + 1) * (GT + 1))
                                    pe.wait_ge(ta, (g + 1) * (GT + 1))
                                for a in range(TPC):
                                    last = nc.tensor.matmul(ps[:, 5], Btok[:, c * TPC + a], xdec[:, a], start=(a == 0), stop=(a == TPC - 1))
                                last.then_inc(st_done, 1)
                            pe.wait_ge(xdt_ready, g * NCH + c + 1)
                            if c:
                                pe.wait_ge(o_read, (g * CPG + c * TPC) * 2)
                            for b in range(NBAT):
                                pe.wait_ge(mt_ready, (g * NCH + c) * NBAT + b + 1)
                                for hh in range(HB):
                                    hd = b * HB + hh
                                    cols = slice(hd * DH, (hd + 1) * DH)
                                    m = mt[b][:, hh]
                                    nc.tensor.matmul(ps[:, 6, cols], m[:, 0:P], xdt[:, 0, cols], start=True, stop=True)
                                    nc.tensor.matmul(ps[:, 7, cols], m[:, P:2 * P], xdt[:, 0, cols], start=True, stop=False)
                                    last = nc.tensor.matmul(ps[:, 7, cols], m[:, 2 * P:3 * P], xdt[:, 1, cols], start=False, stop=True)
                                last.then_inc(yd_done, 1)
                        if more:
                            pe.wait_ge(z_out, (g + 1) * CPG)
                            pe.wait_ge(cb_out, (g + 1) * NCH)
                            conv_product(g + 1, 0)
                        for a in range(TPC):
                            out_turn(NCH - 1, a)
                        for a in range(TPC):
                            out_product(NCH - 1, a)
                        pe.wait_ge(o_read, (g + 1) * 2 * CPG)

                    conv_product(0, 0)
                    with pe.Fori(0, SSM_G - 1) as g:
                        group(g, True)
                    group(SSM_G - 1, False)

                @block.gpsimd
                def _(pool):
                    pool.sem_inc(diff, NBAT)
                    with pool.Fori(0, SSM_G) as g:
                        nc.gpsimd.tensor_copy(acg, acs[:, :, bass.ds(g * HPG, HPG)])
                        nc.gpsimd.tensor_copy(normg, par["norm"][:, bass.ds(g * GT, GT)]).then_inc(acg_ready, 1)
                        pool.wait_ge(acg_ready, g + 1)
                        for c in range(NCH):
                            pool.wait_ge(rb_loaded, (g * NCH + c) * 16 + 16)
                            for b in range(NBAT):
                                if c == 0 and b == 2:
                                    pool.wait_ge(cv_ready, (g + 1) * CTG)
                                    pool.wait_ge(turned, g * (GT + 1) + GT)
                                pool.wait_ge(yd_done, (g * NCH + c) * NBAT + b + 1)
                                pool.sem_inc(slot_seen, 1)
                                for hh in range(HB):
                                    hd = b * HB + hh
                                    nc.gpsimd.tensor_scalar(mt[b][:, hh, 0:CHUNK], rbc[:, hd], acg[:, c * TPC, hd:hd + 1], 0.0, ALU.subtract, ALU.min)
                                    last = nc.gpsimd.tensor_scalar(mt[b][:, hh, CHUNK:LC], rbc[:, hd, P:CHUNK], acg[:, c * TPC + 1, hd:hd + 1], 0.0, ALU.subtract, ALU.min)
                                last.then_inc(diff, 1)
                        pool.wait_ge(o_out, (g + 1) * 2 * CPG)

                @block.scalar
                def _(act):
                    with act.Fori(0, SSM_G) as g:
                        def silu(c):
                            dst = BT if c == GT else CTt if c == GT + 1 else cv[:, c % 2]
                            act.wait_ge(convd, g * CTG + c + 1)
                            nc.scalar.activation(dst, cv[:, c % 2], ACT.Silu).then_inc(cv_ready, 1)

                        def turn_evac(c):
                            act.wait_ge(turned, g * (GT + 1) + c + 1)
                            dst = xs[:, 4:8, c * P:(c + 1) * P] if c < GT else Btok[:, 4:8]
                            nc.scalar.copy(dst, ps[:, 5].rearrange("p (t n) -> p t n", n=P)).then_inc(ta, 1)

                        act.wait_ge(zeroed, 1)
                        for c in range(CTG):
                            if c >= 1:
                                silu(c - 1)
                            if c >= 2:
                                turn_evac(c - 2)
                            act.wait_ge(xw_used, g * CTG + c + 3)
                            if c >= 2:
                                act.wait_ge(convd, g * CTG + c - 1)
                            nc.scalar.copy(raw[:, c % 2, SCONV - 1:SCONV - 1 + SEQ], ps[:, (c % 2) * 2:(c % 2) * 2 + 2].rearrange("p a n -> p (a n)")).then_inc(raw_out, 1)
                        silu(CTG - 1)
                        turn_evac(GT)

                        def tail(c, a):
                            t = c * TPC + a
                            act.wait_ge(y1_, g * CPG + t + 1)
                            nc.scalar.activation(zs[:, a], y[:, a], ACT.Square, accum_out=ssq[:, a:a + 1]).then_inc(sq_done, 1)
                            act.wait_ge(sq_done, g * CPG + t + 1)
                            nc.scalar.activation(ssq[:, a:a + 1], ssq[:, a:a + 1], ACT.Sqrt, bias=eps, scale=1.0 / GW).then_inc(rt_done, 1)

                        def evac_gT(c, a):
                            t = c * TPC + a
                            act.wait_ge(acg_ready, g + 1)
                            act.wait_ge(g_turned, g * CPG + t + 1)
                            if t >= TPC:
                                act.wait_ge(o_used, ((g + 1) * CPG + t - 1) * 2)
                            for k in range(GT):
                                last = nc.scalar.activation(gT[a][:, k], ps[:, g_bank[a], k * P:(k + 1) * P], ACT.Copy, scale=normg[:, k:k + 1])
                            last.then_inc(g_out, 1)

                        def silu_z(c, a):
                            t = c * TPC + a
                            act.wait_ge(z_used, (g + 1) * CPG + t + 1)
                            if t >= TPC:
                                act.wait_ge(y1_, g * CPG + t - TPC + 1)
                            nc.scalar.activation(zs[:, a], ps[:, 1 + a], ACT.Silu).then_inc(z_out, 1)

                        def decays(c, b):
                            act.wait_ge(diff, (g * NCH + c + 1) * NBAT + b + 1)
                            nc.scalar.activation(mt[b], mt[b], ACT.Exp).then_inc(expd, 1)

                        for c in range(NCH):
                            decays(c, 0)
                            silu_z(c, 0)
                            decays(c, 1)
                            decays(c, 2)
                            if c:
                                evac_gT(c - 1, 0)
                                evac_gT(c - 1, 1)
                            silu_z(c, 1)
                            decays(c, 3)
                            for a in range(TPC):
                                tail(c, a)
                        for a in range(TPC):
                            evac_gT(NCH - 1, a)
                        act.wait_ge(o_out, (g + 1) * 2 * CPG)

                @block.vector
                def _(dve):
                    v = nc.vector
                    nc.vector.memset(raw[:, :, 0:SCONV - 1], 0.0).then_inc(zeroed, 1)
                    dve.wait_ge(zeroed, 1)
                    with dve.Fori(0, SSM_G) as g:
                        st = Steps(dve, chain, turn=g, per=CTG * (SCONV - 1) + (NCH - 2) + TPC * (2 + 4 * (NCH - 1)) + CPG)

                        def turn_evac(c):
                            dve.wait_ge(turned, g * (GT + 1) + c + 1)
                            dst = xs[:, 0:4, c * P:(c + 1) * P] if c < GT else Btok[:, 0:4]
                            v.tensor_copy(dst, ps[:, 4].rearrange("p (t n) -> p t n", n=P)).then_inc(tv, 1)

                        for c in range(CTG):
                            if c >= 2:
                                turn_evac(c - 2)
                            dve.wait_ge(raw_out, g * CTG + c + 1)
                            if c >= 2:
                                dve.wait_ge(cv_ready, g * CTG + c - 1)
                                dve.wait_ge(turned, g * (GT + 1) + c - 1)
                            yv = cv[:, c % 2]
                            for j in range(SCONV):
                                u = raw[:, c % 2, j:j + SEQ]
                                w = cw[:, bass.ds(g * CTG + c, 1), j]
                                if j == 0:
                                    st.link(v.tensor_scalar(yv, u, w, par["conv_b"][:, bass.ds(g * CTG + c, 1)], ALU.mult, ALU.add))
                                elif j < SCONV - 1:
                                    st.link(v.scalar_tensor_tensor(yv, u, w, yv, ALU.mult, ALU.add))
                                else:
                                    v.scalar_tensor_tensor(yv, u, w, yv, ALU.mult, ALU.add).then_inc(convd, 1)
                        turn_evac(GT)
                        dve.wait_ge(tv, (g + 1) * (GT + 1))
                        dve.wait_ge(ta, (g + 1) * (GT + 1))

                        def heads(ap):
                            return ap.rearrange("p (h d) -> p h d", d=DH)

                        def out_add(c, a):
                            t = c * TPC + a
                            for h in range(2):
                                dve.wait_ge(o_used, ((g + 1) * CPG + t) * 2 + h + 1)
                                v.tensor_tensor(tq, ps[:, 6 + h], gate[:, 0, h * HALF:(h + 1) * HALF], ALU.mult).then_inc(o_read, 1)
                                dve.wait_ge(o_read, (g * CPG + t) * 2 + h + 1)
                                xt = x[:, t, h * HALF:(h + 1) * HALF]
                                v.tensor_tensor(xt, xt, tq, ALU.add).then_inc(o_out, 1)
                                dve.wait_ge(o_out, (g * CPG + t) * 2 + h + 1)

                        for c in range(NCH):
                            hs = bass.ds(g * HPG, HPG)
                            t0, t1 = c * TPC, (c + 1) * TPC
                            for a in range(TPC):
                                last = v.tensor_tensor(heads(xdt[:, a]), heads(xs[:, t0 + a]), dt[:, t0 + a, hs].unsqueeze(2).to_broadcast([P, HPG, DH]), ALU.mult)
                            last.then_inc(xdt_ready, 1)
                            dve.wait_ge(xdt_ready, g * NCH + c + 1)
                            if c < NCH - 1:
                                for a in range(TPC):
                                    last = v.tensor_tensor(heads(xdec[:, a]), heads(xdt[:, a]), dst[:, t0 + a, hs].unsqueeze(2).to_broadcast([P, HPG, DH]), ALU.mult)
                                last.then_inc(xdec_ready, 1)
                            dve.wait_ge(cb_done, g * NCH + c + 1)
                            at_, n_ = CONST["tri_inc"]
                            v.tensor_tensor(cbt, ps[:, 0, 0:LC], cst[:, at_:at_ + LC], ALU.mult).then_inc(cb_out, 1)
                            dve.wait_ge(cb_out, g * NCH + c + 1)
                            for b in range(NBAT):
                                if c and b >= 2:
                                    out_add(c - 1, b - 2)
                                dve.wait_ge(expd, (g * NCH + c) * NBAT + b + 1)
                                v.tensor_tensor(mt[b], mt[b], bc(cbt, 1, HB), ALU.mult).then_inc(mt_ready, 1)
                            if c:
                                dve.wait_ge(yo_done, g * (NCH - 1) + c)
                                for a in range(TPC):
                                    last = st.did(v.tensor_tensor(heads(y[:, a]), heads(ps[:, 3 + a]), eacs[:, t0 + a, hs].unsqueeze(2).to_broadcast([P, HPG, DH]), ALU.mult))
                            if c < NCH - 1:
                                dve.wait_ge(st_done, g * (NCH - 1) + c + 1)
                                if c == 0:
                                    v.tensor_copy(state, ps[:, 5]).then_inc(st_out, 1)
                                else:
                                    st.link(v.tensor_tensor(heads(state), heads(state), cdec[:, c, hs].unsqueeze(2).to_broadcast([P, HPG, DH]), ALU.mult))
                                    v.tensor_tensor(state, state, ps[:, 5], ALU.add).then_inc(st_out, 1)
                                dve.wait_ge(st_out, g * (NCH - 1) + c + 1)
                            dve.wait_ge(yd_done, (g * NCH + c + 2) * NBAT)
                            for a in range(TPC):
                                t = t0 + a
                                st.link(v.tensor_tensor(heads(tq), heads(xs[:, t]), bc(row["ssm_d"][:, hs], 2, DH), ALU.mult))
                                if c:
                                    st.link(v.tensor_tensor(y[:, a], y[:, a], ps[:, 6 + a], ALU.add))
                                    st.link(v.tensor_tensor(y[:, a], y[:, a], tq, ALU.add))
                                else:
                                    st.link(v.tensor_tensor(y[:, a], tq, ps[:, 6 + a], ALU.add))
                                dve.wait_ge(z_out, g * CPG + t + 1)
                                v.tensor_tensor(y[:, a], y[:, a], zs[:, a], ALU.mult).then_inc(y1_, 1)
                            for a in range(TPC):
                                t = t0 + a
                                dve.wait_ge(rt_done, g * CPG + t + 1)
                                st.link(v.reciprocal(ssq[:, a:a + 1], ssq[:, a:a + 1]))
                                v.tensor_scalar(y[:, a], y[:, a], ssq[:, a:a + 1], None, ALU.mult).then_inc(y2_, 1)
                        for a in range(TPC):
                            out_add(NCH - 1, a)
                        st.end()


        for layer in range(DEPTH):
            (ada_from_sums if layer else ada_phase)(layer)
            norm_phase(layer, 0, False)
            (hybrid_phase if layer % 2 == 0 else ssm_phase)(layer)
            clear_sems()
            norm_phase(layer, 1, True)
            moe_phase(layer, layer == DEPTH - 1)
            if layer < DEPTH - 1:
                clear_sems()


def kernel(**inputs):
    import numpy as np
    import concourse.bacc as bacc
    from concourse import mybir as mb
    from concourse.bass_utils import run_bass_kernel_spmd as run

    a = {k: np.asarray(v) for k, v in inputs.items()}
    f = np.float32
    p = np.arange(P)
    parts = {
        "ident": np.eye(P, dtype=f),
        "tri_strict": (p[:, None] < p[None]).astype(f),
        "tri_inc": (p[:, None] <= p[None]).astype(f),
        "ones": np.ones((P, P), f),
        "tri_inc2": (p[:, None] <= p[None]).astype(f),
        "maskneg": np.where(p[:, None] >= p[None], 0.0, NEG).astype(f),
        "before4": np.broadcast_to((np.arange(J)[None] < np.arange(J)[:, None]).astype(f).reshape(1, -1), (P, J * J)),
        "group_key": np.broadcast_to((G - np.arange(G)).astype(f)[None], (P, G)),
        "step128": np.broadcast_to((P * np.arange(NT)).astype(f)[None], (P, NT)),
        "before16": np.broadcast_to((np.arange(E)[None] < np.arange(E)[:, None]).astype(f).reshape(1, -1), (P, E * E)),
        "chunk_end": np.broadcast_to((P * (1 + np.arange(SLOTS))).astype(f)[None], (P, SLOTS)),
        "iota_chunk": np.broadcast_to(np.arange(SLOTS).astype(f)[None], (P, SLOTS)),
        "iota128": np.broadcast_to(p.astype(f)[None], (P, P)),
        "token_id": (p[:, None] + P * np.arange(NT)[None]).astype(f),
        "eps": np.full((P, 1), EPS, f),
    }
    arrays = {}
    arrays["consts"] = np.concatenate([parts[n] for n in CONST], axis=1)

    def cols(v):
        return v.reshape(-1, P).T

    arrays["pcols"] = np.stack([np.concatenate([cols(a["c"][0]), cols(a["ada_b"][l]), cols(a["norm_mix"][l]), cols(a["norm_ffn"][l])], axis=1)
                                for l in range(DEPTH)], axis=1)
    arrays["mix0"] = np.concatenate([np.tile(a["hy_q_norm"][0], 2)[:, None], np.tile(a["hy_k_norm"][0], 2)[:, None],
                                     cols(a["hy_dw_b"][0]), cols(a["hy_ln_g"][0]), cols(a["hy_ln_b"][0]),
                                     a["hy_dw_w"][0].reshape(CONV_W, CT, P).transpose(2, 1, 0).reshape(P, -1)], axis=1)
    order = [i for g in range(SSM_G) for i in [*range(g * GW // P, (g + 1) * GW // P), SSM_INNER // P + g, SSM_INNER // P + SSM_G + g]]
    arrays["mix1"] = np.concatenate([cols(a["ssm_conv_b"][0])[:, order], cols(a["ssm_norm"][0]),
                                     a["ssm_conv_w"][0].reshape(SCONV, XBC_T, P).transpose(2, 1, 0)[:, order].reshape(P, -1)], axis=1)
    arrays["rows"] = np.broadcast_to(np.concatenate([a["router_bias"], a["ssm_dt_bias"][0], a["ssm_a_log"][0], a["ssm_d"][0]])[None], (P, NROWS))
    ab = a["ada_b"].reshape(DEPTH, N_MOD, D)[:, [2, 5]]
    arrays["gate_bias"] = np.broadcast_to(ab[:, None], (DEPTH, P, 2, D))
    arrays["x"] = a["x"][0]
    arrays["router_w"] = a["router_w"]

    def tiled(w, n):
        k, m = w.shape
        return w.reshape(k // P, P, m // n, n).transpose(2, 1, 0, 3).reshape(m // n, P, -1)

    arrays["ada_w0"] = tiled(a["ada_w"][0], D)
    arrays["ada_w1"] = tiled(a["ada_w"][1], HALF)
    ex = np.empty((DEPTH * E * 6, P, KD * FF // 2), f)
    pieces = ex.reshape(DEPTH, E, 6, P, -1)
    for q, key in enumerate(("exp_w_gate", "exp_w_up")):
        w = a[key].reshape(DEPTH, E, KD, P, 2, FF // 2).transpose(0, 1, 4, 3, 2, 5).reshape(DEPTH, E, 2, P, -1)
        pieces[:, :, q], pieces[:, :, 2 + q] = w[:, :, 0], w[:, :, 1]
    pieces[:, :, 4:] = a["exp_w_down"].reshape(DEPTH, E, 2, FT // 2, P, D).transpose(0, 1, 2, 4, 3, 5).reshape(DEPTH, E, 2, P, -1)
    arrays["experts"] = ex
    w = a["hy_w_in"][0]
    u = w[:, 3 * ATT_W:].reshape(D, 2, CT, P).transpose(0, 2, 1, 3).reshape(D, -1)
    w = tiled(np.concatenate([u, w[:, :3 * ATT_W]], axis=1), 2 * P)
    arrays["hy_in"] = np.concatenate([w, w[:1]])
    arrays["hy_out"] = tiled(a["hy_w_out"][0], D)[0]
    w = a["ssm_w_in"][0]
    arrays["ssm_z"] = tiled(w[:, :SSM_INNER], GW)
    arrays["ssm_xbc"] = tiled(w[:, SSM_INNER:SSM_INNER + XBC_T * P], P)[order]
    arrays["ssm_dt"] = tiled(w[:, SSM_INNER + XBC_T * P:], SSM_HEADS)[0]
    arrays["ssm_out"] = a["ssm_w_out"][0].reshape(SSM_G, GW // P, P, D).transpose(0, 2, 1, 3).reshape(SSM_G, P, -1)
    nc = bacc.Bacc("TRN2", target_bir_lowering=False, num_devices=1)
    arrays = {f"in_{k}": np.ascontiguousarray(v) for k, v in arrays.items()}
    ins = {k[3:]: nc.dram_tensor(k, v.shape, mb.dt.from_np(v.dtype), kind="ExternalInput").ap() for k, v in arrays.items()}
    out = nc.dram_tensor("out_0", (1, SEQ, D), mb.dt.float32, kind="ExternalOutput").ap()
    build(nc, ins, out)
    return run(nc, [arrays], core_ids=[0]).results[0]["out_0"]
```
